# Optimizing a Trainium2 kernel written in Bass

```python
import math
import jax, jax.numpy as jnp
from jax import lax
import numpy as np

D_MODEL = 1024
BATCH = 1
SEQ = 256
DEPTH = 2
DEC_BATCH = 8
DEC_SEQ = 4
PAST_LEN = 2048
PAGE_SIZE = 128

D_MIX = 2 * D_MODEL
D_SSD = D_MIX // 2
SSD_HEAD_DIM = 64
SSD_HEADS = D_SSD // SSD_HEAD_DIM
SSD_GROUPS = 2
SSD_STATE = 128
SSD_CONV_DIM = D_SSD + 2 * SSD_GROUPS * SSD_STATE
CONV_WIDTH = 4
D_RG = D_MIX // 4
RG_BLOCKS = 8
RG_BLOCK_W = D_RG // RG_BLOCKS
RG_C = 8.0
D_RET = D_MIX // 4
RET_HEADS = 4
RET_HEAD_DIM = D_RET // RET_HEADS
ROPE_BASE = 10000.0
CHUNK = 128
IN_DIM = D_SSD + SSD_CONV_DIM + SSD_HEADS + 2 * D_RG + 4 * D_RET
N_EXPERTS = 32
N_EXPERT_GROUPS = 4
EXPERTS_PER_GROUP = N_EXPERTS // N_EXPERT_GROUPS
TOP_K = 2
D_EXPERT = D_MODEL // 2
EXPERT_BLOCK = 128
ALPHA = (2 * DEPTH) ** 0.25
BETA = (8 * DEPTH) ** -0.25
EPS = 1e-5

kernel_name = "hymba_ssd_rglru_retention_moe_step"

def _layernorm(x, g, b):
    xf = x.astype(jnp.float32)
    mu = jnp.mean(xf, -1, keepdims=True)
    var = jnp.mean(jnp.square(xf - mu), -1, keepdims=True)
    return (xf - mu) * lax.rsqrt(var + EPS) * g + b

def _group_rmsnorm(y, w, groups):
    b, L, d = y.shape
    yf = y.astype(jnp.float32).reshape(b, L, groups, d // groups)
    yf = yf * lax.rsqrt(jnp.mean(yf * yf, -1, keepdims=True) + EPS)
    return yf.reshape(b, L, d) * w

def _causal_conv(x, buf, w, bias):
    L = x.shape[1]
    xp = jnp.concatenate([buf.astype(x.dtype), x], axis=1)
    y = bias + sum(xp[:, j:j + L] * w[j] for j in range(CONV_WIDTH))
    return y, xp[:, -(CONV_WIDTH - 1):]

def _rope(x, pos):
    half = x.shape[-1] // 2
    inv = ROPE_BASE ** (-jnp.arange(half, dtype=jnp.float32) / half)
    ang = pos[:, None] * inv[None, :]
    cos = jnp.cos(ang)[None, :, None, :]
    sin = jnp.sin(ang)[None, :, None, :]
    x1 = x[..., :half].astype(jnp.float32)
    x2 = x[..., half:].astype(jnp.float32)
    return jnp.concatenate([x1 * cos - x2 * sin, x2 * cos + x1 * sin], -1)

def _chunked_decay_recurrence(q, k, v, log_a, h0):
    f32 = jnp.float32
    b, L, nh, dk = q.shape
    dv = v.shape[-1]
    blk = CHUNK if L % CHUNK == 0 else L
    nc = L // blk
    qc = q.astype(f32).reshape(b, nc, blk, nh, dk)
    kc = k.astype(f32).reshape(b, nc, blk, nh, dk)
    vc = v.astype(f32).reshape(b, nc, blk, nh, dv)
    acum = jnp.cumsum(log_a.astype(f32).reshape(b, nc, blk, nh), axis=2)
    causal = jnp.tril(jnp.ones((blk, blk), bool))[None, None, :, :, None]
    decay = jnp.exp(jnp.where(causal, acum[:, :, :, None, :] - acum[:, :, None, :, :], -jnp.inf))
    scores = jnp.einsum("bcthd,bcshd->bctsh", qc, kc) * decay
    y = jnp.einsum("bctsh,bcshv->bcthv", scores, vc)
    to_end = jnp.exp(acum[:, :, -1:, :] - acum)
    chunk_state = jnp.einsum("bcshd,bcshv->bchdv", kc * to_end[..., None], vc)
    chunk_decay = jnp.exp(acum[:, :, -1, :])

    def step(S, inp):
        cs, cd = inp
        return cd[:, :, None, None] * S + cs, S

    h_final, h_prev = lax.scan(step, h0.astype(f32),
                               (jnp.moveaxis(chunk_state, 1, 0), jnp.moveaxis(chunk_decay, 1, 0)))
    h_prev = jnp.moveaxis(h_prev, 0, 1)
    y = y + jnp.einsum("bcthd,bchdv->bcthv", qc * jnp.exp(acum)[..., None], h_prev)
    return y.reshape(b, L, nh, dv), h_final

def _ssd_mixer(z, xbc, dt_raw, h0, buf, p):
    b, L, _ = z.shape
    xbc, new_buf = _causal_conv(xbc, buf, p["ssd_conv_w"], p["ssd_conv_b"])
    xbc = jax.nn.silu(xbc)
    xs, Bm, Cm = jnp.split(xbc, [D_SSD, D_SSD + SSD_GROUPS * SSD_STATE], axis=-1)
    xs = xs.reshape(b, L, SSD_HEADS, SSD_HEAD_DIM)
    rep = SSD_HEADS // SSD_GROUPS
    Bh = jnp.repeat(Bm.reshape(b, L, SSD_GROUPS, SSD_STATE), rep, axis=2)
    Ch = jnp.repeat(Cm.reshape(b, L, SSD_GROUPS, SSD_STATE), rep, axis=2)
    dt = jax.nn.softplus(dt_raw.astype(jnp.float32) + p["ssd_dt_bias"])
    A = -jnp.exp(p["ssd_a_log"].astype(jnp.float32))
    y, h_new = _chunked_decay_recurrence(Ch, Bh, xs * dt[..., None], dt * A, h0)
    y = y + p["ssd_d"][:, None] * xs
    y = y.reshape(b, L, D_SSD) * jax.nn.silu(z)
    return _group_rmsnorm(y, p["ssd_norm_w"], SSD_GROUPS), new_buf, h_new

def _lru_combine(left, right):
    a_l, u_l = left
    a_r, u_r = right
    return a_l * a_r, a_r * u_l + u_r

def _rglru_mixer(xr, gate, h0, buf, p):
    b, L, _ = xr.shape
    xc, new_buf = _causal_conv(xr, buf, p["rg_conv_w"], p["rg_conv_b"])
    xb = xc.reshape(b, L, RG_BLOCKS, RG_BLOCK_W)
    r = jax.nn.sigmoid(jnp.einsum("blnj,njk->blnk", xb, p["rg_wa"]).reshape(b, L, D_RG) + p["rg_ba"])
    i = jax.nn.sigmoid(jnp.einsum("blnj,njk->blnk", xb, p["rg_wx"]).reshape(b, L, D_RG) + p["rg_bx"])
    log_a = (-RG_C * jax.nn.softplus(-p["rg_lambda"].astype(jnp.float32))) * r.astype(jnp.float32)
    a = jnp.exp(log_a)
    u = jnp.sqrt(-jnp.expm1(2.0 * log_a)) * (i * xc).astype(jnp.float32)
    u = u.at[:, 0].add(a[:, 0] * h0.astype(jnp.float32))
    _, h = lax.associative_scan(_lru_combine, (a, u), axis=1)
    return h * jax.nn.gelu(gate), new_buf, h[:, -1]

def _retention_mixer(q, k, v, g, pos, h0, p):
    b, L, _ = q.shape
    q = _rope(q.reshape(b, L, RET_HEADS, RET_HEAD_DIM), pos)
    k = _rope(k.reshape(b, L, RET_HEADS, RET_HEAD_DIM), pos) * (RET_HEAD_DIM ** -0.5)
    v = v.reshape(b, L, RET_HEADS, RET_HEAD_DIM)
    log_gamma = jnp.log1p(-jnp.exp2(-5.0 - jnp.arange(RET_HEADS, dtype=jnp.float32)))
    log_a = jnp.broadcast_to(log_gamma, (b, L, RET_HEADS))
    y, h_new = _chunked_decay_recurrence(q, k, v, log_a, h0)
    mu = jnp.mean(y, -1, keepdims=True)
    var = jnp.mean(jnp.square(y - mu), -1, keepdims=True)
    y = ((y - mu) * lax.rsqrt(var + EPS)).reshape(b, L, D_RET) * p["ret_gn_w"]
    return jax.nn.silu(g) * y, h_new

def _moe(h, router_w, router_bias, p):
    b, L, D = h.shape
    T = b * L
    ht = h.reshape(T, D)
    scores = jax.nn.sigmoid((ht @ router_w).astype(jnp.float32))
    choice = (scores + router_bias.astype(jnp.float32)).reshape(T, N_EXPERT_GROUPS, EXPERTS_PER_GROUP)
    group_score = lax.top_k(choice, TOP_K)[0].sum(-1)
    _, g_idx = lax.top_k(group_score, 1)
    in_group = jnp.take_along_axis(choice, g_idx[:, :, None], axis=1)[:, 0]
    _, local = lax.top_k(in_group, TOP_K)
    expert_idx = g_idx * EXPERTS_PER_GROUP + local
    wts = jnp.take_along_axis(scores, expert_idx, axis=1)
    wts = wts / jnp.sum(wts, -1, keepdims=True)
    A = T * TOP_K
    flat_e = expert_idx.reshape(A)
    order = jnp.argsort(flat_e)
    sorted_e = flat_e[order]
    tok = order // TOP_K
    counts = jnp.zeros((N_EXPERTS,), jnp.int32).at[flat_e].add(1)
    padded = (counts + EXPERT_BLOCK - 1) // EXPERT_BLOCK * EXPERT_BLOCK
    pad_end = jnp.cumsum(padded)
    pad_start = pad_end - padded
    start = jnp.cumsum(counts) - counts
    dest = (pad_start - start)[sorted_e] + jnp.arange(A, dtype=jnp.int32)
    n_blocks = (A + N_EXPERTS * (EXPERT_BLOCK - 1) + EXPERT_BLOCK - 1) // EXPERT_BLOCK
    P = n_blocks * EXPERT_BLOCK
    slot_tok = jnp.full((P,), T, jnp.int32).at[dest].set(tok)
    xs = jnp.concatenate([ht, jnp.zeros((1, D), ht.dtype)], 0)[slot_tok].reshape(n_blocks, EXPERT_BLOCK, D)
    block_pos = jnp.arange(n_blocks, dtype=jnp.int32) * EXPERT_BLOCK
    block_expert = jnp.minimum(jnp.sum(pad_end[None, :] <= block_pos[:, None], axis=1), N_EXPERTS - 1)

    def expert_block(args):
        xb, e = args
        return (jax.nn.silu(xb @ p["e_gate"][e]) * (xb @ p["e_up"][e])) @ p["e_down"][e]

    ys = lax.map(expert_block, (xs, block_expert)).reshape(P, D)
    contrib = (ys[dest] * wts.reshape(A)[order][:, None]).astype(ht.dtype)
    out = jnp.zeros((T, D), ht.dtype).at[tok].add(contrib)
    return out.reshape(b, L, D)

def _layer(x, c, pos, st, p, router_w, router_bias):
    ssd_h0, ssd_buf, rg_h0, rg_buf, ret_h0 = st
    b, L, _ = x.shape
    mod = (jax.nn.silu(c) @ p["w_ada"] + p["b_ada"]).reshape(b, 6, D_MODEL)[:, :, None, :]
    sh1, sc1, g1, sh2, sc2, g2 = [mod[:, j] for j in range(6)]
    h = x * (1.0 + sc1) + sh1
    proj = h @ p["w_in"]
    sizes = [D_SSD, SSD_CONV_DIM, SSD_HEADS, D_RG, D_RG, D_RET, D_RET, D_RET, D_RET]
    z, xbc, dt_raw, rg_x, rg_gate, q, k, v, g = jnp.split(proj, np.cumsum(sizes)[:-1].tolist(), axis=-1)
    y_ssd, ssd_buf_new, ssd_h = _ssd_mixer(z, xbc, dt_raw, ssd_h0, ssd_buf, p)
    y_rg, rg_buf_new, rg_h = _rglru_mixer(rg_x, rg_gate, rg_h0, rg_buf, p)
    y_ret, ret_h = _retention_mixer(q, k, v, g, pos, ret_h0, p)
    mix = jnp.concatenate([y_ssd, y_rg, y_ret], -1).astype(x.dtype) @ p["w_out"]
    x = _layernorm(ALPHA * x + (1.0 + g1) * mix, p["ln1_g"], p["ln1_b"]).astype(x.dtype)
    h2 = x * (1.0 + sc2) + sh2
    moe = _moe(h2, router_w, router_bias, p)
    x = _layernorm(ALPHA * x + (1.0 + g2) * moe, p["ln2_g"], p["ln2_b"]).astype(x.dtype)
    return x, (ssd_h, ssd_buf_new, rg_h, rg_buf_new, ret_h)

def _trunk(x, c, pos0, states, params, router_w, router_bias):
    pos = pos0 + jnp.arange(x.shape[1], dtype=jnp.float32)
    new = []
    for l in range(DEPTH):
        x, st = _layer(x, c, pos, states[l], params[l], router_w, router_bias)
        new.append(st)
    ssd = jnp.stack([s[0] for s in new])
    ssd_conv = jnp.stack([s[1] for s in new])
    rg = jnp.stack([s[2] for s in new])
    rg_conv = jnp.stack([s[3] for s in new])
    ret = jnp.stack([s[4] for s in new])
    return x, ssd, ssd_conv, rg, rg_conv, ret

def setup_inputs(seed: int = 0) -> dict:
    key = jax.random.key(seed)
    ks = iter(jax.random.split(key, 48))
    f32 = jnp.float32

    def nrm(shape, s):
        return jax.random.normal(next(ks), shape, f32) * s

    a0 = jax.random.uniform(next(ks), (DEPTH, D_RG), f32, 0.9, 0.999)
    s = a0 ** (1.0 / RG_C)
    rg_lambda = jnp.log(s) - jnp.log1p(-s)
    dt0 = jnp.exp(jax.random.uniform(next(ks), (DEPTH, SSD_HEADS), f32, math.log(1e-3), math.log(1e-1)))
    ssd_dt_bias = dt0 + jnp.log(-jnp.expm1(-dt0))
    ssd_a_log = jnp.log(jax.random.uniform(next(ks), (DEPTH, SSD_HEADS), f32, 1.0, 16.0))
    return {
        "x_prompt": nrm((BATCH, SEQ, D_MODEL), 1.0),
        "x_sample": nrm((DEC_BATCH, DEC_SEQ, D_MODEL), 1.0),
        "c_prompt": nrm((BATCH, D_MODEL), 1.0),
        "c_sample": nrm((DEC_BATCH, D_MODEL), 1.0),
        "state_ssd": nrm((DEPTH, DEC_BATCH, SSD_HEADS, SSD_STATE, SSD_HEAD_DIM), 0.3),
        "state_ssd_conv": nrm((DEPTH, DEC_BATCH, CONV_WIDTH - 1, SSD_CONV_DIM), 1.0),
        "state_rglru": nrm((DEPTH, DEC_BATCH, D_RG), 0.5),
        "state_rglru_conv": nrm((DEPTH, DEC_BATCH, CONV_WIDTH - 1, D_RG), 1.0),
        "state_ret": nrm((DEPTH, DEC_BATCH, RET_HEADS, RET_HEAD_DIM, RET_HEAD_DIM), 0.5),
        "w_ada": nrm((DEPTH, D_MODEL, 6 * D_MODEL), 0.1 * D_MODEL ** -0.5),
        "b_ada": nrm((DEPTH, 6 * D_MODEL), 0.02),
        "w_in": nrm((DEPTH, D_MODEL, IN_DIM), D_MODEL ** -0.5),
        "ssd_conv_w": nrm((DEPTH, CONV_WIDTH, SSD_CONV_DIM), CONV_WIDTH ** -0.5),
        "ssd_conv_b": nrm((DEPTH, SSD_CONV_DIM), 0.02),
        "ssd_dt_bias": ssd_dt_bias,
        "ssd_a_log": ssd_a_log,
        "ssd_d": 1.0 + nrm((DEPTH, SSD_HEADS), 0.1),
        "ssd_norm_w": 1.0 + nrm((DEPTH, D_SSD), 0.02),
        "rg_conv_w": nrm((DEPTH, CONV_WIDTH, D_RG), CONV_WIDTH ** -0.5),
        "rg_conv_b": nrm((DEPTH, D_RG), 0.02),
        "rg_wa": nrm((DEPTH, RG_BLOCKS, RG_BLOCK_W, RG_BLOCK_W), RG_BLOCK_W ** -0.5),
        "rg_ba": nrm((DEPTH, D_RG), 0.02),
        "rg_wx": nrm((DEPTH, RG_BLOCKS, RG_BLOCK_W, RG_BLOCK_W), RG_BLOCK_W ** -0.5),
        "rg_bx": nrm((DEPTH, D_RG), 0.02),
        "rg_lambda": rg_lambda,
        "ret_gn_w": 1.0 + nrm((DEPTH, D_RET), 0.02),
        "w_out": nrm((DEPTH, D_MIX, D_MODEL), BETA * D_MIX ** -0.5),
        "ln1_g": 1.0 + nrm((DEPTH, D_MODEL), 0.02),
        "ln1_b": nrm((DEPTH, D_MODEL), 0.02),
        "router_w": nrm((D_MODEL, N_EXPERTS), D_MODEL ** -0.5),
        "router_bias": nrm((N_EXPERTS,), 0.01),
        "exp_w_gate": nrm((DEPTH, N_EXPERTS, D_MODEL, D_EXPERT), D_MODEL ** -0.5),
        "exp_w_up": nrm((DEPTH, N_EXPERTS, D_MODEL, D_EXPERT), D_MODEL ** -0.5),
        "exp_w_down": nrm((DEPTH, N_EXPERTS, D_EXPERT, D_MODEL), BETA * D_EXPERT ** -0.5),
        "ln2_g": 1.0 + nrm((DEPTH, D_MODEL), 0.02),
        "ln2_b": nrm((DEPTH, D_MODEL), 0.02),
    }

def reference(x_prompt, x_sample, c_prompt, c_sample, state_ssd, state_ssd_conv, state_rglru,
              state_rglru_conv, state_ret, w_ada, b_ada, w_in, ssd_conv_w, ssd_conv_b, ssd_dt_bias,
              ssd_a_log, ssd_d, ssd_norm_w, rg_conv_w, rg_conv_b, rg_wa, rg_ba, rg_wx, rg_bx,
              rg_lambda, ret_gn_w, w_out, ln1_g, ln1_b, router_w, router_bias, exp_w_gate, exp_w_up,
              exp_w_down, ln2_g, ln2_b):
    params = [dict(w_ada=w_ada[l], b_ada=b_ada[l], w_in=w_in[l], ssd_conv_w=ssd_conv_w[l],
                   ssd_conv_b=ssd_conv_b[l], ssd_dt_bias=ssd_dt_bias[l], ssd_a_log=ssd_a_log[l],
                   ssd_d=ssd_d[l], ssd_norm_w=ssd_norm_w[l], rg_conv_w=rg_conv_w[l],
                   rg_conv_b=rg_conv_b[l], rg_wa=rg_wa[l], rg_ba=rg_ba[l], rg_wx=rg_wx[l],
                   rg_bx=rg_bx[l], rg_lambda=rg_lambda[l], ret_gn_w=ret_gn_w[l], w_out=w_out[l],
                   ln1_g=ln1_g[l], ln1_b=ln1_b[l], e_gate=exp_w_gate[l], e_up=exp_w_up[l],
                   e_down=exp_w_down[l], ln2_g=ln2_g[l], ln2_b=ln2_b[l]) for l in range(DEPTH)]
    dt = x_prompt.dtype
    b = x_prompt.shape[0]
    zero_states = [(jnp.zeros((b, SSD_HEADS, SSD_STATE, SSD_HEAD_DIM), dt),
                    jnp.zeros((b, CONV_WIDTH - 1, SSD_CONV_DIM), dt),
                    jnp.zeros((b, D_RG), dt),
                    jnp.zeros((b, CONV_WIDTH - 1, D_RG), dt),
                    jnp.zeros((b, RET_HEADS, RET_HEAD_DIM, RET_HEAD_DIM), dt)) for _ in range(DEPTH)]
    past_states = [(state_ssd[l], state_ssd_conv[l], state_rglru[l], state_rglru_conv[l], state_ret[l])
                   for l in range(DEPTH)]
    y_prompt, ssd_p, ssd_conv_p, rg_p, rg_conv_p, ret_p = _trunk(
        x_prompt, c_prompt, 0.0, zero_states, params, router_w, router_bias)
    y_sample, ssd_s, ssd_conv_s, rg_s, rg_conv_s, ret_s = _trunk(
        x_sample, c_sample, float(PAST_LEN), past_states, params, router_w, router_bias)
    return (y_prompt, y_sample, ssd_p, ssd_conv_p, rg_p, rg_conv_p, ret_p,
            ssd_s, ssd_conv_s, rg_s, rg_conv_s, ret_s)


_drawn_inputs = setup_inputs


def setup_inputs(seed=0):
    import zlib

    import numpy as np

    out = dict(_drawn_inputs(seed))
    spreads = {}
    factors = {'rg_ba': 8.0, 'rg_bx': 4.956, 'ret_gn_w': 3.26}
    for name, (base, spread) in spreads.items():
        noise = np.random.default_rng([zlib.crc32(name.encode()), seed]).standard_normal(out[name].shape)
        drawn = base * np.exp(spread * noise) if base else spread * noise
        out[name] = __import__('jax').numpy.asarray(drawn.astype(out[name].dtype))
    for name, factor in factors.items():
        out[name] = (out[name] * factor).astype(out[name].dtype)
    return out
```

```python
from contextlib import ExitStack

import concourse.bass as bass
from concourse import mybir

F32 = mybir.dt.float32
I32 = mybir.dt.int32
ALU = mybir.AluOpType
ACT = mybir.ActivationFunctionType
AX_X = mybir.AxisListType.X

P = 128
D_MODEL = 1024
KT = D_MODEL // P
SEQ = 256
DEPTH = 2
DEC_BATCH = 8
DEC_SEQ = 4
PAST_LEN = 2048
TS = DEC_BATCH * DEC_SEQ
T = SEQ + TS
NT = 3
ROWS = (P, P, TS)
T0 = (0, P, 2 * P)
D_SSD = 1024
SSD_HEADS, SSD_HD, SSD_GROUPS, SSD_STATE = 16, 64, 2, 128
HG = SSD_HEADS // SSD_GROUPS
SSD_CONV_DIM = D_SSD + 2 * SSD_GROUPS * SSD_STATE
CONV_WIDTH = 4
HALO = CONV_WIDTH - 1
D_RG = 512
RG_BLOCK_W = 64
RG_C = 8.0
D_RET = 512
RET_HEADS, RET_HD = 4, 128
N_EXPERTS, N_GROUPS = 32, 4
EPG = N_EXPERTS // N_GROUPS
D_EXPERT = 512
ALPHA = float((2 * DEPTH) ** 0.25)
EPS = 1e-5
CH = 512
BLK = 32

XT = SSD_CONV_DIM // P
RT = D_RG // P
RAWW = HALO + SEQ + DEC_BATCH * (HALO + DEC_SEQ)
CVW = RAWW - HALO
SS = HALO + SEQ

C_Z, C_XBC = 0, D_SSD
C_DT = C_XBC + SSD_CONV_DIM
C_RGX = C_DT + SSD_HEADS
C_RGG = C_RGX + D_RG
C_Q = C_RGG + D_RG
IN_DIM = C_Q + 4 * D_RET

V_XW, V_XB = 0, CONV_WIDTH * XT
V_RW = V_XB + XT
V_RB = V_RW + CONV_WIDTH * RT
V_BA, V_BX, V_LAM = V_RB + RT, V_RB + 2 * RT, V_RB + 3 * RT
V_N = V_RB + 4 * RT

STREAM = ([("ada", n) for n in range(4)] + [("in", C_RGX), ("in", C_RGG)]
          + [("in", C_XBC + CH * n) for n in range(3)] + [("in", C_Z), ("in", C_Z + CH)]
          + [("in", C_Q + CH * n) for n in range(4)] + [("out", 0), ("out", 1)]
          + [("ada", n) for n in range(4, 12)] + [("out", 2), ("out", 3)])
NBMAX = 2 * ((2 * T // BLK + N_EXPERTS + 2 + 1) // 2)
NS = 3
PER_SLOT = len(STREAM) // NS
assert PER_SLOT * NS == len(STREAM)


FILLER = {1 + c * NT + j: (2 + c, j) for c in range(2) for j in range(NT)}


def ada_steps(chunks):
    out = [(("ada", chunks[0]), "A")]
    for n, c in enumerate(chunks):
        if n + 1 < len(chunks):
            out.append((("ada", chunks[n + 1]), "A"))
        out += [(("mp", c), "D"), (("ms", c), "D")]
    return out


def ssd_steps(i):
    out = [(("cb", i), "D")]
    out += [(("dec", i, q), "D") for q in range(4 if i < 2 else 1)]
    if i == 1:
        out += [(("yo", i, g), "D") for g in range(2)]
    if i < 2:
        out += [(("cs", i, g), "D") for g in range(2)]
    else:
        for b in range(DEC_BATCH):
            out += [(("st", b, g), "D") for g in range(2)]
            if b in FILLER:
                out.append((("q", *FILLER[b]), "A"))
    if i == 0:
        out += [(("z", 1, j), "A") for j in (1, 2)]
    return out + [(("yi", i, g), "D") for g in range(2)]


def ret_steps(i):
    out = [(("sc", i), "D")]
    if i == 0:
        out.append((("mix_a", 1, 1), "A"))
    if i == 1:
        out.append((("ro", i), "D"))
    if i < 2:
        out.append((("rs", i), "D"))
    else:
        for b in range(DEC_BATCH):
            out.append((("rt", b), "D"))
            if 1 <= b <= 6:
                out.append((("ada", 5 + b), "A"))
    if i == 0:
        out.append((("mix_a", 2, 0), "A"))
    out.append((("ri", i), "D"))
    if i == 0:
        out.append((("mix_a", 2, 1), "A"))
    if i == 1:
        out += [(("ada", 4), "A"), (("ada", 5), "A")]
    return out + [(("yrt", i), "A")]


def bank_plan():
    out = [(("vec",), "D"), (("halo",), "D"), (("h0rg",), "D")]
    out += ada_steps(range(4))
    out += [(("ht", i, a), "A") for i in range(NT) for a in range(2)]
    out += [(("rgx", m), "A") for m in range(RT)] + [(("rgg", m), "A") for m in range(RT)]
    for m in range(XT + 1):
        if m < XT:
            out.append((("fm", m), "A"))
        if m >= 3:
            out.append((("xst", m - 3), "A"))
    out += [(("tail", q), "A") for q in range((XT + RT) // 4)]
    out.append((("dt",), "D"))
    out += [(("rga", m), "A") for m in range(RT)] + [(("rgi", m), "A") for m in range(RT)]
    out += [(("z", 0, i), "A") for i in range(NT)]
    out += [(("cum",), "D"), (("z", 1, 0), "A"), (("rgo",), "D")]
    for i in range(NT):
        out += ssd_steps(i)
        if i < 2:
            out += [(("q", i, j), "A") for j in range(NT)]
    out += [(("yt", i, a), "A") for i in range(2) for a in range(2)]
    out += [(("mix_a", 0, a), "A") for a in range(2)]
    out += [(("yt", 2, a), "A") for a in range(2)] + [(("mix_a", 1, 0), "A")]
    out += [(("qk", i, a), "A") for i in range(NT) for a in range(2)]
    for i in range(NT):
        out += ret_steps(i)
    out += [((w, c), "D") for c in (4, 5) for w in ("mp", "ms")]
    out += [(("mix", i, a), "D") for i in range(NT) for a in range(2)]
    out += [((w, c), "A") for c in range(6, 12) for w in ("mp", "ms")]
    out += [(("h2t", i, a), "A") for i in range(NT) for a in range(2)]
    out += [(("logit",), "A"), (("rank",), "D")] + [(("bc", v), "D") for v in range(4)]
    return out


ROT = 6
PLAN = bank_plan()
PLACE = {key: n for n, (key, _) in enumerate(PLAN)}


def const_table():
    import numpy as np
    t = np.arange(P)
    s4 = np.arange(TS)
    cols, parts, at = {}, [], [0]

    def put(name, a):
        a = np.asarray(a, np.float64)
        full = np.zeros((P, a.shape[1]), np.float32)
        full[:a.shape[0]] = a
        cols[name] = (at[0], at[0] + a.shape[1])
        at[0] += a.shape[1]
        parts.append(full)

    put("ident", np.eye(P))
    put("tri", t[:, None] <= t[None, :])
    put("strict", t[:, None] < t[None, :])
    put("ones", np.ones((P, 1)))
    same = (s4[:, None] // DEC_SEQ) == (s4[None, :] // DEC_SEQ)
    put("tri_s", same & (s4[:, None] <= s4[None, :]))
    put("blk_s", same)
    put("own", (s4[:, None] // DEC_SEQ) == np.arange(DEC_BATCH)[None, :])
    put("bmask", np.tile(((s4[None, :] // DEC_SEQ) == np.arange(DEC_BATCH)[:, None]).reshape(1, -1), (P, 1)))
    half = RET_HD // 2
    inv = (10000.0 ** (-np.arange(half, dtype=np.float32) / half)).astype(np.float32)
    pos = np.zeros((P, NT), np.float32)
    pos[:, 0], pos[:, 1] = t, t + P
    pos[:TS, 2] = PAST_LEN + s4 % DEC_SEQ
    ang = (pos[:, :, None] * inv[None, None, :]).astype(np.float32).astype(np.float64)
    put("cos", np.cos(ang).reshape(P, -1))
    put("sin", np.sin(ang).reshape(P, -1))
    lg = np.log1p(-np.exp2(-5.0 - np.arange(RET_HEADS)))
    scale = RET_HD ** -0.5
    d = (t[None, :] - t[:, None])[:, None, :]
    put("dr", np.where(d >= 0, np.exp(d * lg[None, :, None]), 0).reshape(P, -1) * scale)
    d = (s4[None, :] - s4[:, None])[:, None, :]
    put("dr_s", np.where((d >= 0) & same[:, None, :], np.exp(d * lg[None, :, None]), 0).reshape(TS, -1) * scale)
    put("qdec", np.exp((t[:, None] + 1) * lg))
    put("qdec_s", np.exp((s4[:, None] % DEC_SEQ + 1) * lg))
    put("kdec", np.exp((P - 1 - t[:, None]) * lg) * scale)
    put("kdec_s", np.exp((DEC_SEQ - 1 - s4[:, None] % DEC_SEQ) * lg) * scale)
    put("gam", np.tile(np.exp(P * lg), (P, 1)))
    put("gam_s", np.tile(np.exp(DEC_SEQ * lg), (P, 1)))
    put("iota", np.tile(np.arange(2 * BLK), (P, 1)))
    put("slot", np.stack([t % BLK, t % BLK + BLK], 1))
    put("pref", np.tile(N_EXPERTS - np.arange(N_EXPERTS), (P, 1)))
    put("atleast", np.tile(np.arange(N_EXPERTS) < 2, (P, 1)))
    put("gp", (t % 32 == 0)[:, None])
    put("gs", (t[:, None] % 32) == 1 + s4[None, :] // DEC_SEQ)
    valid = np.ones((P, NT))
    valid[TS:, 2] = 0
    put("valid", valid)
    put("eps", np.full((P, 1), EPS))
    return cols, np.concatenate(parts, 1)


class Signal:

    def __init__(self, sem, per_layer):
        self.sem, self.per_layer = sem, per_layer

    def at(self, l, k):
        return l * self.per_layer + k

    def stand(self, eng):
        eng.sem_inc(self.sem, 1)


def trunk(nc, A, O):
    cc, _ = const_table()
    ctx = ExitStack()
    with ctx:
        base = (nc.sbuf_base + 63) // 64 * 64
        top = [base]

        def size(shape):
            n = 4
            for s in shape[1:]:
                n *= s
            return (n + 31) // 32 * 32

        def fixed(name, shape, dt=F32):
            t = nc.alloc_sbuf_tensor_at(name, shape, dt, offset=top[0])
            top[0] += size(shape)
            return t

        class Region:
            def __init__(self, start):
                self.at = start

            def new(self, name, shape, dt=F32):
                t = nc.alloc_sbuf_tensor_at(name, shape, dt, offset=self.at)
                self.at += size(shape)
                return t

        SLOT = KT * CH
        ring = fixed("ring", [P, 3, SLOT])
        x_tm = fixed("x_tm", [P, NT, D_MODEL])
        h_tm = fixed("h_tm", [P, NT, D_MODEL])
        hT = fixed("hT", [P, KT, T])
        lnp = fixed("lnp", [P, 2, D_MODEL])
        pb = top[0]
        fixed("spare", [P, 2, CH])
        part = fixed("part", [P, 2, CH])
        pbr = Region(pb)
        xTb = pbr.new("xTb", [P, KT, 2 * BLK])
        hTb = pbr.new("hTb", [P, 2, P])
        hb = pbr.new("hb", [P, 2, P])
        sg = pbr.new("sg", [P, 2, P])
        con = fixed("con", [P, max(b for _, b in cc.values())])
        cT = fixed("cT", [P, KT, 32])
        vecT = fixed("vecT", [P, V_N])
        halo = fixed("halo", [P, XT + RT, DEC_BATCH * HALO])
        h0rg = fixed("h0rg", [P, RT, DEC_BATCH])
        cl = fixed("cl", [P, 4, RT])
        bc16 = fixed("bc16", [P, 3, SSD_HEADS])
        dts = fixed("dts", [P, 4, NT, SSD_HEADS])
        cum = fixed("cum", [P, 2, NT, SSD_HEADS])
        ex = fixed("ex", [P, 3, NT, SSD_HEADS])
        tbh = fixed("tbh", [P, DEC_BATCH, SSD_HEADS])
        stat = fixed("stat", [P, 64])
        rgl = fixed("rgl", [P, RT, 1 + DEC_BATCH])
        rw = fixed("rw", [P, KT, N_EXPERTS])
        rbias = fixed("rbias", [P, N_EXPERTS])
        wdt = fixed("wdt", [P, KT, SSD_HEADS])
        M = top[0]
        m1 = Region(M)
        R1 = m1.at
        qkvg = m1.new("qkvg", [P, NT, 4 * D_RET])
        r1 = Region(R1)
        xcT = r1.new("xcT", [P, RT, T])
        rgr = r1.new("rgr", [P, RT, T])
        rgi = r1.new("rgi", [P, RT, T])
        rgt = r1.new("rgt", [P, RT, T])
        tailT = r1.new("tailT", [P, XT + RT, HALO * (1 + DEC_BATCH)])
        yrg = m1.new("yrg", [P, RT, T])
        BCT = m1.new("BCT", [P, 4, T])
        yreT = nc.alloc_sbuf_tensor_at("yreT", [P, RET_HEADS, T], F32, offset=m1.at - 4 * T * 4)
        c0 = m1.at
        raw = m1.new("raw", [P, 4, RAWW])
        xsT = m1.new("xsT", [P, 4, T])
        cv = m1.new("cv", [P, 2, CVW])
        convend = m1.at
        r2 = Region(c0)
        Pm = r2.new("Pm", [P, 4, 4 * P])
        Sm = r2.new("Sm", [P, 2 * P])
        assert r2.at <= convend
        r2 = Region(c0)
        Pr = r2.new("Pr", [P, 4 * P])
        Y2 = r2.new("Y2", [P, D_RET])
        Km = r2.new("Km", [TS, 2, D_RET])
        assert r2.at <= convend <= M + 3 * SLOT * 4
        g0 = M + 3 * SLOT * 4
        m1 = Region(g0)
        h0s = m1.new("h0s", [P, 2, SSD_HEADS * SSD_HD])
        S = m1.new("S", [P, SSD_HEADS * SSD_HD])
        xdt = m1.new("xdt", [P, D_SSD])
        xw = m1.new("xw", [P, D_SSD])
        zb = m1.new("zb", [P, NT, D_SSD])
        xs = m1.new("xs", [P, NT, D_SSD + 2 * SSD_STATE])
        mix_end = m1.at
        mod1 = Region(g0).new("mod1", [P, 2, 2, D_MODEL])
        r2 = Region(g0)
        wab = r2.new("wab", [P, 2, RT, P])
        rgo = nc.alloc_sbuf_tensor_at("rgo", [1 + DEC_BATCH, D_RG], F32, offset=g0 + 4096)
        tails = nc.alloc_sbuf_tensor_at("tails", [HALO * (1 + DEC_BATCH), (XT + RT) * P], F32, offset=g0 + 8192)
        R = nc.alloc_sbuf_tensor_at("R", [P, D_RET], F32, offset=g0 + 8192)
        QmB = nc.alloc_sbuf_tensor_at("QmB", [P, RET_HEADS, DEC_BATCH, TS], F32, offset=g0)
        CmB = nc.alloc_sbuf_tensor_at("CmB", [P, SSD_GROUPS, DEC_BATCH, TS], F32, offset=g0 + 8192)
        r2 = Region(g0 + 3 * 4096)
        r0s = r2.new("r0s", [P, 2, D_RET])
        vw = r2.new("vw", [P, D_RET])
        qkT = Region(g0 + 5 * 4096).new("qkT", [P, 2 * RET_HEADS, T])
        rq = Region(g0 + 5 * 4096 + 3 * 4096).new("rq", [P, NT, 2 * D_RET])
        r2 = Region(g0 + 5 * 4096 + 3 * 4096)
        vrow = r2.new("vrow", [V_N, P])
        hrow = r2.new("hrow", [DEC_BATCH * HALO, (XT + RT) * P])
        grow = r2.new("grow", [DEC_BATCH, D_RG])
        bias = nc.alloc_sbuf_tensor_at("bias", [12, CH], F32, offset=pb)
        ada_at = lambda c: part[:, c % 2, :] if c < 6 else qkvg[:, (c - 6) // 2, (c % 2) * CH:(c % 2 + 1) * CH]
        AXb = nc.alloc_sbuf_tensor_at("AXb", [P, 2, 4 * P], F32, offset=pb)
        tmp = nc.alloc_sbuf_tensor_at("tmp", [P, D_MODEL], F32, offset=pb + 4096)
        BmB = Region(c0 + 9216).new("BmB", [TS, 2, 2 * SSD_STATE])
        assert c0 + 9216 + 2048 <= convend
        ring1 = nc.alloc_sbuf_tensor_at("ring1", [P, 3, SLOT], F32, offset=M)
        m2 = Region(g0)
        gate = m2.new("gate", [P, 2, D_MODEL])
        sh2 = m2.new("sh2", [P, 2, D_MODEL])
        ys = nc.alloc_sbuf_tensor_at("ys", [P, 2, D_MODEL], F32, offset=g0 + 8192)
        sc2 = m2.new("sc2", [P, 2, D_MODEL])
        rt = nc.alloc_sbuf_tensor_at("rt", [P, 13, NT, N_EXPERTS], F32, offset=g0 + 2 * 8192)
        acc = m2.new("acc", [P, 2, D_MODEL])
        accs = m2.new("accs", [P, D_MODEL // 4])
        dbc = m2.new("dbc", [P, 4, T])
        selw = m2.new("selw", [P, 2, T])
        selt2 = m2.new("selt2", [P, 2, T])
        sel = m2.new("sel", [P, 2, NT, 2 * BLK])
        selt = m2.new("selt", [P, NT, 2, 2 * BLK])
        dtm = m2.new("dtm", [P, 2, NT, 2])
        scol = m2.new("scol", [P, 2])
        nblk = m2.new("nblk", [P, 5, N_EXPERTS])
        bew = nc.alloc_sbuf_tensor_at("bew", [1, NBMAX, N_EXPERTS], F32, offset=g0 + 3 * 8192)
        bei = m2.new("bei", [1, 64], I32)
        npi = m2.new("npi", [P, N_EXPERTS], I32)
        assert max(mix_end, m2.at) <= nc.sbuf_usable_end

        ps = ctx.enter_context(nc.psum_tensor("ps", [P, 8, 512], F32))

        def C(name, rows=P, lo=0, n=None):
            a, b = cc[name]
            if b - a == 1 and n is not None:
                return con[0:rows, a:b].to_broadcast([rows, n])
            return con[0:rows, a + lo:(b if n is None else a + lo + n)]


        def sem(name):
            return ctx.enter_context(nc.semaphore(name))

        def sig(name, per_layer):
            return Signal(sem(name), per_layer)

        idle = {e: sig(f"stood_{e}", 0) for e in ("pe", "sp", "pool")}

        filled = sig("filled", len(PLAN))
        takers = {"A": sig("taken_act", sum(e == "A" for _, e in PLAN)),
                  "D": sig("taken_dve", sum(e == "D" for _, e in PLAN))}

        def nth_taken(key):
            n = PLACE[key]
            return sum(e == PLAN[n][1] for _, e in PLAN[:n + 1])

        def takes(l, key):
            t = takers[PLAN[PLACE[key]][1]]
            return t.sem, t.at(l, nth_taken(key))

        def emptied(l, key):
            n = PLACE[key]
            return takes(l, PLAN[n - ROT][0]) if n >= ROT else (begun, l + 1)

        def fills(l, key):
            return filled.at(l, PLACE[key] + 1)

        def bank(key):
            return ps[:, PLACE[key] % ROT, :]

        TA, TD, FL = takers["A"].sem, takers["D"].sem, filled.sem

        con_in = sem("con_in")
        c_silu, c_turned, c_ready = sem("c_silu"), sem("c_turned"), sem("c_ready")
        open_ = sem("ring_open")
        begun = sem("layer_begun")
        st_full = [sig(f"stream_full{s}", 16 * PER_SLOT) for s in range(NS)]
        st_used = [sig(f"stream_used{s}", PER_SLOT) for s in range(NS)]
        bias_in = sig("bias_in", 16)
        gate_used = sig("gate_used", 1)
        mod_done = sig("mod_done", 6)
        small_in = sig("small_in", 16 * 17)
        rows_turned = sig("rows_turned", 1)
        wab_zero = sig("wab_zero", 1)
        wab_in = sig("wab_in", 16 * 16)
        h_done = sig("h_done", NT)
        cv_ready = sig("conv_ready", XT + RT)
        cv_out = sig("conv_out", XT + RT)
        tails_out = sig("tails_out", 16 * 4)
        rgo_ready = sig("rg_state_ready", 1)
        rgo_out = sig("rg_state_out", 32)
        rgl_ready = sig("rg_last_ready", 1)
        rg_gates = sig("rg_gates", 1)
        rg_sq = sig("rg_sq", 1)
        rg_root = sig("rg_root", 1)
        rg_done = sig("rg_done", 1)
        lam_abs = sig("lam_abs", 1)
        lam_ln = sig("lam_ln", 1)
        lam_c = sig("lam_c", 1)
        dt_abs = sig("dt_abs", 1)
        dt_ln = sig("dt_ln", 1)
        loga_ready = sig("loga_ready", 1)
        cum_ready = sig("cum_ready", 1)
        cum_exp = sig("cum_exp", 1)
        xw_ready = sig("xw_ready", NT)
        arg_ready = sig("decay_arg_ready", 9)
        exp_ready = sig("decay_ready", 9)
        P_ready = sig("scores_ready", 9)
        S_ready = sig("state_ready", 4)
        S_out = sig("state_out", 16)
        Cm_ready = sig("Cm_ready", 1)
        Bm_ready = sig("Bm_ready", DEC_BATCH)
        h0_in = [sig(f"h0_in{s}", 16 * DEC_BATCH // 2) for s in range(2)]
        h0_new = sig("h0_new", 2 * DEC_BATCH)
        h0_out = [sig(f"h0_out{s}", 16 * DEC_BATCH // 2) for s in range(2)]
        hold_full = sig("hold_full", 3)
        hold_free = sig("hold_free", 3)
        var_ready = sig("var_ready", 8)
        rstd_ready = sig("rstd_ready", 8)
        y_ready = sig("y_ready", NT)
        ssd_done = sig("ssd_done", 1)
        rope_ready = sig("rope_ready", NT)
        Pr_ready = sig("ret_scores_ready", NT)
        vw_ready = sig("vw_ready", NT)
        R_ready = sig("ret_state_ready", 2)
        R_out = sig("ret_state_out", 16)
        Qm_ready = sig("Qm_ready", 1)
        Km_ready = sig("Km_ready", DEC_BATCH)
        r0_in = [sig(f"r0_in{s}", 16 * DEC_BATCH // 2) for s in range(2)]
        r0_new = sig("r0_new", DEC_BATCH)
        r0_out = [sig(f"r0_out{s}", 16 * DEC_BATCH // 2) for s in range(2)]
        yr_ready = sig("yr_ready", NT)
        ret_done = sig("ret_done", 1)
        mix_over = sig("mix_over", 1)
        ln1_in = sig("ln1_in", 32)
        x1_done = sig("x1_done", 1)
        ln2_in = sig("ln2_in", 32)
        h2_ready = sig("h2_ready", NT)
        score_fill = sig("score_fill", 1)
        oh_ready = sig("oh_ready", 1)
        dtm_ready = sig("dtm_ready", 1)
        plan_ready = sig("plan_ready", 1)
        stores_out = sig("stores_out", 1)
        y_out = sem("y_out")
        gu_full = [sem(f"gate_up_full{b}") for b in range(2)]
        dn_full = [sem(f"down_full{b}") for b in range(2)]
        gu_used = [sem(f"gate_up_used{b}") for b in range(2)]
        dn_used = [sem(f"down_used{b}") for b in range(2)]
        sel_ready, g_full, g_taken = sem("sel_ready"), sem("gather_full"), sem("gather_taken")
        u_full, sg_ready, hb_ready = sem("up_full"), sem("silu_ready"), sem("hidden_ready")
        t_full, ht_ready = sem("turned_full"), sem("turned_taken")
        d_full, ysa, ysd = sem("down_out_full"), sem("ys_act"), sem("ys_dve")
        selw_ready, s_full, acc_taken = sem("selw_ready"), sem("spread_full"), sem("acc_taken")

        block = ctx.enter_context(nc.Block())
        w_dt = lambda l: A["w_in"][l][:, C_DT:C_DT + SSD_HEADS].rearrange("(k p) n -> p k n", p=P)

        @block.sync
        def _(sp):
            sp.sem_inc(open_, 1)
            sp.dma_start(con[:], A["con"]).then_inc(con_in, 16)
            sp.dma_start(h_tm[0:1, 0, :], A["c_prompt"]).then_inc(con_in, 16)
            sp.dma_start(h_tm[1:1 + DEC_BATCH, 0, :], A["c_sample"]).then_inc(con_in, 16)
            sp.dma_start(x_tm[:, 0:2, :], A["x_prompt"][0].rearrange("(i p) d -> p i d", p=P)).then_inc(con_in, 16)
            sp.dma_start(x_tm[0:TS, 2, :], A["x_sample"].rearrange("b s d -> (b s) d")).then_inc(con_in, 16)
            sp.dma_start(rw[:], A["router_w"].rearrange("(k p) e -> p k e", p=P)).then_inc(con_in, 16)
            sp.dma_start(rbias[:], A["router_bias"].unsqueeze(0).to_broadcast([P, N_EXPERTS])).then_inc(con_in, 16)
            before = sp.alloc_register("pairs_before")
            sp.reg_mov(before, 0)
            with sp.Fori(0, DEPTH) as l:
                for n, (kind, at) in enumerate(STREAM):
                    s, r = n % NS, n // NS
                    if r:
                        sp.wait_ge(st_used[s].sem, st_used[s].at(l, r))
                    else:
                        sp.wait_ge(open_, l + 1)
                    idle["sp"].stand(sp)
                    if kind == "ada":
                        src = A["w_ada"][l][:, at * CH:(at + 1) * CH].rearrange("(k p) n -> p k n", p=P)
                    elif kind == "in":
                        src = A["w_in"][l][:, at:at + CH].rearrange("(k p) n -> p k n", p=P)
                    else:
                        src = A["w_out"][l][at * 4 * P:(at + 1) * 4 * P, :].rearrange("(k p) n -> p k n", p=P)
                    dst = ring[:, s, :].rearrange("p (k n) -> p k n", n=D_MODEL if kind == "out" else CH)
                    sp.dma_start(dst, src).then_inc(st_full[s].sem, 16)

                def experts(b, e):
                    dst = (ring, ring1)[b]
                    for j, name in enumerate(("exp_w_gate", "exp_w_up")):
                        sp.dma_start(dst[:, j, :].rearrange("p (k n) -> p k n", n=D_EXPERT),
                                     A[name][l, e].rearrange("(k p) n -> p k n", p=P)).then_inc(gu_full[b], 16)

                def experts_down(b, e):
                    dst = (ring, ring1)[b]
                    sp.dma_start(dst[:, 2, :].rearrange("p (k n) -> p k n", n=D_MODEL),
                                 A["exp_w_down"][l, e].rearrange("(k p) n -> p k n", p=P)).then_inc(dn_full[b], 16)

                for s in range(NS):
                    sp.wait_ge(st_used[s].sem, st_used[s].at(l, PER_SLOT))
                    idle["sp"].stand(sp)
                experts(0, 0)
                experts_down(0, 0)
                sp.wait_ge(mix_over.sem, mix_over.at(l, 1))
                idle["sp"].stand(sp)
                experts(1, 1)
                experts_down(1, 1)
                sp.wait_ge(plan_ready.sem, plan_ready.at(l, 1))
                idle["sp"].stand(sp)
                pairs = sp.value_load(npi[0:1, 0:1], min_val=2, max_val=NBMAX // 2)
                done = sp.snap(before)
                with sp.Fori(1, pairs) as q:
                    for b in range(2):
                        e = sp.value_load(bei[0:1, bass.ds(2 * q + b, 1)], min_val=0, max_val=N_EXPERTS - 1)
                        sp.wait_ge(gu_used[b], done + q)
                        experts(b, e)
                        sp.wait_ge(dn_used[b], done + q)
                        experts_down(b, e)
                sp.reg_add(before, before, pairs)
            sp.wait_ge(begun, DEPTH + 1)
            sp.dma_start(O["y_prompt"][0].rearrange("(i p) d -> p i d", p=P), x_tm[:, 0:2, :]).then_inc(y_out, 16)
            sp.dma_start(O["y_sample"].rearrange("b s d -> (b s) d"), x_tm[0:TS, 2, :]).then_inc(y_out, 16)
            sp.wait_ge(y_out, 32)

        @block.gpsimd
        def _(pool):
            with pool.Fori(0, DEPTH) as l:
                pool.wait_ge(begun, l + 1)
                idle["pool"].stand(pool)

                def small(dst, src):
                    pool.dma_start(dst, src).then_inc(small_in.sem, 16)

                def rowsof(name, lead=None):
                    v = A[name][l]
                    return v.rearrange("j (m p) -> (j m) p", p=P) if lead else v.rearrange("(m p) -> m p", p=P)

                small(vrow[V_XW:V_XB, :], rowsof("ssd_conv_w", True))
                small(vrow[V_XB:V_RW, :], rowsof("ssd_conv_b"))
                small(vrow[V_RW:V_RB, :], rowsof("rg_conv_w", True))
                small(vrow[V_RB:V_BA, :], rowsof("rg_conv_b"))
                small(vrow[V_BA:V_BX, :], rowsof("rg_ba"))
                small(vrow[V_BX:V_LAM, :], rowsof("rg_bx"))
                small(vrow[V_LAM:V_N, :], rowsof("rg_lambda"))
                small(hrow[:, 0:SSD_CONV_DIM], A["state_ssd_conv"][l].rearrange("b j c -> (b j) c"))
                small(hrow[:, SSD_CONV_DIM:], A["state_rglru_conv"][l].rearrange("b j c -> (b j) c"))
                small(grow[:], A["state_rglru"][l])
                for n, name in enumerate(("ssd_dt_bias", "ssd_a_log", "ssd_d")):
                    small(bc16[:, n, :], A[name][l].unsqueeze(0).to_broadcast([P, SSD_HEADS]))
                small(lnp[:, 0, :], A["ssd_norm_w"][l].unsqueeze(0).to_broadcast([P, D_SSD]))
                small(lnp[:, 1, 0:D_RET], A["ret_gn_w"][l].unsqueeze(0).to_broadcast([P, D_RET]))
                small(wdt[:], w_dt(l))

                small(bias[:], A["b_ada"][l].rearrange("(c n) -> c n", n=CH))
                pool.wait_ge(h_done.sem, h_done.at(l, NT))
                idle["pool"].stand(pool)
                nc.gpsimd.memset(wab[:], 0.0).then_inc(wab_zero.sem, 1)
                pool.wait_ge(wab_zero.sem, wab_zero.at(l, 1))
                idle["pool"].stand(pool)
                for w, name in enumerate(("rg_wa", "rg_wx")):
                    v = A[name][l].rearrange("(m u) j k -> u j m k", u=2)
                    for u in range(2):
                        lo = u * RG_BLOCK_W
                        for m in range(RT):
                            pool.dma_start(wab[lo:lo + RG_BLOCK_W, w, m, lo:lo + RG_BLOCK_W], v[u, :, m, :]
                                           ).then_inc(wab_in.sem, 16)
                pool.wait_ge(*takes(l, ("tail", 3)))
                idle["pool"].stand(pool)
                for name, c0_, c1_ in (("ssd_conv", 0, SSD_CONV_DIM), ("rglru_conv", SSD_CONV_DIM, (XT + RT) * P)):
                    pool.dma_start(O[name + "_p"][l, 0], tails[0:HALO, c0_:c1_]).then_inc(tails_out.sem, 16)
                    pool.dma_start(O[name + "_s"][l].rearrange("b j c -> (b j) c"), tails[HALO:, c0_:c1_]
                                   ).then_inc(tails_out.sem, 16)
                pool.wait_ge(rgo_ready.sem, rgo_ready.at(l, 1))
                idle["pool"].stand(pool)
                pool.dma_start(O["rglru_p"][l], rgo[0:1, :]).then_inc(rgo_out.sem, 16)
                pool.dma_start(O["rglru_s"][l], rgo[1:, :]).then_inc(rgo_out.sem, 16)
                pool.wait_ge(rgo_out.sem, rgo_out.at(l, 32))
                idle["pool"].stand(pool)

                def load_h0(b):
                    pool.dma_start(h0s[:, b % 2, :].rearrange("n (h v) -> n h v", v=SSD_HD),
                                   A["state_ssd"][l, b].rearrange("h n v -> n h v")).then_inc(h0_in[b % 2].sem, 16)

                load_h0(0)
                load_h0(1)
                pool.wait_ge(S_ready.sem, S_ready.at(l, 4))
                idle["pool"].stand(pool)
                pool.dma_start(O["ssd_p"][l, 0].rearrange("h n v -> n h v"),
                               S[:].rearrange("n (h v) -> n h v", v=SSD_HD)).then_inc(S_out.sem, 16)
                for b in range(DEC_BATCH):
                    pool.wait_ge(h0_new.sem, h0_new.at(l, 2 * b + 2))
                    idle["pool"].stand(pool)
                    pool.dma_start(O["ssd_s"][l, b].rearrange("h n v -> n h v"),
                                   h0s[:, b % 2, :].rearrange("n (h v) -> n h v", v=SSD_HD)
                                   ).then_inc(h0_out[b % 2].sem, 16)
                    if b + 2 < DEC_BATCH:
                        pool.wait_ge(h0_out[b % 2].sem, h0_out[b % 2].at(l, 16 * (b // 2 + 1)))
                        idle["pool"].stand(pool)
                        load_h0(b + 2)
                pool.wait_ge(ssd_done.sem, ssd_done.at(l, 1))
                idle["pool"].stand(pool)

                pool.dma_start(bias[:], A["b_ada"][l].rearrange("(c n) -> c n", n=CH)).then_inc(bias_in.sem, 16)

                def load_r0(b):
                    pool.dma_start(r0s[:, b % 2, :].rearrange("n (h v) -> n h v", v=RET_HD),
                                   A["state_ret"][l, b].rearrange("h n v -> n h v")).then_inc(r0_in[b % 2].sem, 16)

                load_r0(0)
                load_r0(1)
                pool.wait_ge(R_ready.sem, R_ready.at(l, 2))
                idle["pool"].stand(pool)
                pool.dma_start(O["ret_p"][l, 0].rearrange("h n v -> n h v"),
                               R[:].rearrange("n (h v) -> n h v", v=RET_HD)).then_inc(R_out.sem, 16)
                for b in range(DEC_BATCH):
                    pool.wait_ge(r0_new.sem, r0_new.at(l, b + 1))
                    idle["pool"].stand(pool)
                    pool.dma_start(O["ret_s"][l, b].rearrange("h n v -> n h v"),
                                   r0s[:, b % 2, :].rearrange("n (h v) -> n h v", v=RET_HD)
                                   ).then_inc(r0_out[b % 2].sem, 16)
                    if b + 2 < DEC_BATCH:
                        pool.wait_ge(r0_out[b % 2].sem, r0_out[b % 2].at(l, 16 * (b // 2 + 1)))
                        idle["pool"].stand(pool)
                        load_r0(b + 2)
                pool.wait_ge(tails_out.sem, tails_out.at(l, 64))
                idle["pool"].stand(pool)
                pool.wait_ge(S_out.sem, S_out.at(l, 16))
                idle["pool"].stand(pool)
                pool.wait_ge(R_out.sem, R_out.at(l, 16))
                idle["pool"].stand(pool)
                for b in range(2):
                    pool.wait_ge(h0_out[b].sem, h0_out[b].at(l, 16 * DEC_BATCH // 2))
                    idle["pool"].stand(pool)
                    pool.wait_ge(r0_out[b].sem, r0_out[b].at(l, 16 * DEC_BATCH // 2))
                    idle["pool"].stand(pool)
                pool.sem_inc(stores_out.sem, 1)
                pool.wait_ge(ret_done.sem, ret_done.at(l, 1))
                idle["pool"].stand(pool)
                pool.dma_start(lnp[:, 0, :], A["ln1_g"][l].unsqueeze(0).to_broadcast([P, D_MODEL])).then_inc(ln1_in.sem, 16)
                pool.dma_start(lnp[:, 1, :], A["ln1_b"][l].unsqueeze(0).to_broadcast([P, D_MODEL])).then_inc(ln1_in.sem, 16)
                pool.wait_ge(x1_done.sem, x1_done.at(l, 1))
                idle["pool"].stand(pool)
                pool.dma_start(lnp[:, 0, :], A["ln2_g"][l].unsqueeze(0).to_broadcast([P, D_MODEL])).then_inc(ln2_in.sem, 16)
                pool.dma_start(lnp[:, 1, :], A["ln2_b"][l].unsqueeze(0).to_broadcast([P, D_MODEL])).then_inc(ln2_in.sem, 16)

        @block.tensor
        def _(pe):
            mm, tr = nc.tensor.matmul, nc.tensor.transpose
            pe.wait_ge(con_in, 16 * 7)
            pe.wait_ge(c_silu, 1)
            for k in range(KT):
                last = tr(ps[:, 6, 9 * k:9 * k + 9], h_tm[0:9, 0, k * P:(k + 1) * P], C("ident", 9, 0, 9))
            last.then_inc(c_turned, 1)
            pe.wait_ge(c_ready, 1)
            before = pe.alloc_register("pairs_before")
            pe.reg_mov(before, 0)
            with pe.Fori(0, DEPTH) as l:
                pe.wait_ge(begun, l + 1)

                def stream(n):
                    pe.wait_ge(st_full[n % NS].sem, st_full[n % NS].at(l, 16 * (n // NS + 1)))
                    return ring[:, n % NS, :].rearrange("p (k n) -> p k n",
                                                        n=D_MODEL if STREAM[n][0] == "out" else CH)

                pe.wait_ge(small_in.sem, small_in.at(l, 16 * 17))
                pe.wait_ge(*emptied(l, ("vec",)))
                o = bank(("vec",))
                tr(o[:, 0:V_N], vrow[:], C("ident", V_N, 0, V_N)).then_inc(FL, 1)
                pe.wait_ge(*emptied(l, ("halo",)))
                idle["pe"].stand(pe)
                o = bank(("halo",))
                n = DEC_BATCH * HALO
                for m in range(XT + RT):
                    last = tr(o[:, m * n:(m + 1) * n], hrow[:, m * P:(m + 1) * P], C("ident", n, 0, n))
                last.then_inc(FL, 1)
                pe.wait_ge(*emptied(l, ("h0rg",)))
                idle["pe"].stand(pe)
                o = bank(("h0rg",))
                for m in range(RT):
                    last = tr(o[:, m * DEC_BATCH:(m + 1) * DEC_BATCH], grow[:, m * P:(m + 1) * P],
                              C("ident", DEC_BATCH, 0, DEC_BATCH))
                last.then_inc(FL, 1)

                def ada(c, n):
                    w = stream(n)
                    pe.wait_ge(*emptied(l, ("ada", c)))
                    o = bank(("ada", c))
                    for r in range(2):
                        for g in range(4):
                            k = 4 * r + g
                            mm(o[32 * g:32 * g + 32, :], cT[:, k, :], w[:, k, :], start=(r == 0), stop=(r == 1 and g > 0),
                                      skip_group_check=True)
                    mm(o[0:32, :], C("ident", 12, c, 1).to_broadcast([12, 32]), bias[:], start=False, stop=True,
                       skip_group_check=True).then_inc(FL, 1)

                def spread(c):
                    pe.wait_ge(*takes(l, ("ada", c)))
                    idle["pe"].stand(pe)
                    pe.wait_ge(*emptied(l, ("mp", c)))
                    o = bank(("mp", c))
                    mm(o[:, :], C("gp", P, 0, P), ada_at(c), start=True, stop=True).then_inc(FL, 1)
                    pe.wait_ge(*emptied(l, ("ms", c)))
                    o = bank(("ms", c))
                    mm(o[0:TS, :], C("gs"), ada_at(c), start=True, stop=True).then_inc(FL, 1)

                def free_slot(n):
                    pe.drain().then_inc(st_used[n % NS].sem, 1)

                def ada_run(chunks, n0):
                    ada(chunks[0], n0)
                    free_slot(n0)
                    for j, c in enumerate(chunks):
                        if j + 1 < len(chunks):
                            ada(chunks[j + 1], n0 + j + 1)
                            free_slot(n0 + j + 1)
                        spread(c)

                ada_run(range(4), 0)
                n = 4

                def turn_rows(src, key, i):
                    R_ = ROWS[i]
                    for a in range(2):
                        pe.wait_ge(*emptied(l, (key, i, a)))
                        if i == 2:
                            idle["pe"].stand(pe)
                        o = bank((key, i, a))
                        for k in range(4):
                            last = tr(o[:, k * R_:(k + 1) * R_], src[0:R_, i, (4 * a + k) * P:(4 * a + k + 1) * P],
                                      C("ident", R_, 0, R_))
                        last.then_inc(FL, 1)

                for i in range(NT):
                    pe.wait_ge(h_done.sem, h_done.at(l, i + 1))
                    turn_rows(h_tm, "ht", i)
                pe.wait_ge(*takes(l, ("ht", NT - 1, 1)))
                idle["pe"].stand(pe)

                def features(w, m, key):
                    pe.wait_ge(*emptied(l, key))
                    o = bank(key)
                    for k in range(KT):
                        last = mm(o[:, 0:T], w[:, k, m * P:(m + 1) * P], hT[:, k, :], start=(k == 0), stop=(k == KT - 1))
                    last.then_inc(FL, 1)

                def tokens(w, key, c, i):
                    pe.wait_ge(*emptied(l, (key, c, i)))
                    o = bank((key, c, i))
                    for k in range(KT):
                        last = mm(o[0:ROWS[i], :], hT[:, k, T0[i]:T0[i] + ROWS[i]], w[:, k, :], start=(k == 0),
                                  stop=(k == KT - 1))
                    last.then_inc(FL, 1)

                for key in ("rgx", "rgg"):
                    w = stream(n)
                    for m in range(RT):
                        features(w, m, (key, m))
                    free_slot(n)
                    n += 1
                for m in range(XT + 1):
                    if m < XT:
                        if m % 4 == 0:
                            w = stream(n)
                        features(w, m % 4, ("fm", m))
                        if m % 4 == 3:
                            free_slot(n)
                            n += 1
                    if m >= 3:
                        u = m - 3
                        pe.wait_ge(cv_out.sem, cv_out.at(l, RT + u + 1))
                        pe.wait_ge(*emptied(l, ("xst", u)))
                        o = bank(("xst", u))
                        src = xsT[:, u % 4, :] if u < 8 else BCT[:, u - 8, :]
                        for i in range(NT):
                            last = tr(o[0:ROWS[i], i * P:(i + 1) * P], src[:, T0[i]:T0[i] + ROWS[i]], C("ident"))
                        last.then_inc(FL, 1)
                pe.wait_ge(cv_ready.sem, cv_ready.at(l, XT + RT))
                for q in range((XT + RT) // 4):
                    pe.wait_ge(*emptied(l, ("tail", q)))
                    o = bank(("tail", q))
                    for m in range(4):
                        last = tr(o[0:HALO * (1 + DEC_BATCH), m * P:(m + 1) * P], tailT[:, 4 * q + m, :], C("ident"))
                    last.then_inc(FL, 1)
                pe.wait_ge(*emptied(l, ("dt",)))
                o = bank(("dt",))
                for i in range(NT):
                    for k in range(KT):
                        last = mm(o[0:ROWS[i], i * SSD_HEADS:(i + 1) * SSD_HEADS], hT[:, k, T0[i]:T0[i] + ROWS[i]],
                                  wdt[:, k, :], start=(k == 0), stop=(k == KT - 1))
                last.then_inc(FL, 1)
                pe.wait_ge(wab_in.sem, wab_in.at(l, 16 * 16))
                for key, w in (("rga", 0), ("rgi", 1)):
                    for m in range(RT):
                        pe.wait_ge(cv_out.sem, cv_out.at(l, m + 1))
                        pe.wait_ge(*emptied(l, (key, m)))
                        o = bank((key, m))
                        mm(o[:, 0:T], wab[:, w, m, :], xcT[:, m, :], start=True, stop=True).then_inc(FL, 1)
                w = stream(n)
                for j in range(NT):
                    tokens(w, "z", 0, j)
                free_slot(n)
                n += 1

                pe.wait_ge(loga_ready.sem, loga_ready.at(l, 1))
                pe.wait_ge(*emptied(l, ("cum",)))
                o = bank(("cum",))
                for i in range(NT):
                    R_ = ROWS[i]
                    for kind, name in enumerate(("tri", "ones") if i < 2 else ("tri_s", "blk_s")):
                        at = (kind * NT + i) * SSD_HEADS
                        mm(o[0:R_, at:at + SSD_HEADS], C(name, R_, 0, R_), dts[0:R_, 3, i, :], start=True, stop=True)
                at = 2 * NT * SSD_HEADS
                mm(o[:, at:at + DEC_BATCH * SSD_HEADS], C("ones", TS, 0, P), tmp[0:TS, 0:DEC_BATCH * SSD_HEADS],
                   start=True, stop=True).then_inc(FL, 1)
                w_z1 = stream(n)
                tokens(w_z1, "z", 1, 0)
                pe.wait_ge(rgl_ready.sem, rgl_ready.at(l, 1))
                pe.wait_ge(*emptied(l, ("rgo",)))
                o = bank(("rgo",))
                for m in range(RT):
                    last = tr(o[0:1 + DEC_BATCH, m * P:(m + 1) * P], rgl[:, m, :], C("ident"))
                last.then_inc(FL, 1)

                def ssd(i, n0):
                    R_, t0 = ROWS[i], T0[i]
                    tri = "tri" if i < 2 else "tri_s"
                    HQ = 4 if i < 2 else SSD_HEADS
                    pe.wait_ge(*emptied(l, ("cb", i)))
                    if i == 2:
                        idle["pe"].stand(pe)
                    o = bank(("cb", i))
                    for g in range(SSD_GROUPS):
                        last = mm(o[0:R_, g * R_:(g + 1) * R_], BCT[:, g, t0:t0 + R_], BCT[:, 2 + g, t0:t0 + R_],
                                  start=True, stop=True)
                    last.then_inc(FL, 1)
                    for q in range(SSD_HEADS // HQ):
                        pe.wait_ge(*emptied(l, ("dec", i, q)))
                        if i == 2:
                            idle["pe"].stand(pe)
                        o = bank(("dec", i, q))
                        for j in range(HQ):
                            h = q * HQ + j
                            last = mm(o[0:R_, j * R_:(j + 1) * R_], dts[0:R_, 3, i, h:h + 1].to_broadcast([R_, R_]),
                                      C(tri, R_, 0, R_), start=True, stop=True)
                        last.then_inc(FL, 1)
                    if i == 1:
                        pe.wait_ge(S_ready.sem, S_ready.at(l, 2))
                        for g in range(2):
                            pe.wait_ge(*emptied(l, ("yo", i, g)))
                            o = bank(("yo", i, g))
                            mm(o[:, :], BCT[:, 2 + g, t0:t0 + R_], S[:, g * 512:(g + 1) * 512], start=True, stop=True
                               ).then_inc(FL, 1)
                    pe.wait_ge(xw_ready.sem, xw_ready.at(l, i + 1))
                    if i < 2:
                        for g in range(2):
                            pe.wait_ge(*emptied(l, ("cs", i, g)))
                            o = bank(("cs", i, g))
                            mm(o[:, :], xs[:, i, D_SSD + g * P:D_SSD + (g + 1) * P], xw[:, g * 512:(g + 1) * 512],
                               start=True, stop=True).then_inc(FL, 1)
                    else:
                        pe.wait_ge(Cm_ready.sem, Cm_ready.at(l, 1))
                        for b in range(DEC_BATCH):
                            pe.wait_ge(h0_in[b % 2].sem, h0_in[b % 2].at(l, 16 * (b // 2 + 1)))
                            for g in range(2):
                                last = mm(ps[0:TS, 6 + g, :], CmB[:, g, b, :], h0s[:, b % 2, g * 512:(g + 1) * 512],
                                          start=(b == 0), stop=(b == DEC_BATCH - 1), skip_group_check=True)
                                if b == DEC_BATCH - 1:
                                    last.then_inc(hold_full.sem, 1)
                            pe.wait_ge(Bm_ready.sem, Bm_ready.at(l, b + 1))
                            for g in range(2):
                                pe.wait_ge(*emptied(l, ("st", b, g)))
                                o = bank(("st", b, g))
                                mm(o[:, :], BmB[:, b % 2, g * P:(g + 1) * P], xw[0:TS, g * 512:(g + 1) * 512],
                                   start=True, stop=True).then_inc(FL, 1)
                            if b in FILLER:
                                c, j = FILLER[b]
                                tokens(stream(n0 + c - 2), "q", c, j)
                                if j == NT - 1:
                                    free_slot(n0 + c - 2)
                    if i == 0:
                        for j in (1, 2):
                            tokens(w_z1, "z", 1, j)
                        free_slot(n0)
                    pe.wait_ge(P_ready.sem, P_ready.at(l, (4, 8, 9)[i]))
                    for g in range(2):
                        pe.wait_ge(*emptied(l, ("yi", i, g)))
                        if i == 2:
                            idle["pe"].stand(pe)
                        o = bank(("yi", i, g))
                        for j in range(HG):
                            h = g * HG + j
                            p_ = (Pm[0:R_, h // 4, (h % 4) * P:(h % 4) * P + P] if i < 2
                                  else Pm[0:R_, 0, h * TS:(h + 1) * TS])
                            last = mm(o[0:R_, j * SSD_HD:(j + 1) * SSD_HD], p_, xdt[0:R_, h * SSD_HD:(h + 1) * SSD_HD],
                                      start=True, stop=True)
                        last.then_inc(FL, 1)

                ssd(0, n)
                n += 1
                for i in range(2):
                    if i:
                        ssd(i, n)
                    w = stream(n)
                    for j in range(NT):
                        tokens(w, "q", i, j)
                    free_slot(n)
                    n += 1
                ssd(2, n)
                n += 2
                n_out, n_ada = n, n + 2

                def mix_a(i, a):
                    w = [stream(n_out), stream(n_out + 1)]
                    if a == 0:
                        pe.wait_ge(*takes(l, ("yt", i, 1)))
                        idle["pe"].stand(pe)
                    pe.wait_ge(*emptied(l, ("mix_a", i, a)))
                    o = bank(("mix_a", i, a))
                    for k in range(KT):
                        last = mm(o[0:ROWS[i], :], hT[:, k, T0[i]:T0[i] + ROWS[i]],
                                  w[k // 4][:, k % 4, a * 512:(a + 1) * 512], start=(k == 0), stop=(k == KT - 1))
                    last.then_inc(FL, 1)

                def ada_here(c):
                    ada(c, n_ada + c - 4)
                    free_slot(n_ada + c - 4)

                for i in range(2):
                    pe.wait_ge(y_ready.sem, y_ready.at(l, i + 1))
                    turn_rows(h_tm, "yt", i)
                for a in range(2):
                    mix_a(0, a)
                pe.wait_ge(y_ready.sem, y_ready.at(l, 3))
                turn_rows(h_tm, "yt", 2)
                mix_a(1, 0)
                for i in range(NT):
                    pe.wait_ge(rope_ready.sem, rope_ready.at(l, i + 1))
                    turn_rows(rq, "qk", i)

                def ret(i):
                    R_, t0 = ROWS[i], T0[i]
                    pe.wait_ge(*emptied(l, ("sc", i)))
                    if i == 2:
                        idle["pe"].stand(pe)
                    o = bank(("sc", i))
                    for h in range(RET_HEADS):
                        last = mm(o[0:R_, h * R_:(h + 1) * R_], qkT[:, RET_HEADS + h, t0:t0 + R_], qkT[:, h, t0:t0 + R_],
                                  start=True, stop=True)
                    last.then_inc(FL, 1)
                    if i == 0:
                        mix_a(1, 1)
                    if i == 1:
                        pe.wait_ge(R_ready.sem, R_ready.at(l, 1))
                        pe.wait_ge(*emptied(l, ("ro", i)))
                        o = bank(("ro", i))
                        for h in range(RET_HEADS):
                            last = mm(o[:, h * P:(h + 1) * P], qkT[:, h, t0:t0 + R_], R[:, h * P:(h + 1) * P],
                                      start=True, stop=True)
                        last.then_inc(FL, 1)
                    pe.wait_ge(vw_ready.sem, vw_ready.at(l, i + 1))
                    if i < 2:
                        pe.wait_ge(*emptied(l, ("rs", i)))
                        o = bank(("rs", i))
                        for h in range(RET_HEADS):
                            last = mm(o[:, h * P:(h + 1) * P], rq[:, i, D_RET + h * P:D_RET + (h + 1) * P],
                                      vw[:, h * P:(h + 1) * P], start=True, stop=True)
                        last.then_inc(FL, 1)
                    else:
                        pe.wait_ge(Qm_ready.sem, Qm_ready.at(l, 1))
                        for b in range(DEC_BATCH):
                            pe.wait_ge(r0_in[b % 2].sem, r0_in[b % 2].at(l, 16 * (b // 2 + 1)))
                            for h in range(RET_HEADS):
                                last = mm(ps[0:TS, 6, h * P:(h + 1) * P], QmB[:, h, b, :], r0s[:, b % 2, h * P:(h + 1) * P],
                                          start=(b == 0 and h == 0), stop=(b == DEC_BATCH - 1), skip_group_check=True)
                            if b == DEC_BATCH - 1:
                                last.then_inc(hold_full.sem, 1)
                            pe.wait_ge(Km_ready.sem, Km_ready.at(l, b + 1))
                            pe.wait_ge(*emptied(l, ("rt", b)))
                            o = bank(("rt", b))
                            for h in range(RET_HEADS):
                                last = mm(o[:, h * P:(h + 1) * P], Km[:, b % 2, h * P:(h + 1) * P],
                                          vw[0:TS, h * P:(h + 1) * P], start=True, stop=True)
                            last.then_inc(FL, 1)
                            if 1 <= b <= 6:
                                ada_here(5 + b)
                    if i == 0:
                        mix_a(2, 0)
                    pe.wait_ge(Pr_ready.sem, Pr_ready.at(l, i + 1))
                    pe.wait_ge(*emptied(l, ("ri", i)))
                    if i == 2:
                        idle["pe"].stand(pe)
                    o = bank(("ri", i))
                    for h in range(RET_HEADS):
                        last = mm(o[0:R_, h * P:(h + 1) * P], Pr[0:R_, h * R_:(h + 1) * R_],
                                  qkvg[0:R_, i, 2 * D_RET + h * P:2 * D_RET + (h + 1) * P], start=True, stop=True)
                    last.then_inc(FL, 1)
                    if i == 0:
                        mix_a(2, 1)
                        free_slot(n_out)
                        free_slot(n_out + 1)
                    if i == 1:
                        pe.wait_ge(bias_in.sem, bias_in.at(l, 16))
                        ada_here(4)
                        ada_here(5)
                    pe.wait_ge(yr_ready.sem, yr_ready.at(l, i + 1))
                    pe.wait_ge(*emptied(l, ("yrt", i)))
                    if i == 2:
                        idle["pe"].stand(pe)
                    o = bank(("yrt", i))
                    for h in range(RET_HEADS):
                        last = tr(o[:, h * R_:(h + 1) * R_], Y2[0:R_, h * P:(h + 1) * P], C("ident", R_, 0, R_))
                    last.then_inc(FL, 1)

                pe.wait_ge(hold_free.sem, hold_free.at(l, 2))
                pe.wait_ge(*takes(l, ("qk", 2, 1)))
                idle["pe"].stand(pe)
                for i in range(NT):
                    ret(i)
                for c in (4, 5):
                    spread(c)

                pe.wait_ge(*takes(l, ("yrt", 2)))
                idle["pe"].stand(pe)
                n = n_ada + 8
                w = [stream(n), stream(n + 1)]
                for i in range(NT):
                    for a in range(2):
                        pe.wait_ge(*emptied(l, ("mix", i, a)))
                        o = bank(("mix", i, a))
                        for k in range(8):
                            y = (yrg, yreT)[k // 4][:, k % 4, T0[i]:T0[i] + ROWS[i]]
                            last = mm(o[0:ROWS[i], :], y, w[k // 4][:, k % 4, a * 512:(a + 1) * 512],
                                      start=(k == 0), stop=(k == 7))
                        last.then_inc(FL, 1)
                free_slot(n)
                free_slot(n + 1)
                n += 2
                for c in range(6, 12):
                    spread(c)
                pe.drain().then_inc(mix_over.sem, 1)
                assert n == len(STREAM)

                for i in range(NT):
                    pe.wait_ge(h2_ready.sem, h2_ready.at(l, i + 1))
                    turn_rows(h_tm, "h2t", i)
                pe.wait_ge(*takes(l, ("h2t", 2, 1)))
                idle["pe"].stand(pe)
                pe.wait_ge(*emptied(l, ("logit",)))
                o = bank(("logit",))
                for i in range(NT):
                    for k in range(KT):
                        last = mm(o[0:ROWS[i], i * N_EXPERTS:(i + 1) * N_EXPERTS], hT[:, k, T0[i]:T0[i] + ROWS[i]],
                                  rw[:, k, :], start=(k == 0), stop=(k == KT - 1))
                last.then_inc(FL, 1)
                pe.wait_ge(oh_ready.sem, oh_ready.at(l, 1))
                pe.wait_ge(*emptied(l, ("rank",)))
                o = bank(("rank",))
                for i in range(NT + 1):
                    R_ = ROWS[i] if i < NT else P
                    upto = list(range(min(i, NT - 1) + 1))
                    for j in upto:
                        K_ = ROWS[j]
                        st = C("strict" if j == i else "ones", K_, 0, R_)
                        last = mm(o[0:R_, i * N_EXPERTS:(i + 1) * N_EXPERTS], st, rt[0:K_, 7, j, :],
                                  start=(j == 0), stop=(j == upto[-1]))
                last.then_inc(FL, 1)
                pe.wait_ge(dtm_ready.sem, dtm_ready.at(l, 1))
                for v in range(4):
                    pe.wait_ge(*emptied(l, ("bc", v)))
                    o = bank(("bc", v))
                    for i in range(NT):
                        R_ = ROWS[i]
                        last = mm(o[:, T0[i]:T0[i] + R_], dtm[0:R_, v // 2, i, v % 2:v % 2 + 1].to_broadcast([R_, P]),
                                  C("ident", R_, 0, R_), start=True, stop=True)
                    last.then_inc(FL, 1)

                pe.wait_ge(*takes(l, ("bc", 3)))
                idle["pe"].stand(pe)
                pe.wait_ge(hold_free.sem, hold_free.at(l, 3))
                idle["pe"].stand(pe)
                done = pe.snap(before)
                pairs = pe.value_load(npi[0:1, 0:1], min_val=2, max_val=NBMAX // 2)

                def gather(q, count):
                    pe.wait_ge(sel_ready, count)
                    for k in range(KT):
                        for i in range(NT):
                            last = mm(ps[:, 6, k * 2 * BLK:(k + 1) * 2 * BLK], h_tm[0:ROWS[i], i, k * P:(k + 1) * P],
                                      sel[0:ROWS[i], 0, i, :], start=(i == 0), stop=(i == NT - 1))
                    last.then_inc(g_full, 1)

                gather(0, done + l + 1)
                with pe.Fori(0, pairs) as q:
                    d = pe.snap(done + q)
                    pe.wait_ge(g_taken, d + l + 2)
                    for b in range(2):
                        w = (ring, ring1)[b]
                        pe.wait_ge(gu_full[b], 32 * d + 32)
                        pe.wait_ge(hb_ready, 2 * d + 1)
                        for k in range(KT):
                            for j in range(4):
                                last = mm(ps[32 * j:32 * j + 32, b, 0:2 * P], xTb[:, k, b * BLK:(b + 1) * BLK],
                                          w[:, 0:2, k * D_EXPERT + j * P:k * D_EXPERT + (j + 1) * P],
                                          start=(k == 0), stop=(k == KT - 1), skip_group_check=True)
                        last.then_inc(u_full, 1)
                        pe.drain().then_inc(gu_used[b], 1)

                    def turn(b):
                        pe.wait_ge(hb_ready, 2 * d + 2 + b)
                        pe.wait_ge(ht_ready, 2 * d + 1 + b)
                        tr(ps[:, 7, b * P:(b + 1) * P], hb[:, b, :], C("ident")).then_inc(t_full, 1)

                    turn(0)
                    gather(q + 1, d + l + 2)
                    turn(1)
                    for b in range(2):
                        w = (ring, ring1)[b]
                        pe.wait_ge(dn_full[b], 16 * d + 16)
                        pe.wait_ge(ht_ready, 2 * d + 2 + b)
                        for a in range(2):
                            pe.wait_ge((ysa, ysd)[a], 2 * d + 1 + b)
                            for j in range(4):
                                last = mm(ps[32 * j:32 * j + 32, 2 + a, :], hTb[:, b, j * BLK:(j + 1) * BLK],
                                          w[:, 2, j * D_MODEL + a * 512:j * D_MODEL + (a + 1) * 512],
                                          start=True, stop=True)
                            last.then_inc(d_full, 1)
                        pe.drain().then_inc(dn_used[b], 1)
                    pe.wait_ge(selw_ready, d + 1)
                    pe.wait_ge(ysa, 2 * d + 3)
                    pe.wait_ge(ysd, 2 * d + 3)
                    for j in range(5):
                        pe.wait_ge(acc_taken, 5 * d + 1 + (0, 0, 1, 2, 3)[j])
                        o = ps[:, 4 + j % 2, :]
                        if j < 4:
                            i, a = divmod(j, 2)
                            for b in range(2):
                                last = mm(o[:, :], selw[:, b, T0[i]:T0[i] + P], ys[:, b, a * 512:(a + 1) * 512],
                                          start=(b == 0), stop=(b == 1))
                        else:
                            for b in range(2):
                                for c in range(4):
                                    last = mm(o[32 * c:32 * c + 32, 0:256], selw[:, b, T0[2]:T], ys[:, b, c * 256:(c + 1) * 256],
                                              start=(b == 0), stop=(b == 1), skip_group_check=True)
                        last.then_inc(s_full, 1)
                pe.reg_add(before, before, pairs)
                pe.drain().then_inc(open_, 1)

        @block.scalar
        def _(act):
            f = nc.scalar.activation
            cp = lambda o_, i_: f(o_, i_, ACT.Copy)
            act.wait_ge(con_in, 16 * 7)
            f(h_tm[0:9, 0, :], h_tm[0:9, 0, :], ACT.Silu).then_inc(c_silu, 1)
            for s_ in (g_taken, ht_ready, ysa):
                act.sem_inc(s_, 1)
            before = act.alloc_register("pairs_before")
            act.reg_mov(before, 0)
            with act.Fori(0, DEPTH) as l:
                def take_rows(dst, key, i):
                    R_ = ROWS[i]
                    for a in range(2):
                        act.wait_ge(filled.sem, fills(l, (key, i, a)))
                        o = bank((key, i, a))
                        cp(dst[:, 4 * a:4 * a + 4, T0[i]:T0[i] + R_],
                           o[:, 0:4 * R_].rearrange("p (k t) -> p k t", k=4)).then_inc(TA, 1)

                def take_ada(chunks):
                    for c in chunks:
                        act.wait_ge(filled.sem, fills(l, ("ada", c)))
                        o = bank(("ada", c))
                        if 2 <= c < 6:
                            act.wait_ge(mod_done.sem, mod_done.at(l, c - 1))
                        cp(ada_at(c), o[:, :]).then_inc(TA, 1)

                take_ada(range(4))
                for i in range(NT):
                    take_rows(hT, "ht", i)

                act.wait_ge(lam_abs.sem, lam_abs.at(l, 1))
                f(cl[:, 2, :], cl[:, 1, :], ACT.Exp, scale=-1.0)
                act.drain()
                f(cl[:, 2, :], cl[:, 2, :], ACT.Ln, bias=1.0).then_inc(lam_ln.sem, 1)

                def take_raw(u, key):
                    act.wait_ge(filled.sem, fills(l, key))
                    o = bank(key)
                    if u >= 4:
                        act.wait_ge(cv_ready.sem, cv_ready.at(l, u - 3))
                    cp(raw[:, u % 4, HALO:SS], o[:, 0:SEQ])
                    cp(raw[:, u % 4, SS:].rearrange("p (b j) -> p b j", b=DEC_BATCH)[:, :, HALO:],
                       o[:, SEQ:T].rearrange("p (b j) -> p b j", b=DEC_BATCH)).then_inc(TA, 1)

                def conv_out(u):
                    act.wait_ge(cv_ready.sem, cv_ready.at(l, u + 1))
                    fn = ACT.Copy if u < RT else ACT.Silu
                    m = u - RT
                    dst = xcT[:, u, :] if u < RT else xsT[:, m % 4, :] if m < 8 else BCT[:, m - 8, :]
                    src = cv[:, u % 2, :]
                    f(dst[:, 0:SEQ], src[:, 0:SEQ], fn)
                    f(dst[:, SEQ:T].rearrange("p (b j) -> p b j", b=DEC_BATCH)[:, 0:DEC_BATCH - 1, :],
                      src[:, SS:SS + 7 * (DEC_BATCH - 1)].rearrange("p (b j) -> p b j", j=7)[:, :, 0:DEC_SEQ], fn)
                    f(dst[:, T - DEC_SEQ:T], src[:, CVW - DEC_SEQ:CVW], fn).then_inc(cv_out.sem, 1)

                for m in range(RT):
                    take_raw(m, ("rgx", m))
                for m in range(RT):
                    act.wait_ge(filled.sem, fills(l, ("rgg", m)))
                    o = bank(("rgg", m))
                    f(yrg[:, m, :], o[:, 0:T], ACT.Gelu_apprx_tanh).then_inc(TA, 1)
                for u in range(RT):
                    conv_out(u)
                for m in range(XT + 1):
                    if m < XT:
                        take_raw(RT + m, ("fm", m))
                    if m >= 2:
                        conv_out(RT + m - 2)
                    if m >= 3:
                        u = m - 3
                        act.wait_ge(filled.sem, fills(l, ("xst", u)))
                        o = bank(("xst", u))
                        cp(xs[:, 0:2, u * P:(u + 1) * P],
                           o[:, 0:2 * P].rearrange("p (i n) -> p i n", i=2))
                        cp(xs[0:TS, 2, u * P:(u + 1) * P], o[0:TS, 2 * P:3 * P]).then_inc(TA, 1)
                conv_out(RT + XT - 1)
                for q in range((XT + RT) // 4):
                    act.wait_ge(filled.sem, fills(l, ("tail", q)))
                    o = bank(("tail", q))
                    cp(tails[:, q * 512:(q + 1) * 512], o[0:HALO * (1 + DEC_BATCH), :]) .then_inc(TA, 1)

                def take_z(c, i):
                    act.wait_ge(filled.sem, fills(l, ("z", c, i)))
                    o = bank(("z", c, i))
                    f(zb[0:ROWS[i], i, c * CH:(c + 1) * CH], o[0:ROWS[i], :], ACT.Silu).then_inc(TA, 1)

                act.wait_ge(dt_abs.sem, dt_abs.at(l, 1))
                f(dts[:, 2, :, :], dts[:, 2, :, :], ACT.Exp, scale=-1.0)
                f(bc16[:, 1, :], bc16[:, 1, :], ACT.Exp)
                act.drain()
                f(dts[:, 2, :, :], dts[:, 2, :, :], ACT.Ln, bias=1.0).then_inc(dt_ln.sem, 1)

                for key, dst, row in (("rga", rgr, V_BA), ("rgi", rgi, V_BX)):
                    for m in range(RT):
                        act.wait_ge(filled.sem, fills(l, (key, m)))
                        o = bank((key, m))
                        f(dst[:, m, :], o[:, 0:T], ACT.Sigmoid, bias=vecT[:, row + m:row + m + 1]).then_inc(TA, 1)
                act.drain()
                act.wait_ge(lam_c.sem, lam_c.at(l, 1))
                for m in range(RT):
                    f(rgt[:, m, :], rgr[:, m, :], ACT.Tanh, scale=cl[:, 1, m:m + 1])
                act.drain()
                for m in range(RT):
                    last = f(rgr[:, m, :], rgr[:, m, :], ACT.Exp, scale=cl[:, 0, m:m + 1])
                last.then_inc(rg_gates.sem, 1)
                act.wait_ge(rg_sq.sem, rg_sq.at(l, 1))
                f(rgt[:, :, :], rgt[:, :, :], ACT.Sqrt).then_inc(rg_root.sem, 1)
                for i in range(NT):
                    take_z(0, i)

                act.wait_ge(cum_ready.sem, cum_ready.at(l, 1))
                f(ex[:, 2, :, :], ex[:, 2, :, :], ACT.Exp)
                f(ex[:, 0:2, :, :], cum[:, :, :, :], ACT.Exp)
                f(tbh[:], tbh[:], ACT.Exp).then_inc(cum_exp.sem, 1)
                take_z(1, 0)

                def rstd(k, R_, lo, n_):
                    act.wait_ge(var_ready.sem, var_ready.at(l, k))
                    v = stat[0:R_, lo:lo + n_]
                    f(v, v, ACT.Ln, bias=C("eps", R_))
                    act.drain()
                    f(v, v, ACT.Exp, scale=-0.5).then_inc(rstd_ready.sem, 1)

                for i in range(NT):
                    for q in range(4 if i < 2 else 1):
                        n_ = (0, 4, 8)[i] + q
                        act.wait_ge(arg_ready.sem, arg_ready.at(l, n_ + 1))
                        b_ = AXb[0:ROWS[i], n_ % 2, :]
                        f(b_, b_, ACT.Exp).then_inc(exp_ready.sem, 1)
                    if i == 0:
                        take_z(1, 1)
                        take_z(1, 2)
                    if i < 2:
                        rstd(i + 1, ROWS[i], 0, 2)
                    if i == 0:
                        act.wait_ge(rg_done.sem, rg_done.at(l, 1))
                    for c in (i,) if i < 2 else (2, 3):
                        for j in range(NT):
                            act.wait_ge(filled.sem, fills(l, ("q", c, j)))
                            o = bank(("q", c, j))
                            f(qkvg[0:ROWS[j], j, c * CH:(c + 1) * CH], o[0:ROWS[j], :],
                              ACT.Copy if c < 3 else ACT.Silu).then_inc(TA, 1)

                def take_mix_a(i, a):
                    act.wait_ge(filled.sem, fills(l, ("mix_a", i, a)))
                    o = bank(("mix_a", i, a))
                    cp(h_tm[0:ROWS[i], i, a * 512:(a + 1) * 512], o[0:ROWS[i], :]).then_inc(TA, 1)

                take_rows(hT, "yt", 0)
                take_rows(hT, "yt", 1)
                rstd(3, TS, 0, 2)
                take_mix_a(0, 0)
                take_mix_a(0, 1)
                take_rows(hT, "yt", 2)
                take_mix_a(1, 0)
                for i in range(NT):
                    take_rows(qkT, "qk", i)
                for i in range(NT):
                    if i == 0:
                        take_mix_a(1, 1)
                        take_mix_a(2, 0)
                    if i == 2:
                        take_ada(range(6, 12))
                    rstd(NT + i + 1, ROWS[i], 0, RET_HEADS)
                    if i == 0:
                        take_mix_a(2, 1)
                    if i == 1:
                        take_ada((4, 5))
                    act.wait_ge(filled.sem, fills(l, ("yrt", i)))
                    o = bank(("yrt", i))
                    R_ = ROWS[i]
                    cp(yreT[:, :, T0[i]:T0[i] + R_], o[:, 0:4 * R_].rearrange("p (k t) -> p k t", k=4)).then_inc(TA, 1)
                act.wait_ge(stores_out.sem, stores_out.at(l, 1))
                for c in range(6, 12):
                    if c == 10:
                        rstd(2 * NT + 1, P, 0, NT)
                        act.wait_ge(gate_used.sem, gate_used.at(l, 1))
                    dst, sl = (sh2, sc2, gate)[c // 2 - 3], slice(c % 2 * CH, (c % 2 + 1) * CH)
                    for w_, (name, R_) in enumerate((("mp", P), ("ms", TS))):
                        act.wait_ge(filled.sem, fills(l, (name, c)))
                        o = bank((name, c))
                        f(dst[0:R_, w_, sl], o[0:R_, :], ACT.Identity, bias=0.0 if c < 8 else 1.0).then_inc(TA, 1)
                for i in range(NT):
                    take_rows(hT, "h2t", i)
                act.wait_ge(score_fill.sem, score_fill.at(l, 1))
                act.wait_ge(filled.sem, fills(l, ("logit",)))
                o = bank(("logit",))
                f(rt[:, 0, 0:2, :], o[:, 0:2 * N_EXPERTS].rearrange("p (i e) -> p i e", i=2), ACT.Sigmoid)
                f(rt[0:TS, 0, 2, :], o[0:TS, 2 * N_EXPERTS:3 * N_EXPERTS], ACT.Sigmoid).then_inc(TA, 1)

                act.wait_ge(plan_ready.sem, plan_ready.at(l, 1))
                done = act.snap(before)
                pairs = act.value_load(npi[0:1, 0:1], min_val=2, max_val=NBMAX // 2)

                def take_gather(count):
                    act.wait_ge(g_full, count)
                    cp(xTb[:], ps[:, 6, :].rearrange("p (k t) -> p k t", k=KT)).then_inc(g_taken, 1)

                take_gather(done + l + 1)
                with act.Fori(0, pairs) as q:
                    d = act.snap(done + q)
                    for b in range(2):
                        act.wait_ge(u_full, 2 * d + 1 + b)
                        f(sg[:, b, :], ps[:, b, 0:P], ACT.Silu).then_inc(sg_ready, 1)

                    def take_turned(b):
                        act.wait_ge(t_full, 2 * d + 1 + b)
                        cp(hTb[:, b, :], ps[:, 7, b * P:(b + 1) * P]).then_inc(ht_ready, 1)

                    take_turned(0)
                    take_gather(d + l + 2)
                    take_turned(1)
                    for b in range(2):
                        act.wait_ge(d_full, 4 * d + 1 + 2 * b)
                        cp(ys[:, b, 0:512], ps[:, 2, :]).then_inc(ysa, 1)
                act.reg_add(before, before, pairs)
                rstd(2 * NT + 2, P, 0, NT)

        @block.vector
        def _(dve):
            V = nc.vector
            tt, ts, stt, cpy = V.tensor_tensor, V.tensor_scalar, V.scalar_tensor_tensor, V.tensor_copy
            D = dve.drain
            V.memset(cT[:], 0.0)
            V.memset(dts[:], 0.0)
            V.memset(cum[:], 0.0)
            V.memset(stat[:], 1.0)
            for s_ in (hb_ready, ysd, acc_taken):
                dve.sem_inc(s_, 1)
            D()
            dve.wait_ge(c_turned, 1)
            cpy(cT[:, :, 0:9], ps[:, 6, 0:72].rearrange("p (k c) -> p k c", k=KT)).then_inc(c_ready, 1)
            dve.drain().then_inc(begun, 1)
            before = dve.alloc_register("pairs_before")
            dve.reg_mov(before, 0)

            def over(ap, n_, axis=2):
                sh = list(ap.shape)
                sh.insert(axis, n_)
                return ap.unsqueeze(axis).to_broadcast(sh)

            with dve.Fori(0, DEPTH) as l:
                dve.wait_ge(filled.sem, fills(l, ("vec",)))
                o = bank(("vec",))
                cpy(vecT[:], o[:, 0:V_N]).then_inc(TD, 1)
                dve.wait_ge(filled.sem, fills(l, ("halo",)))
                o = bank(("halo",))
                cpy(halo[:].rearrange("p m n -> p (m n)"), o[:, 0:(XT + RT) * DEC_BATCH * HALO]).then_inc(TD, 1)
                dve.wait_ge(filled.sem, fills(l, ("h0rg",)))
                o = bank(("h0rg",))
                cpy(h0rg[:].rearrange("p m n -> p (m n)"), o[:, 0:RT * DEC_BATCH]).then_inc(TD, 1)
                V.memset(raw[:, :, 0:HALO], 0.0)
                D()
                lam = vecT[:, V_LAM:V_N]
                ts(cl[:, 1, :], lam, -1.0, None, ALU.mult)
                D()
                tt(cl[:, 1, :], cl[:, 1, :], lam, ALU.max)
                ts(cl[:, 0, :], lam, -1.0, 0.0, ALU.mult, ALU.max)
                D().then_inc(lam_abs.sem, 1)

                def mods(chunks):
                    for c in chunks:
                        j, a = divmod(c, 2)
                        dst = (mod1[:, 0], mod1[:, 1], gate)[j]
                        one = 1.0 if j else 0.0
                        sl = slice(a * CH, (a + 1) * CH)
                        dve.wait_ge(filled.sem, fills(l, ("mp", c)))
                        o = bank(("mp", c))
                        ts(dst[:, 0, sl], o[:, :], one, None, ALU.add).then_inc(TD, 1)
                        dve.wait_ge(filled.sem, fills(l, ("ms", c)))
                        o = bank(("ms", c))
                        ts(dst[0:TS, 1, sl], o[0:TS, :], one, None, ALU.add).then_inc(TD, 1)
                        dve.drain().then_inc(mod_done.sem, 1)

                mods(range(4))
                for i in range(NT):
                    R_, w_ = ROWS[i], int(i == 2)
                    tt(h_tm[0:R_, i, :], x_tm[0:R_, i, :], mod1[0:R_, 1, w_, :], ALU.mult)
                    D()
                    tt(h_tm[0:R_, i, :], h_tm[0:R_, i, :], mod1[0:R_, 0, w_, :], ALU.add).then_inc(h_done.sem, 1)
                dve.wait_ge(lam_ln.sem, lam_ln.at(l, 1))
                tt(cl[:, 3, :], cl[:, 0, :], cl[:, 2, :], ALU.add)
                D()
                ts(cl[:, 0, :], cl[:, 3, :], -RG_C, None, ALU.mult)
                ts(cl[:, 1, :], cl[:, 3, :], RG_C, None, ALU.mult)
                D().then_inc(lam_c.sem, 1)

                for u in range(RT + XT):
                    key = ("rgx", u) if u < RT else ("fm", u - RT)
                    m = u if u < RT else u - RT
                    mt = XT + u if u < RT else m
                    w0, nm, b0 = (V_RW, RT, V_RB) if u < RT else (V_XW, XT, V_XB)
                    tap = lambda j: vecT[:, w0 + j * nm + m:w0 + j * nm + m + 1]
                    r_, c_ = raw[:, u % 4, :], cv[:, u % 2, :]
                    seqs = r_[:, SS:].rearrange("p (b j) -> p b j", b=DEC_BATCH)
                    if u >= 4:
                        dve.wait_ge(cv_ready.sem, cv_ready.at(l, u - 3))
                    cpy(seqs[:, :, 0:HALO], halo[:, mt, :].rearrange("p (b j) -> p b j", b=DEC_BATCH))
                    D()
                    dve.wait_ge(*takes(l, key))
                    cpy(tailT[:, mt, 0:HALO], r_[:, SS - HALO:SS])
                    cpy(tailT[:, mt, HALO:].rearrange("p (b j) -> p b j", b=DEC_BATCH), seqs[:, :, DEC_SEQ:])
                    if u >= 2:
                        dve.wait_ge(cv_out.sem, cv_out.at(l, u - 1))
                    ts(c_, r_[:, 0:CVW], tap(0), vecT[:, b0 + m:b0 + m + 1], ALU.mult, ALU.add)
                    for j in range(1, CONV_WIDTH):
                        D()
                        stt(c_, r_[:, j:j + CVW], tap(j), c_, ALU.mult, ALU.add)
                    dve.drain().then_inc(cv_ready.sem, 1)

                dve.wait_ge(filled.sem, fills(l, ("dt",)))
                o = bank(("dt",))
                tt(dts[:, 0, 0:2, :], o[:, 0:32].rearrange("p (i h) -> p i h", i=2), over(bc16[:, 0, :], 2, 1), ALU.add)
                tt(dts[0:TS, 0, 2, :], o[0:TS, 32:48], bc16[0:TS, 0, :], ALU.add).then_inc(TD, 1)
                D()
                ts(dts[:, 1], dts[:, 0], -1.0, None, ALU.mult)
                D()
                tt(dts[:, 2], dts[:, 0], dts[:, 1], ALU.max)
                D().then_inc(dt_abs.sem, 1)
                dve.wait_ge(dt_ln.sem, dt_ln.at(l, 1))
                stt(dts[:, 1], dts[:, 0], 0.0, dts[:, 2], ALU.max, ALU.add)
                D()
                stt(dts[:, 3], dts[:, 1], -1.0, over(bc16[:, 1, :], NT, 1), ALU.mult, ALU.mult)
                D()
                tt(tmp[0:TS, 0:P].rearrange("p (b h) -> p b h", b=DEC_BATCH), over(dts[0:TS, 3, 2, :], DEC_BATCH, 1),
                   over(C("own", TS), SSD_HEADS), ALU.mult)
                D().then_inc(loga_ready.sem, 1)

                dve.wait_ge(rg_gates.sem, rg_gates.at(l, 1))
                tt(rgi[:], rgi[:], xcT[:], ALU.mult)
                D()
                tt(xcT[:], rgr[:], rgr[:], ALU.mult)
                D()
                stt(rgt[:], xcT[:], 1.0, rgt[:], ALU.add, ALU.mult)
                D().then_inc(rg_sq.sem, 1)
                dve.wait_ge(rg_root.sem, rg_root.at(l, 1))
                tt(rgi[:], rgi[:], rgt[:], ALU.mult)
                first = slice(SEQ, T, DEC_SEQ)
                tt(h0rg[:], h0rg[:], rgr[:, :, first], ALU.mult)
                D()
                tt(rgi[:, :, first], rgi[:, :, first], h0rg[:], ALU.add)
                V.memset(rgr[:, :, first], 0.0)
                D()
                for m in range(RT):
                    V.tensor_tensor_scan(xcT[:, m, :], rgr[:, m, :], rgi[:, m, :], 0.0, ALU.mult, ALU.add)
                D()
                cpy(rgl[:, :, 0:1], xcT[:, :, SEQ - 1:SEQ])
                cpy(rgl[:, :, 1:], xcT[:, :, SEQ + DEC_SEQ - 1:T:DEC_SEQ])
                D().then_inc(rgl_ready.sem, 1)
                tt(yrg[:], yrg[:], xcT[:], ALU.mult).then_inc(rg_done.sem, 1)

                dve.wait_ge(filled.sem, fills(l, ("cum",)))
                o = bank(("cum",))
                n_ = NT * SSD_HEADS
                v = o[:, 0:2 * n_].rearrange("p (k i h) -> p k i h", k=2, i=NT)
                cpy(cum[:, :, 0:2, :], v[:, :, 0:2, :])
                cpy(cum[0:TS, :, 2, :], v[0:TS, :, 2, :])
                cpy(tbh[:].rearrange("p b h -> p (b h)"), o[:, 2 * n_:2 * n_ + P]).then_inc(TD, 1)
                D()
                tt(ex[:, 2], cum[:, 1], cum[:, 0], ALU.subtract)
                D().then_inc(cum_ready.sem, 1)
                dve.wait_ge(filled.sem, fills(l, ("rgo",)))
                o = bank(("rgo",))
                dve.wait_ge(wab_in.sem, wab_in.at(l, 256))
                cpy(rgo[:], o[0:1 + DEC_BATCH, :]).then_inc(TD, 1)
                D().then_inc(rgo_ready.sem, 1)
                dve.wait_ge(cum_exp.sem, cum_exp.at(l, 1))
                dve.wait_ge(tails_out.sem, tails_out.at(l, 64))

                hv = lambda ap: ap.rearrange("p (h v) -> p h v", v=SSD_HD)

                def rstd(k, i=None):
                    D().then_inc(var_ready.sem, 1)
                    dve.wait_ge(rstd_ready.sem, rstd_ready.at(l, k))

                for i in range(NT):
                    R_ = ROWS[i]
                    HQ = 4 if i < 2 else SSD_HEADS
                    mask = C("tri" if i < 2 else "tri_s", R_, 0, R_)
                    tt(hv(xdt[0:R_, :]), hv(xs[0:R_, i, 0:D_SSD]), over(dts[0:R_, 1, i, :], SSD_HD), ALU.mult)
                    D()
                    tt(hv(xw[0:R_, :]), hv(xdt[0:R_, :]), over(ex[0:R_, 2, i, :], SSD_HD), ALU.mult)
                    D().then_inc(xw_ready.sem, 1)
                    dve.wait_ge(filled.sem, fills(l, ("cb", i)))
                    o = bank(("cb", i))
                    sm = Sm[0:R_, 0:2 * R_].rearrange("p (g t) -> p g t", g=2)
                    tt(sm, o[0:R_, 0:2 * R_].rearrange("p (g t) -> p g t", g=2), over(mask, 2, 1), ALU.mult).then_inc(TD, 1)
                    nq = SSD_HEADS // HQ
                    base_ = (0, 4, 8)[i]

                    def arg(q):
                        dve.wait_ge(filled.sem, fills(l, ("dec", i, q)))
                        o = bank(("dec", i, q))
                        for j in range(HQ):
                            h = q * HQ + j
                            last = ts(AXb[0:R_, (base_ + q) % 2, j * R_:(j + 1) * R_], o[0:R_, j * R_:(j + 1) * R_],
                                      cum[0:R_, 0, i, h:h + 1], 0.0, ALU.subtract, ALU.min)
                        last.then_inc(TD, 1)
                        dve.drain().then_inc(arg_ready.sem, 1)

                    def scores(q):
                        dve.wait_ge(exp_ready.sem, exp_ready.at(l, base_ + q + 1))
                        a_ = AXb[0:R_, (base_ + q) % 2, :]
                        if i < 2:
                            tt(Pm[:, q, :].rearrange("p (j t) -> p j t", j=4), a_.rearrange("p (j t) -> p j t", j=4),
                               over(sm[:, q // 2, :], 4, 1), ALU.mult)
                        else:
                            for g in range(2):
                                tt(Pm[0:R_, 0, g * 256:(g + 1) * 256].rearrange("p (j t) -> p j t", j=HG),
                                   a_[:, g * 256:(g + 1) * 256].rearrange("p (j t) -> p j t", j=HG),
                                   over(sm[:, g, :], HG, 1), ALU.mult)
                        D().then_inc(P_ready.sem, 1)

                    for q in range(nq):
                        arg(q)
                        if q:
                            scores(q - 1)
                    scores(nq - 1)
                    ea = lambda g: over(ex[0:R_, 0, i, g * HG:(g + 1) * HG], SSD_HD)
                    Y = lambda g: h_tm[0:R_, i, g * 512:(g + 1) * 512]
                    if i == 1:
                        for g in range(2):
                            dve.wait_ge(filled.sem, fills(l, ("yo", i, g)))
                            o = bank(("yo", i, g))
                            tt(hv(Y(g)), hv(o[:, :]), ea(g), ALU.mult).then_inc(TD, 1)
                    if i < 2:
                        for g in range(2):
                            dve.wait_ge(filled.sem, fills(l, ("cs", i, g)))
                            o = bank(("cs", i, g))
                            sg_ = S[:, g * 512:(g + 1) * 512]
                            if i == 0:
                                cpy(sg_, o[:, :]).then_inc(TD, 1)
                            else:
                                tt(hv(sg_), hv(sg_), over(ex[:, 1, i, g * HG:(g + 1) * HG], SSD_HD), ALU.mult)
                                D()
                                tt(sg_, sg_, o[:, :], ALU.add).then_inc(TD, 1)
                            dve.drain().then_inc(S_ready.sem, 1)
                    else:
                        dve.wait_ge(S_out.sem, S_out.at(l, 16))
                        for g in range(2):
                            tt(CmB[:, g], over(BCT[:, 2 + g, SEQ:T], DEC_BATCH, 1),
                               C("bmask").rearrange("p (b t) -> p b t", b=DEC_BATCH), ALU.mult)
                        D().then_inc(Cm_ready.sem, 1)
                        for b in range(DEC_BATCH):
                            ts(BmB[:, b % 2, :], xs[0:TS, 2, D_SSD:], C("own", TS, b, 1), None, ALU.mult)
                            D().then_inc(Bm_ready.sem, 1)
                            dve.wait_ge(h0_in[b % 2].sem, h0_in[b % 2].at(l, 16 * (b // 2 + 1)))
                            for g in range(2):
                                dve.wait_ge(filled.sem, fills(l, ("st", b, g)))
                                o = bank(("st", b, g))
                                sg_ = h0s[:, b % 2, g * 512:(g + 1) * 512]
                                tt(hv(sg_), hv(sg_), over(tbh[:, b, g * HG:(g + 1) * HG], SSD_HD), ALU.mult)
                                D()
                                tt(sg_, sg_, o[:, :], ALU.add).then_inc(TD, 1)
                                dve.drain().then_inc(h0_new.sem, 1)
                        for g in range(2):
                            dve.wait_ge(hold_full.sem, hold_full.at(l, g + 1))
                            tt(hv(Y(g)), hv(ps[0:TS, 6 + g, :]), ea(g), ALU.mult).then_inc(hold_free.sem, 1)
                    D()
                    for g in range(2):
                        dve.wait_ge(filled.sem, fills(l, ("yi", i, g)))
                        o = bank(("yi", i, g))
                        if i == 0:
                            cpy(Y(g), o[0:R_, :]).then_inc(TD, 1)
                        else:
                            tt(Y(g), Y(g), o[0:R_, :], ALU.add).then_inc(TD, 1)
                    tt(hv(xdt[0:R_, :]), hv(xs[0:R_, i, 0:D_SSD]), over(bc16[0:R_, 2, :], SSD_HD), ALU.mult)
                    D()
                    y_ = h_tm[0:R_, i, :]
                    tt(y_, y_, xdt[0:R_, :], ALU.add)
                    D()
                    dve.wait_ge(*takes(l, ("z", 1, i)))
                    tt(y_, y_, zb[0:R_, i, :], ALU.mult)
                    D()
                    for g in range(2):
                        V.bn_stats(stat[0:R_, 8 + 6 * g:14 + 6 * g], Y(g))
                    D()
                    for g in range(2):
                        V.bn_aggr(stat[0:R_, 32 + 2 * g:34 + 2 * g], stat[0:R_, 8 + 6 * g:14 + 6 * g])
                    D()
                    mv = stat[0:R_, 32:36].rearrange("p (g k) -> p g k", k=2)
                    tt(stat[0:R_, 0:2], mv[:, :, 0], mv[:, :, 0], ALU.mult)
                    D()
                    tt(stat[0:R_, 0:2], stat[0:R_, 0:2], mv[:, :, 1], ALU.add)
                    rstd(i + 1)
                    for g in range(2):
                        stt(Y(g), Y(g), stat[0:R_, g:g + 1], lnp[0:R_, 0, g * 512:(g + 1) * 512], ALU.mult, ALU.mult)
                    D().then_inc(y_ready.sem, 1)
                D().then_inc(ssd_done.sem, 1)

                hh = lambda ap: ap.rearrange("p (h c v) -> p h c v", c=2, v=RET_HD // 2)
                for i in range(NT):
                    R_ = ROWS[i]
                    for j in range(2):
                        dve.wait_ge(*takes(l, ("q", j, i)))
                    src, dst = hh(qkvg[0:R_, i, 0:2 * D_RET]), hh(rq[0:R_, i, :])
                    t1 = tmp[0:R_, 0:512].rearrange("p (h v) -> p h v", v=64)
                    t2 = tmp[0:R_, 512:1024].rearrange("p (h v) -> p h v", v=64)
                    cs_ = over(C("cos", R_, 64 * i, 64), 8, 1)
                    sn_ = over(C("sin", R_, 64 * i, 64), 8, 1)
                    tt(dst[:, :, 0, :], src[:, :, 0, :], cs_, ALU.mult)
                    tt(t1, src[:, :, 1, :], sn_, ALU.mult)
                    tt(dst[:, :, 1, :], src[:, :, 1, :], cs_, ALU.mult)
                    tt(t2, src[:, :, 0, :], sn_, ALU.mult)
                    D()
                    tt(dst[:, :, 0, :], dst[:, :, 0, :], t1, ALU.subtract)
                    tt(dst[:, :, 1, :], dst[:, :, 1, :], t2, ALU.add)
                    D().then_inc(rope_ready.sem, 1)
                h4 = lambda ap: ap.rearrange("p (h v) -> p h v", h=RET_HEADS)
                for b in range(2):
                    dve.wait_ge(h0_out[b].sem, h0_out[b].at(l, 16 * DEC_BATCH // 2))
                dve.wait_ge(*takes(l, ("q", 3, NT - 1)))
                for i in range(NT):
                    R_ = ROWS[i]
                    sfx = "_s" if i == 2 else ""
                    tt(h4(vw[0:R_, :]), h4(qkvg[0:R_, i, 2 * D_RET:3 * D_RET]), over(C("kdec" + sfx, R_), P), ALU.mult)
                    D().then_inc(vw_ready.sem, 1)
                    if i == 2:
                        dve.wait_ge(*takes(l, ("qk", 2, 0)))
                        for h in range(RET_HEADS):
                            tt(QmB[:, h], over(qkT[:, h, SEQ:T], DEC_BATCH, 1),
                               C("bmask").rearrange("p (b t) -> p b t", b=DEC_BATCH), ALU.mult)
                        D().then_inc(Qm_ready.sem, 1)
                    dve.wait_ge(filled.sem, fills(l, ("sc", i)))
                    o = bank(("sc", i))
                    tt(Pr[0:R_, 0:4 * R_], o[0:R_, 0:4 * R_], C("dr" + sfx, R_), ALU.mult).then_inc(TD, 1)
                    D().then_inc(Pr_ready.sem, 1)
                    if i:
                        dve.wait_ge(filled.sem, filled.at(l, PLACE["yrt", i - 1] + 1))
                    if i == 1:
                        dve.wait_ge(filled.sem, fills(l, ("ro", i)))
                        o = bank(("ro", i))
                        tt(h4(Y2[:]), h4(o[:, :]), over(C("qdec"), P), ALU.mult).then_inc(TD, 1)
                    if i < 2:
                        dve.wait_ge(filled.sem, fills(l, ("rs", i)))
                        o = bank(("rs", i))
                        if i == 0:
                            cpy(R[:], o[:, :]).then_inc(TD, 1)
                        else:
                            tt(h4(R[:]), h4(R[:]), over(C("gam"), P), ALU.mult)
                            D()
                            tt(R[:], R[:], o[:, :], ALU.add).then_inc(TD, 1)
                        dve.drain().then_inc(R_ready.sem, 1)
                    else:
                        for b in range(DEC_BATCH):
                            ts(Km[:, b % 2, :], rq[0:TS, 2, D_RET:], C("own", TS, b, 1), None, ALU.mult)
                            D().then_inc(Km_ready.sem, 1)
                            dve.wait_ge(r0_in[b % 2].sem, r0_in[b % 2].at(l, 16 * (b // 2 + 1)))
                            dve.wait_ge(filled.sem, fills(l, ("rt", b)))
                            o = bank(("rt", b))
                            r_ = r0s[:, b % 2, :]
                            tt(h4(r_), h4(r_), over(C("gam_s"), P), ALU.mult)
                            D()
                            tt(r_, r_, o[:, :], ALU.add).then_inc(TD, 1)
                            dve.drain().then_inc(r0_new.sem, 1)
                        dve.wait_ge(hold_full.sem, hold_full.at(l, 3))
                        tt(h4(Y2[0:TS, :]), h4(ps[0:TS, 6, :]), over(C("qdec_s", TS), P), ALU.mult).then_inc(hold_free.sem, 1)
                    D()
                    y_ = Y2[0:R_, :]
                    dve.wait_ge(filled.sem, fills(l, ("ri", i)))
                    o = bank(("ri", i))
                    if i == 0:
                        cpy(y_, o[0:R_, :]).then_inc(TD, 1)
                    else:
                        tt(y_, y_, o[0:R_, :], ALU.add).then_inc(TD, 1)
                    D()
                    for h in range(RET_HEADS):
                        V.bn_stats(stat[0:R_, 8 + 6 * h:14 + 6 * h], y_[:, h * P:(h + 1) * P])
                    D()
                    for h in range(RET_HEADS):
                        V.bn_aggr(stat[0:R_, 32 + 2 * h:34 + 2 * h], stat[0:R_, 8 + 6 * h:14 + 6 * h])
                    D()
                    mv = stat[0:R_, 32:40].rearrange("p (g k) -> p g k", k=2)
                    cpy(stat[0:R_, 0:RET_HEADS], mv[:, :, 1])
                    rstd(NT + i + 1)
                    for h in range(RET_HEADS):
                        ts(y_[:, h * P:(h + 1) * P], y_[:, h * P:(h + 1) * P], stat[0:R_, 32 + 2 * h:33 + 2 * h],
                           stat[0:R_, h:h + 1], ALU.subtract, ALU.mult)
                    D()
                    tt(y_, y_, lnp[0:R_, 1, 0:D_RET], ALU.mult)
                    D()
                    tt(y_, y_, qkvg[0:R_, i, 3 * D_RET:], ALU.mult)
                    D().then_inc(yr_ready.sem, 1)
                D().then_inc(ret_done.sem, 1)

                def norm(k, gain):
                    for i in range(NT):
                        for a in range(2):
                            V.bn_stats(stat[0:ROWS[i], 8 + 12 * i + 6 * a:14 + 12 * i + 6 * a],
                                       x_tm[0:ROWS[i], i, a * 512:(a + 1) * 512])
                    D()
                    for i in range(NT):
                        V.bn_aggr(stat[0:ROWS[i], 48 + 2 * i:50 + 2 * i], stat[0:ROWS[i], 8 + 12 * i:20 + 12 * i])
                    D()
                    cpy(stat[:, 0:2], stat[:, 48:52].rearrange("p (i k) -> p i k", k=2)[:, :, 1])
                    cpy(stat[0:TS, 2:3], stat[0:TS, 53:54])
                    rstd(k)
                    for i in range(NT):
                        R_ = ROWS[i]
                        ts(x_tm[0:R_, i, :], x_tm[0:R_, i, :], stat[0:R_, 48 + 2 * i:49 + 2 * i], stat[0:R_, i:i + 1],
                           ALU.subtract, ALU.mult)
                    D()
                    gain(0)
                    for i in range(NT):
                        tt(x_tm[0:ROWS[i], i, :], x_tm[0:ROWS[i], i, :], lnp[0:ROWS[i], 0, :], ALU.mult)
                    D()
                    for i in range(NT):
                        tt(x_tm[0:ROWS[i], i, :], x_tm[0:ROWS[i], i, :], lnp[0:ROWS[i], 1, :], ALU.add)

                mods(range(4, 6))
                for i in range(NT):
                    R_, w_ = ROWS[i], int(i == 2)
                    for a in range(2):
                        sl = slice(a * 512, (a + 1) * 512)
                        dve.wait_ge(filled.sem, fills(l, ("mix", i, a)))
                        o = bank(("mix", i, a))
                        tt(h_tm[0:R_, i, sl], o[0:R_, :], h_tm[0:R_, i, sl], ALU.add).then_inc(TD, 1)
                        D()
                        tt(h_tm[0:R_, i, sl], h_tm[0:R_, i, sl], gate[0:R_, w_, sl], ALU.mult)
                    D()
                    stt(x_tm[0:R_, i, :], x_tm[0:R_, i, :], ALPHA, h_tm[0:R_, i, :], ALU.mult, ALU.add)
                D()
                dve.sem_inc(gate_used.sem, 1)
                norm(2 * NT + 1, lambda _: dve.wait_ge(ln1_in.sem, ln1_in.at(l, 32)))
                D().then_inc(x1_done.sem, 1)
                dve.wait_ge(*takes(l, ("ms", 9)))
                for i in range(NT):
                    R_, w_ = ROWS[i], int(i == 2)
                    tt(h_tm[0:R_, i, :], x_tm[0:R_, i, :], sc2[0:R_, w_, :], ALU.mult)
                    D()
                    tt(h_tm[0:R_, i, :], h_tm[0:R_, i, :], sh2[0:R_, w_, :], ALU.add).then_inc(h2_ready.sem, 1)
                D()

                V.memset(rt[:, 0], 0.5)
                V.memset(dtm[:], 0.0)
                D().then_inc(score_fill.sem, 1)
                dve.wait_ge(*takes(l, ("logit",)))
                G3 = NT * N_GROUPS
                g8 = lambda k_: rt[:, k_].rearrange("p i (g e) -> p (i g) e", e=EPG)
                pref = over(C("pref"), NT, 1)
                small_ = lambda k_: rt[:, 12].rearrange("p i e -> p (i e)")[:, k_ * G3:(k_ + 1) * G3]

                def top(v, oh, s_, m_, pf):
                    V.tensor_reduce(m_, v, AX_X, ALU.max)
                    D()
                    tt(oh, v, over(m_, v.shape[2]), ALU.is_equal)
                    D()
                    tt(oh, oh, pf, ALU.mult)
                    D()
                    V.tensor_reduce(s_, oh, AX_X, ALU.max)
                    D()
                    tt(oh, oh, over(s_, v.shape[2]), ALU.is_equal)
                    D()

                tt(rt[:, 1], rt[:, 0], over(rbias[:], NT, 1), ALU.add)
                tt(rt[:, 8], pref, pref, ALU.max)
                D()
                top(g8(1), g8(5), small_(0), small_(1), g8(8))
                stt(rt[:, 6], rt[:, 5], -1e30, rt[:, 1], ALU.mult, ALU.add)
                D()
                V.tensor_reduce(small_(2), g8(6), AX_X, ALU.max)
                D()
                tt(small_(1), small_(1), small_(2), ALU.add)
                D()
                g4 = lambda k_: small_(k_).rearrange("p (i g) -> p i g", g=N_GROUPS)
                n1, n2 = stat[:, 0:NT], stat[:, 4:4 + NT]
                top(g4(1), g4(2), n1, n2, over(C("pref", P, 0, N_GROUPS), NT, 1))
                ts(small_(3), small_(2), 1e30, -1e30, ALU.mult, ALU.add)
                tt(g8(2), g8(1), over(small_(2), EPG), ALU.mult)
                D()
                tt(g8(2), g8(2), over(small_(3), EPG), ALU.add)
                D()
                top(rt[:, 2], rt[:, 3], n1, n2, pref)
                stt(rt[:, 2], rt[:, 3], -1e30, rt[:, 2], ALU.mult, ALU.add)
                D()
                top(rt[:, 2], rt[:, 4], n1, n2, pref)
                for k in range(2):
                    tt(rt[:, 5 + k], rt[:, 3 + k], rt[:, 0], ALU.mult)
                D()
                for k in range(2):
                    V.tensor_reduce(dtm[:, 1, :, k], rt[:, 5 + k], AX_X, ALU.add)
                D()
                tt(n1, dtm[:, 1, :, 0], dtm[:, 1, :, 1], ALU.add)
                D()
                V.reciprocal(n2, n1)
                D()
                tt(dtm[:, 1], dtm[:, 1], over(n2, 2), ALU.mult)
                for k in range(2):
                    tt(rt[:, 3 + k], rt[:, 3 + k], over(C("valid"), N_EXPERTS), ALU.mult)
                D()
                tt(rt[:, 7], rt[:, 3], rt[:, 4], ALU.add)
                D().then_inc(oh_ready.sem, 1)
                dve.wait_ge(filled.sem, fills(l, ("rank",)))
                o = bank(("rank",))
                cpy(rt[:, 9, 0:2, :], o[:, 0:64].rearrange("p (i e) -> p i e", i=2))
                cpy(rt[0:TS, 9, 2, :], o[0:TS, 64:96])
                cpy(nblk[:, 0, :], o[:, 96:128]).then_inc(TD, 1)
                V.memset(nblk[:, 4, :], 1.0)
                D()
                ts(npi[:], nblk[:, 0, :], float(BLK - 1), None, ALU.add)
                D()
                ts(npi[:], npi[:], BLK.bit_length() - 1, None, ALU.arith_shift_right)
                D()
                cpy(nblk[:, 1, :], npi[:])
                D()
                tt(nblk[:, 1, :], nblk[:, 1, :], C("atleast"), ALU.max)
                D()
                V.tensor_tensor_scan(nblk[:, 2, :], nblk[:, 4, :], nblk[:, 1, :], 0.0, ALU.mult, ALU.add)
                D()
                tt(nblk[:, 3, :], nblk[:, 2, :], nblk[:, 1, :], ALU.subtract)
                D()
                ts(nblk[:, 3, :], nblk[:, 3, :], float(BLK), None, ALU.mult)
                D()
                tt(bew[:], over(C("iota", 1, 0, NBMAX), N_EXPERTS), over(nblk[0:1, 2, :], NBMAX, 1), ALU.is_ge)
                for i in range(NT):
                    R_ = ROWS[i]
                    tt(rt[0:R_, 10, i, :], rt[0:R_, 9, i, :], nblk[0:R_, 3, :], ALU.add)
                    D()
                    for k in range(2):
                        tt(rt[0:R_, 5 + k, i, :], rt[0:R_, 3 + k, i, :], rt[0:R_, 10, i, :], ALU.mult)
                    D()
                    for k in range(2):
                        V.tensor_reduce(dtm[0:R_, 0, i, k:k + 1], rt[0:R_, 5 + k, i, :], AX_X, ALU.add)
                D().then_inc(dtm_ready.sem, 1)
                V.tensor_reduce(rt[0:1, 11, :, :].rearrange("p i e -> p (i e)")[:, 0:NBMAX], bew[:], AX_X, ALU.add)
                ts(npi[0:1, 0:1], nblk[0:1, 2, N_EXPERTS - 1:N_EXPERTS], 1.0, None, ALU.add)
                D()
                ts(bei[:, 0:NBMAX], rt[0:1, 11, :, :].rearrange("p i e -> p (i e)")[:, 0:NBMAX], float(N_EXPERTS - 1), None, ALU.min)
                ts(npi[0:1, 0:1], npi[0:1, 0:1], 1, None, ALU.arith_shift_right)
                D().then_inc(plan_ready.sem, 1)
                for v in range(4):
                    dve.wait_ge(filled.sem, fills(l, ("bc", v)))
                    o = bank(("bc", v))
                    cpy(dbc[:, v, :], o[:, 0:T]).then_inc(TD, 1)
                V.memset(acc[:], 0.0)
                V.memset(accs[:], 0.0)
                cpy(scol[:], C("slot"))
                D()

                done = dve.snap(before)
                pairs = dve.value_load(npi[0:1, 0:1], min_val=2, max_val=NBMAX // 2)

                def select():
                    dv = dtm[:, 0].rearrange("p i k -> p (i k)")
                    st_ = selt[:].rearrange("p i k s -> p (i k) s")
                    tt(st_, over(C("iota"), 2 * NT, 1), over(dv, 2 * BLK), ALU.is_equal)
                    D()
                    tt(sel[:, 0], selt[:, :, 0, :], selt[:, :, 1, :], ALU.add)
                    ts(dv, dv, float(-2 * BLK), None, ALU.add)
                    D().then_inc(sel_ready, 1)

                select()
                with dve.Fori(0, pairs) as q:
                    d = dve.snap(done + q)
                    dve.wait_ge(g_full, d + l + 1)
                    select()
                    for b in range(2):
                        stt(selw[:, b, :], dbc[:, 0, :], scol[:, b:b + 1], dbc[:, 2, :], ALU.is_equal, ALU.mult)
                        stt(selt2[:, b, :], dbc[:, 1, :], scol[:, b:b + 1], dbc[:, 3, :], ALU.is_equal, ALU.mult)
                    D()
                    tt(selw[:], selw[:], selt2[:], ALU.add)
                    ts(scol[:], scol[:], float(2 * BLK), None, ALU.add)
                    D().then_inc(selw_ready, 1)
                    for b in range(2):
                        dve.wait_ge(sg_ready, 2 * d + 1 + b)
                        tt(hb[:, b, :], sg[:, b, :], ps[:, b, P:2 * P], ALU.mult)
                        D().then_inc(hb_ready, 1)
                    for b in range(2):
                        dve.wait_ge(d_full, 4 * d + 2 + 2 * b)
                        cpy(ys[:, b, 512:1024], ps[:, 3, :])
                        D().then_inc(ysd, 1)
                    for j in range(5):
                        dve.wait_ge(s_full, 5 * d + 1 + j)
                        if j < 4:
                            i, a = divmod(j, 2)
                            v = acc[:, i, a * 512:(a + 1) * 512]
                            tt(v, v, ps[:, 4 + j % 2, :], ALU.add)
                        else:
                            tt(accs[:], accs[:], ps[:, 4, 0:256], ALU.add)
                        D().then_inc(acc_taken, 1)
                dve.reg_add(before, before, pairs)
                after = dve.snap(before)
                dve.wait_ge(g_taken, after + l + 2)

                for c in range(4):
                    cpy(h_tm[0:TS, 2, c * 256:(c + 1) * 256], accs[32 * c:32 * c + TS, :])
                for i in range(2):
                    tt(acc[:, i, :], acc[:, i, :], gate[:, 0, :], ALU.mult)
                D()
                tt(h_tm[0:TS, 2, :], h_tm[0:TS, 2, :], gate[0:TS, 1, :], ALU.mult)
                D()
                for i in range(NT):
                    R_ = ROWS[i]
                    m_ = acc[:, i, :] if i < 2 else h_tm[0:TS, 2, :]
                    stt(x_tm[0:R_, i, :], x_tm[0:R_, i, :], ALPHA, m_, ALU.mult, ALU.add)
                D()
                norm(2 * NT + 2, lambda _: dve.wait_ge(ln2_in.sem, ln2_in.at(l, 32)))
                D().then_inc(begun, 1)


_IN = ["x_prompt", "x_sample", "c_prompt", "c_sample", "state_ssd", "state_ssd_conv", "state_rglru",
       "state_rglru_conv", "state_ret", "w_ada", "b_ada", "w_in", "ssd_conv_w", "ssd_conv_b", "ssd_dt_bias",
       "ssd_a_log", "ssd_d", "ssd_norm_w", "rg_conv_w", "rg_conv_b", "rg_wa", "rg_ba", "rg_wx", "rg_bx",
       "rg_lambda", "ret_gn_w", "w_out", "ln1_g", "ln1_b", "router_w", "router_bias", "exp_w_gate", "exp_w_up",
       "exp_w_down", "ln2_g", "ln2_b"]
_OUT = [("y_prompt", (1, SEQ, D_MODEL)), ("y_sample", (DEC_BATCH, DEC_SEQ, D_MODEL))]
for _s, _b in (("p", 1), ("s", DEC_BATCH)):
    _OUT += [(f"ssd_{_s}", (DEPTH, _b, SSD_HEADS, SSD_STATE, SSD_HD)),
             (f"ssd_conv_{_s}", (DEPTH, _b, HALO, SSD_CONV_DIM)),
             (f"rglru_{_s}", (DEPTH, _b, D_RG)),
             (f"rglru_conv_{_s}", (DEPTH, _b, HALO, D_RG)),
             (f"ret_{_s}", (DEPTH, _b, RET_HEADS, RET_HD, RET_HD))]


def kernel(**inputs):
    import numpy as np
    import concourse.bacc as bacc
    from concourse.bass_utils import run_bass_kernel_spmd

    nc = bacc.Bacc("TRN2", target_bir_lowering=False, num_devices=1)
    arrays, A, O = {}, {}, {}
    given = [(name, np.ascontiguousarray(inputs[name])) for name in _IN]
    given.append(("con", const_table()[1]))
    for name, a in given:
        arrays[f"in_{name}"] = a
        A[name] = nc.dram_tensor(f"in_{name}", a.shape, mybir.dt.from_np(a.dtype), kind="ExternalInput").ap()
    for name, shape in _OUT:
        O[name] = nc.dram_tensor(f"out_{name}", shape, F32, kind="ExternalOutput").ap()
    trunk(nc, A, O)
    r = run_bass_kernel_spmd(nc, [arrays], core_ids=[0])
    return tuple(r.results[0][f"out_{name}"] for name, _ in _OUT)
```

```python
from contextlib import ExitStack

import concourse.bass as bass
from concourse import mybir

F32 = mybir.dt.float32
I32 = mybir.dt.int32
ALU = mybir.AluOpType
ACT = mybir.ActivationFunctionType
AX_X = mybir.AxisListType.X

P = 128
D_MODEL = 1024
KT = D_MODEL // P
SEQ = 256
DEPTH = 2
DEC_BATCH = 8
DEC_SEQ = 4
PAST_LEN = 2048
TS = DEC_BATCH * DEC_SEQ
T = SEQ + TS
NT = 3
ROWS = (P, P, TS)
T0 = (0, P, 2 * P)
D_SSD = 1024
SSD_HEADS, SSD_HD, SSD_GROUPS, SSD_STATE = 16, 64, 2, 128
HG = SSD_HEADS // SSD_GROUPS
SSD_CONV_DIM = D_SSD + 2 * SSD_GROUPS * SSD_STATE
CONV_WIDTH = 4
HALO = CONV_WIDTH - 1
D_RG = 512
RG_BLOCK_W = 64
RG_C = 8.0
D_RET = 512
RET_HEADS, RET_HD = 4, 128
N_EXPERTS, N_GROUPS = 32, 4
EPG = N_EXPERTS // N_GROUPS
D_EXPERT = 512
ALPHA = float((2 * DEPTH) ** 0.25)
EPS = 1e-5
CH = 512
BLK = 32

XT = SSD_CONV_DIM // P
RT = D_RG // P
RAWW = HALO + SEQ + DEC_BATCH * (HALO + DEC_SEQ)
CVW = RAWW - HALO
SS = HALO + SEQ

C_Z, C_XBC = 0, D_SSD
C_DT = C_XBC + SSD_CONV_DIM
C_RGX = C_DT + SSD_HEADS
C_RGG = C_RGX + D_RG
C_Q = C_RGG + D_RG
IN_DIM = C_Q + 4 * D_RET

V_XW, V_XB = 0, CONV_WIDTH * XT
V_RW = V_XB + XT
V_RB = V_RW + CONV_WIDTH * RT
V_BA, V_BX, V_LAM = V_RB + RT, V_RB + 2 * RT, V_RB + 3 * RT
V_N = V_RB + 4 * RT

STREAM = ([("ada", n) for n in range(4)] + [("in", C_RGX), ("in", C_RGG)]
          + [("in", C_XBC + CH * n) for n in range(3)] + [("in", C_Z), ("in", C_Z + CH)]
          + [("in", C_Q + CH * n) for n in range(4)] + [("out", 0), ("out", 1)]
          + [("ada", n) for n in range(4, 12)] + [("out", 2), ("out", 3)])
NBMAX = 2 * ((2 * T // BLK + N_EXPERTS + 2 + 1) // 2)
NS = 3
PER_SLOT = len(STREAM) // NS
assert PER_SLOT * NS == len(STREAM)


PARTS = ("s", 0, 1, 2)

FILLER = {-1: ((2, "s"), (2, 0)), 1: ((2, 1),), 2: ((2, 2),), 3: ((3, "s"), (3, 0)), 5: ((3, 1),), 6: ((3, 2),)}


def ssd_steps(i):
    out = [(("cb", i), "D")]
    out += [(("dec", i, q), "D") for q in range(4 if i < 2 else 1)]
    if i == 1:
        out += [(("yo", i, g), "D") for g in range(2)]
    if i < 2:
        out += [(("cs", i, g), "D") for g in range(2)]
    else:
        out += [(("q", c, j), "A") for c, j in FILLER[-1]]
        for b in range(DEC_BATCH):
            out += [(("st", b, g), "D") for g in range(2)]
            out += [(("q", c, j), "A") for c, j in FILLER.get(b, ())]
    if i == 0:
        out += [(("z", 1, j), "A") for j in (1, 2)]
    return out + [(("yi", i, g), "D") for g in range(2)]


MIX_ORDER = ((0, 0), (0, 1), (1, 0), (2, 0), (2, 1), (1, 1))
NORM_ORDER = (0, 2, 1)


def ret_steps(i):
    out = [(("sc", i), "D")]
    if i:
        out.append((("yrt", i - 1), "A"))
    if i == 0:
        out.append((("mix_a", 1, 1), "A"))
    if i == 1:
        out.append((("ro", i), "D"))
    if i < 2:
        out.append((("rs", i), "D"))
    else:
        for b in range(DEC_BATCH):
            out.append((("rt", b), "D"))
            if 1 <= b <= 6:
                out.append((("ada", 5 + b), "A"))
    if i == 0:
        out.append((("mix_a", 2, 0), "A"))
    out.append((("ri", i), "D"))
    if i == 0:
        out.append((("mix_a", 2, 1), "A"))
    if i == 1:
        out += [(("ada", 4), "A"), (("ada", 5), "A")]
    return out


def bank_plan():
    out = [(("ada", c), "A") for c in range(4)]
    out += [(("vec",), "D"), (("halo",), "D")]
    out += [(("mt", 0), "D"), (("xt", 0), "A"), (("xt", 1), "A")]
    out += [(("mt", 1), "D"), (("xt", 2), "A"), (("xt", 3), "A"), (("xts",), "D")]
    out += [(("rgx", m), "A") for m in range(RT)] + [(("rgg", m), "A") for m in range(RT)]
    for m in range(XT + 1):
        if m < XT:
            out.append((("fm", m), "A"))
        if m >= 3:
            out.append((("xst", m - 3), "A"))
    out += [(("tail", q), "A") for q in range((XT + RT) // 4)]
    out += [(("dt",), "D"), (("h0rg",), "D")]
    out += [(("rga", m), "A") for m in range(RT)] + [(("rgi", m), "A") for m in range(RT)]
    out += [(("z", 0, j), "A") for j in PARTS]
    out += [(("cum",), "D"), (("z", 1, "s"), "A"), (("z", 1, 0), "A"), (("rgo",), "D")]
    for i in range(NT):
        out += ssd_steps(i)
        if i < 2:
            out += [(("q", i, j), "A") for j in PARTS]
    out += [(("yt", i, a), "A") for i in range(2) for a in range(2)]
    out += [(("mix_a", 0, a), "A") for a in range(2)]
    out += [(("yt", 2, a), "A") for a in range(2)] + [(("mix_a", 1, 0), "A")]
    out += [(("qk", i, a), "A") for i in range(NT) for a in range(2)]
    for i in range(NT):
        out += ret_steps(i)
    out += [((w, c), "D") for c in (4, 5) for w in ("mp", "ms")]
    out += [(("mix", *b), "D") for b in MIX_ORDER[:2]] + [(("yrt", 2), "A")]
    out += [(("mix_s", a), "A") for a in range(2)] + [(("mix", *b), "D") for b in MIX_ORDER[2:5]]
    out += [((w, c), "A") for c in range(6, 10) for w in ("mp", "ms")]
    out += [(("mix", *MIX_ORDER[5]), "D")]
    out += [((w, c), "A") for c in (10, 11) for w in ("mp", "ms")]
    out += [(("h2t", i, a), "A") for i in NORM_ORDER for a in range(2)]
    out += [(("logit",), "A"), (("rank",), "D")] + [(("bc", v), "D") for v in range(4)]
    return out


ROT = 6
PLAN = bank_plan()
PLACE = {key: n for n, (key, _) in enumerate(PLAN)}


def const_table():
    import numpy as np
    t = np.arange(P)
    s4 = np.arange(TS)
    cols, parts, at = {}, [], [0]

    def put(name, a):
        a = np.asarray(a, np.float64)
        full = np.zeros((P, a.shape[1]), np.float32)
        full[:a.shape[0]] = a
        cols[name] = (at[0], at[0] + a.shape[1])
        at[0] += a.shape[1]
        parts.append(full)

    put("ident", np.eye(P))
    put("tri", t[:, None] <= t[None, :])
    put("strict", t[:, None] < t[None, :])
    put("ones", np.ones((P, 1)))
    same = (s4[:, None] // DEC_SEQ) == (s4[None, :] // DEC_SEQ)
    put("tri_s", same & (s4[:, None] <= s4[None, :]))
    put("blk_s", same)
    put("own", (s4[:, None] // DEC_SEQ) == np.arange(DEC_BATCH)[None, :])
    put("bmask", np.tile(((s4[None, :] // DEC_SEQ) == np.arange(DEC_BATCH)[:, None]).reshape(1, -1), (P, 1)))
    half = RET_HD // 2
    inv = (10000.0 ** (-np.arange(half, dtype=np.float32) / half)).astype(np.float32)
    pos = np.zeros((P, NT), np.float32)
    pos[:, 0], pos[:, 1] = t, t + P
    pos[:TS, 2] = PAST_LEN + s4 % DEC_SEQ
    ang = (pos[:, :, None] * inv[None, None, :]).astype(np.float32).astype(np.float64)
    put("cos", np.cos(ang).reshape(P, -1))
    put("sin", np.sin(ang).reshape(P, -1))
    lg = np.log1p(-np.exp2(-5.0 - np.arange(RET_HEADS)))
    scale = RET_HD ** -0.5
    d = (t[None, :] - t[:, None])[:, None, :]
    put("dr", np.where(d >= 0, np.exp(d * lg[None, :, None]), 0).reshape(P, -1) * scale)
    d = (s4[None, :] - s4[:, None])[:, None, :]
    put("dr_s", np.where((d >= 0) & same[:, None, :], np.exp(d * lg[None, :, None]), 0).reshape(TS, -1) * scale)
    put("qdec", np.exp((t[:, None] + 1) * lg))
    put("qdec_s", np.exp((s4[:, None] % DEC_SEQ + 1) * lg))
    put("kdec", np.exp((P - 1 - t[:, None]) * lg) * scale)
    put("kdec_s", np.exp((DEC_SEQ - 1 - s4[:, None] % DEC_SEQ) * lg) * scale)
    put("gam", np.tile(np.exp(P * lg), (P, 1)))
    put("gam_s", np.tile(np.exp(DEC_SEQ * lg), (P, 1)))
    put("iota", np.tile(np.arange(2 * BLK), (P, 1)))
    put("slot", np.stack([t % BLK, t % BLK + BLK], 1))
    put("pref", np.tile(N_EXPERTS - np.arange(N_EXPERTS), (P, 1)))
    put("atleast", np.tile(np.arange(N_EXPERTS) < 2, (P, 1)))
    put("gs", (t[:, None] % 32) == 1 + s4[None, :] // DEC_SEQ)
    valid = np.ones((P, NT))
    valid[TS:, 2] = 0
    put("valid", valid)
    put("fold", (t[:, None] % 32) == np.arange(32)[None, :])
    put("eps", np.full((P, 1), EPS))
    return cols, np.concatenate(parts, 1)


class Signal:

    def __init__(self, sem, per_layer):
        self.sem, self.per_layer = sem, per_layer

    def at(self, l, k):
        return l * self.per_layer + k

    def stand(self, eng):
        eng.sem_inc(self.sem, 1)


def trunk(nc, A, O):
    cc, _ = const_table()
    ctx = ExitStack()
    with ctx:
        base = (nc.sbuf_base + 63) // 64 * 64
        top = [base]

        def size(shape):
            n = 4
            for s in shape[1:]:
                n *= s
            return (n + 31) // 32 * 32

        def fixed(name, shape, dt=F32):
            t = nc.alloc_sbuf_tensor_at(name, shape, dt, offset=top[0])
            top[0] += size(shape)
            return t

        class Region:
            def __init__(self, start):
                self.at = start

            def new(self, name, shape, dt=F32):
                t = nc.alloc_sbuf_tensor_at(name, shape, dt, offset=self.at)
                self.at += size(shape)
                return t

        SLOT = KT * CH
        ring = fixed("ring", [P, 3, SLOT])
        x_tm = fixed("x_tm", [P, NT, D_MODEL])
        h_tm = fixed("h_tm", [P, NT, D_MODEL])
        ht0 = top[0]
        hT = fixed("hT", [P, KT, T])
        lnp = fixed("lnp", [P, 2, D_MODEL])
        pb = top[0]
        spare = fixed("spare", [P, 4, CH])
        pbr = Region(pb)

        xTb = pbr.new("xTb", [P, KT, 2 * BLK])
        hTb = pbr.new("hTb", [P, 2, P])
        hb = pbr.new("hb", [P, 2, P])
        sg = pbr.new("sg", [P, 2, P])
        con = fixed("con", [P, max(b for _, b in cc.values())])
        modT = fixed("modT", [P, 2, KT, 1 + DEC_BATCH])
        cT = fixed("cT", [P, KT, 32])
        vecT = fixed("vecT", [P, V_N])
        halo = fixed("halo", [P, XT + RT, DEC_BATCH * HALO])
        h0rg = fixed("h0rg", [P, RT, DEC_BATCH])
        cl = fixed("cl", [P, 4, RT])
        bc16 = fixed("bc16", [P, 3, SSD_HEADS])
        dts = fixed("dts", [P, 4, NT, SSD_HEADS])
        cum = fixed("cum", [P, 2, NT, SSD_HEADS])
        ex = fixed("ex", [P, 3, NT, SSD_HEADS])
        tbh = fixed("tbh", [P, DEC_BATCH, SSD_HEADS])
        stat = fixed("stat", [P, 64])
        rgl = fixed("rgl", [P, RT, 1 + DEC_BATCH])
        rw = fixed("rw", [P, KT, N_EXPERTS])
        rbias = fixed("rbias", [P, N_EXPERTS])
        wdt = fixed("wdt", [P, KT, SSD_HEADS])
        M = top[0]
        m1 = Region(M)
        R1 = m1.at
        qkvg = m1.new("qkvg", [P, NT, 4 * D_RET])
        r1 = Region(R1)
        xcT = r1.new("xcT", [P, RT, T])
        rgr = r1.new("rgr", [P, RT, T])
        rgi = r1.new("rgi", [P, RT, T])
        rgt = r1.new("rgt", [P, RT, T])
        tailT = r1.new("tailT", [P, XT + RT, HALO * (1 + DEC_BATCH)])
        yrg = m1.new("yrg", [P, RT, T])
        BCT = m1.new("BCT", [P, 4, T])
        yreT = nc.alloc_sbuf_tensor_at("yreT", [P, RET_HEADS, T], F32, offset=m1.at - 4 * T * 4)
        c0 = m1.at
        raw = m1.new("raw", [P, 4, RAWW])
        xsT = m1.new("xsT", [P, 4, T])
        cv = m1.new("cv", [P, 2, CVW])
        convend = m1.at
        r2 = Region(c0)
        Pm = r2.new("Pm", [P, 4, 4 * P])
        Sm = r2.new("Sm", [P, 2 * P])
        assert r2.at <= convend
        r2 = Region(c0)
        Pr = r2.new("Pr", [P, 4 * P])
        Y2 = r2.new("Y2", [P, D_RET])
        Km = r2.new("Km", [TS, 2, D_RET])
        assert r2.at <= convend <= M + 3 * SLOT * 4
        g0 = M + 3 * SLOT * 4
        m1 = Region(g0)
        h0s = [m1.new(f"h0s{n}", [P, SSD_HEADS * SSD_HD]) for n in range(2)]
        h0s.append(nc.alloc_sbuf_tensor_at("h0s2", [P, SSD_HEADS * SSD_HD], F32, offset=pb + 4096))
        S = m1.new("S", [P, SSD_HEADS * SSD_HD])
        xdt = m1.new("xdt", [P, D_SSD])
        xw = m1.new("xw", [P, D_SSD])
        zb = m1.new("zb", [P, NT, D_SSD])
        xs = m1.new("xs", [P, NT, D_SSD + 2 * SSD_STATE])
        mix_end = m1.at
        r2 = Region(g0)
        wab = r2.new("wab", [P, 2, RT, P])
        rgo = nc.alloc_sbuf_tensor_at("rgo", [1 + DEC_BATCH, D_RG], F32, offset=g0 + 4096)
        tails = nc.alloc_sbuf_tensor_at("tails", [HALO * (1 + DEC_BATCH), (XT + RT) * P], F32, offset=g0 + 8192)
        R = nc.alloc_sbuf_tensor_at("R", [P, D_RET], F32, offset=g0 + 8192)
        QmB = nc.alloc_sbuf_tensor_at("QmB", [P, RET_HEADS, DEC_BATCH, TS], F32, offset=g0)
        CmB = nc.alloc_sbuf_tensor_at("CmB", [P, SSD_GROUPS, DEC_BATCH, TS], F32, offset=g0 + 8192)
        r2 = Region(g0 + 3 * 4096)
        r0s = r2.new("r0s", [P, 3, D_RET])
        vw = r2.new("vw", [P, D_RET])
        qkT = Region(g0 + 5 * 4096).new("qkT", [P, 2 * RET_HEADS, T])
        rq = Region(g0 + 5 * 4096 + 3 * 4096).new("rq", [P, NT, 2 * D_RET])
        r2 = Region(g0 + 5 * 4096 + 3 * 4096)
        grow = h_tm[0:DEC_BATCH, 2, 0:D_RG]
        hrow = nc.alloc_sbuf_tensor_at("hrow", [DEC_BATCH * HALO, (XT + RT) * P], F32, offset=ht0)
        vrow = nc.alloc_sbuf_tensor_at("vrow", [V_N, P], F32, offset=ht0 + (XT + RT) * P * 4)
        assert (XT + RT + 1) * P <= KT * T
        bias = nc.alloc_sbuf_tensor_at("bias", [12, CH], F32, offset=pb + 3 * CH * 4)
        ada_at = lambda c: qkvg[:, 0, c * CH:(c + 1) * CH] if c < 4 else spare[:, c % 2, :] if c < 6 else qkvg[:, (c - 6) // 2, (c % 2) * CH:(c % 2 + 1) * CH]
        assert pbr.at <= pb + 3 * CH * 4
        AXb = nc.alloc_sbuf_tensor_at("AXb", [P, 2, 4 * P], F32, offset=pb)
        tmp = nc.alloc_sbuf_tensor_at("tmp", [P, D_MODEL], F32, offset=pb + 4096)
        BmB = Region(c0 + 9216).new("BmB", [TS, 2, 2 * SSD_STATE])
        assert c0 + 9216 + 2048 <= convend
        ring1 = nc.alloc_sbuf_tensor_at("ring1", [P, 3, SLOT], F32, offset=M)
        m2 = Region(g0)
        gate = m2.new("gate", [P, 2, D_MODEL])
        sh2 = m2.new("sh2", [P, 2, D_MODEL])
        ys = nc.alloc_sbuf_tensor_at("ys", [P, 2, D_MODEL], F32, offset=g0 + 8192)
        sc2 = m2.new("sc2", [P, 2, D_MODEL])
        rt = nc.alloc_sbuf_tensor_at("rt", [P, 13, NT, N_EXPERTS], F32, offset=g0 + 2 * 8192)
        acc = m2.new("acc", [P, 2, D_MODEL])
        accs = m2.new("accs", [P, D_MODEL // 4])
        dbc = m2.new("dbc", [P, 4, T])
        selw = m2.new("selw", [P, 2, T])
        selt2 = m2.new("selt2", [P, 2, T])
        sel = m2.new("sel", [P, 2, NT, 2 * BLK])
        selt = m2.new("selt", [P, NT, 2, 2 * BLK])
        dtm = m2.new("dtm", [P, 2, NT, 2])
        scol = m2.new("scol", [P, 2])
        nblk = m2.new("nblk", [P, 5, N_EXPERTS])
        bew = nc.alloc_sbuf_tensor_at("bew", [1, NBMAX, N_EXPERTS], F32, offset=g0 + 3 * 8192)
        bei = m2.new("bei", [1, 64], I32)
        npi = m2.new("npi", [P, N_EXPERTS], I32)
        assert max(mix_end, m2.at) <= nc.sbuf_usable_end

        ps = ctx.enter_context(nc.psum_tensor("ps", [P, 8, 512], F32))

        def C(name, rows=P, lo=0, n=None):
            a, b = cc[name]
            if b - a == 1 and n is not None:
                return con[0:rows, a:b].to_broadcast([rows, n])
            return con[0:rows, a + lo:(b if n is None else a + lo + n)]


        def sem(name):
            return ctx.enter_context(nc.semaphore(name))

        def sig(name, per_layer):
            return Signal(sem(name), per_layer)

        idle = {e: sig(f"stood_{e}", 0) for e in ("pe", "act", "sp", "pool")}

        filled = sig("filled", len(PLAN))
        takers = {"A": sig("taken_act", sum(e == "A" for _, e in PLAN)),
                  "D": sig("taken_dve", sum(e == "D" for _, e in PLAN))}

        def nth_taken(key):
            n = PLACE[key]
            return sum(e == PLAN[n][1] for _, e in PLAN[:n + 1])

        def takes(l, key):
            t = takers[PLAN[PLACE[key]][1]]
            return t.sem, t.at(l, nth_taken(key))

        def emptied(l, key):
            n = PLACE[key]
            return takes(l, PLAN[n - ROT][0]) if n >= ROT else (settled, l + 1)

        def fills(l, key):
            return filled.at(l, PLACE[key] + 1)

        def bank(key):
            return ps[:, PLACE[key] % ROT, :]

        TA, TD, FL = takers["A"].sem, takers["D"].sem, filled.sem

        OF_BUF = [len(range(s, DEC_BATCH, 3)) for s in range(3)]
        con_in = sem("con_in")
        c_silu, c_turned, c_ready = sem("c_silu"), sem("c_turned"), sem("c_ready")
        settled = sem("settled")
        begun = sem("layer_begun")
        st_full = [sig(f"stream_full{s}", 16 * PER_SLOT) for s in range(NS)]
        st_used = [sig(f"stream_used{s}", PER_SLOT) for s in range(NS)]
        bias_in = sig("bias_in", 32)
        small_room = sem("small_room")
        late_in = sig("late_in", 16 * 3)
        modT_ready = sig("modT_ready", 1)
        gate_used = sig("gate_used", 1)
        small_in = sig("small_in", 16 * 13)
        wab_zero = sig("wab_zero", 1)
        wab_in = sig("wab_in", 16 * 16)
        cv_ready = sig("conv_ready", XT + RT)
        cv_out = sig("conv_out", XT + RT)
        tails_out = sig("tails_out", 16 * 4)
        rgo_ready = sig("rg_state_ready", 1)
        rgo_out = sig("rg_state_out", 32)
        rgl_ready = sig("rg_last_ready", 1)
        rg_gates = sig("rg_gates", 1)
        rg_sq = sig("rg_sq", 1)
        rg_root = sig("rg_root", 1)
        rg_done = sig("rg_done", 1)
        lam_abs = sig("lam_abs", 1)
        lam_ln = sig("lam_ln", 1)
        lam_c = sig("lam_c", 1)
        dt_abs = sig("dt_abs", 1)
        dt_ln = sig("dt_ln", 1)
        loga_ready = sig("loga_ready", 1)
        cum_ready = sig("cum_ready", 1)
        cum_exp = sig("cum_exp", 1)
        xw_ready = sig("xw_ready", NT)
        arg_ready = sig("decay_arg_ready", 9)
        exp_ready = sig("decay_ready", 9)
        P_ready = sig("scores_ready", 9)
        S_ready = sig("state_ready", 4)
        S_out = sig("state_out", 16)
        Cm_ready = sig("Cm_ready", 1)
        Bm_ready = sig("Bm_ready", DEC_BATCH)
        h0_in = [sig(f"h0_in{s}", 16 * OF_BUF[s]) for s in range(3)]
        h0_new = sig("h0_new", 2 * DEC_BATCH)
        h0_out = [sig(f"h0_out{s}", 16 * OF_BUF[s]) for s in range(3)]
        hold_full = sig("hold_full", 3)
        hold_free = sig("hold_free", 3)
        var_ready = sig("var_ready", 3 * NT + 1)
        rstd_ready = sig("rstd_ready", 3 * NT + 1)
        y_ready = sig("y_ready", NT)
        ssd_done = sig("ssd_done", 1)
        rope_ready = sig("rope_ready", NT)
        Pr_ready = sig("ret_scores_ready", NT)
        vw_ready = sig("vw_ready", NT)
        R_ready = sig("ret_state_ready", 2)
        R_out = sig("ret_state_out", 16)
        Qm_ready = sig("Qm_ready", 1)
        Km_ready = sig("Km_ready", DEC_BATCH)
        r0_in = [sig(f"r0_in{s}", 16 * OF_BUF[s]) for s in range(3)]
        r0_new = sig("r0_new", DEC_BATCH)
        r0_out = [sig(f"r0_out{s}", 16 * OF_BUF[s]) for s in range(3)]
        yr_ready = sig("yr_ready", NT)
        ret_done = sig("ret_done", 1)
        mix_over = sig("mix_over", 1)
        ln1_in = sig("ln1_in", 32)
        x1_done = sig("x1_done", 1)
        ln2_in = sig("ln2_in", 32)
        h2_ready = sig("h2_ready", NT)
        score_fill = sig("score_fill", 1)
        oh_ready = sig("oh_ready", 1)
        dtm_ready = sig("dtm_ready", 1)
        plan_ready = sig("plan_ready", 1)
        stores_out = sig("stores_out", 1)
        y_out = sem("y_out")
        gu_full = [sem(f"gate_up_full{b}") for b in range(2)]
        dn_full = [sem(f"down_full{b}") for b in range(2)]
        gu_used = [sem(f"gate_up_used{b}") for b in range(2)]
        dn_used = [sem(f"down_used{b}") for b in range(2)]
        sel_ready, g_full, g_taken = sem("sel_ready"), sem("gather_full"), sem("gather_taken")
        u_full, sg_ready, hb_ready = sem("up_full"), sem("silu_ready"), sem("hidden_ready")
        t_full, ht_ready = sem("turned_full"), sem("turned_taken")
        d_full, ysa, ysd = sem("down_out_full"), sem("ys_act"), sem("ys_dve")
        selw_ready, s_full, acc_taken = sem("selw_ready"), sem("spread_full"), sem("acc_taken")

        block = ctx.enter_context(nc.Block())
        w_dt = lambda l: A["w_in"][l][:, C_DT:C_DT + SSD_HEADS].rearrange("(k p) n -> p k n", p=P)

        @block.sync
        def _(sp):
            for b in range(2):
                sp.sem_inc(gu_used[b], 1)
                sp.sem_inc(dn_used[b], 1)
            sp.dma_start(h_tm[0:1, 0, :], A["c_prompt"]).then_inc(con_in, 16)
            sp.dma_start(h_tm[1:1 + DEC_BATCH, 0, :], A["c_sample"]).then_inc(con_in, 16)
            sp.dma_start(con[:], A["con"]).then_inc(con_in, 16)
            sp.dma_start(x_tm[:, 0:2, :], A["x_prompt"][0].rearrange("(i p) d -> p i d", p=P)).then_inc(con_in, 16)
            sp.dma_start(x_tm[0:TS, 2, :], A["x_sample"].rearrange("b s d -> (b s) d")).then_inc(con_in, 16)
            sp.dma_start(rw[:], A["router_w"].rearrange("(k p) e -> p k e", p=P)).then_inc(con_in, 16)
            sp.dma_start(rbias[:], A["router_bias"].unsqueeze(0).to_broadcast([P, N_EXPERTS])).then_inc(con_in, 16)
            before = sp.alloc_register("pairs_before")
            sp.reg_mov(before, 0)
            with sp.Fori(0, DEPTH) as l:
                seen = sp.snap(before)
                for n, (kind, at) in enumerate(STREAM):
                    s, r = n % NS, n // NS
                    if r:
                        sp.wait_ge(st_used[s].sem, st_used[s].at(l, r))
                    else:
                        sp.wait_ge((gu_used if n < 2 else dn_used)[0], seen + 1)
                    idle["sp"].stand(sp)
                    if kind == "ada":
                        src = A["w_ada"][l][:, at * CH:(at + 1) * CH].rearrange("(k p) n -> p k n", p=P)
                    elif kind == "in":
                        src = A["w_in"][l][:, at:at + CH].rearrange("(k p) n -> p k n", p=P)
                    else:
                        src = A["w_out"][l][at * 4 * P:(at + 1) * 4 * P, :].rearrange("(k p) n -> p k n", p=P)
                    dst = ring[:, s, :].rearrange("p (k n) -> p k n", n=D_MODEL if kind == "out" else CH)
                    sp.dma_start(dst, src).then_inc(st_full[s].sem, 16)

                def experts(b, e):
                    dst = (ring, ring1)[b]
                    for j, name in enumerate(("exp_w_gate", "exp_w_up")):
                        sp.dma_start(dst[:, j, :].rearrange("p (k n) -> p k n", n=D_EXPERT),
                                     A[name][l, e].rearrange("(k p) n -> p k n", p=P)).then_inc(gu_full[b], 16)

                def experts_down(b, e):
                    dst = (ring, ring1)[b]
                    sp.dma_start(dst[:, 2, :].rearrange("p (k n) -> p k n", n=D_MODEL),
                                 A["exp_w_down"][l, e].rearrange("(k p) n -> p k n", p=P)).then_inc(dn_full[b], 16)

                for s in range(NS):
                    sp.wait_ge(st_used[s].sem, st_used[s].at(l, PER_SLOT))
                    idle["sp"].stand(sp)
                experts(0, 0)
                experts_down(0, 0)
                sp.wait_ge(mix_over.sem, mix_over.at(l, 1))
                idle["sp"].stand(sp)
                experts(1, 1)
                experts_down(1, 1)
                sp.wait_ge(plan_ready.sem, plan_ready.at(l, 1))
                idle["sp"].stand(sp)
                pairs = sp.value_load(npi[0:1, 0:1], min_val=2, max_val=NBMAX // 2)
                done = sp.snap(before)
                with sp.Fori(1, pairs) as q:
                    for b in range(2):
                        e = sp.value_load(bei[0:1, bass.ds(2 * q + b, 1)], min_val=0, max_val=N_EXPERTS - 1)
                        sp.wait_ge(gu_used[b], done + q + 1)
                        experts(b, e)
                        sp.wait_ge(dn_used[b], done + q + 1)
                        experts_down(b, e)
                sp.reg_add(before, before, pairs)
            sp.wait_ge(begun, DEPTH + 1)
            sp.dma_start(O["y_prompt"][0].rearrange("(i p) d -> p i d", p=P), x_tm[:, 0:2, :]).then_inc(y_out, 16)
            sp.dma_start(O["y_sample"].rearrange("b s d -> (b s) d"), x_tm[0:TS, 2, :]).then_inc(y_out, 16)
            sp.wait_ge(y_out, 32)

        @block.gpsimd
        def _(pool):
            with pool.Fori(0, DEPTH) as l:
                pool.wait_ge(small_room, l + 1)
                idle["pool"].stand(pool)

                def small(dst, src):
                    pool.dma_start(dst, src).then_inc(small_in.sem, 16)

                def late(dst, src):
                    pool.dma_start(dst, src).then_inc(late_in.sem, 16)

                def rowsof(name, lead=None):
                    v = A[name][l]
                    return v.rearrange("j (m p) -> (j m) p", p=P) if lead else v.rearrange("(m p) -> m p", p=P)

                pool.dma_start(bias[:], A["b_ada"][l].rearrange("(c n) -> c n", n=CH)).then_inc(bias_in.sem, 16)
                small(vrow[V_XW:V_XB, :], rowsof("ssd_conv_w", True))
                small(vrow[V_XB:V_RW, :], rowsof("ssd_conv_b"))
                small(vrow[V_RW:V_RB, :], rowsof("rg_conv_w", True))
                small(vrow[V_RB:V_BA, :], rowsof("rg_conv_b"))
                small(vrow[V_BA:V_BX, :], rowsof("rg_ba"))
                small(vrow[V_BX:V_LAM, :], rowsof("rg_bx"))
                small(vrow[V_LAM:V_N, :], rowsof("rg_lambda"))
                small(hrow[:, 0:SSD_CONV_DIM], A["state_ssd_conv"][l].rearrange("b j c -> (b j) c"))
                small(hrow[:, SSD_CONV_DIM:], A["state_rglru_conv"][l].rearrange("b j c -> (b j) c"))
                for n, name in enumerate(("ssd_dt_bias", "ssd_a_log", "ssd_d")):
                    small(bc16[:, n, :], A[name][l].unsqueeze(0).to_broadcast([P, SSD_HEADS]))
                small(wdt[:], w_dt(l))

                pool.wait_ge(begun, l + 1)
                idle["pool"].stand(pool)
                late(grow, A["state_rglru"][l])
                late(lnp[:, 0, :], A["ssd_norm_w"][l].unsqueeze(0).to_broadcast([P, D_SSD]))
                late(lnp[:, 1, 0:D_RET], A["ret_gn_w"][l].unsqueeze(0).to_broadcast([P, D_RET]))
                nc.gpsimd.memset(wab[:], 0.0).then_inc(wab_zero.sem, 1)
                pool.wait_ge(wab_zero.sem, wab_zero.at(l, 1))
                idle["pool"].stand(pool)
                for w, name in enumerate(("rg_wa", "rg_wx")):
                    v = A[name][l].rearrange("(m u) j k -> u j m k", u=2)
                    for u in range(2):
                        lo = u * RG_BLOCK_W
                        for m in range(RT):
                            pool.dma_start(wab[lo:lo + RG_BLOCK_W, w, m, lo:lo + RG_BLOCK_W], v[u, :, m, :]
                                           ).then_inc(wab_in.sem, 16)
                pool.wait_ge(*takes(l, ("tail", 3)))
                idle["pool"].stand(pool)
                for name, c0_, c1_ in (("ssd_conv", 0, SSD_CONV_DIM), ("rglru_conv", SSD_CONV_DIM, (XT + RT) * P)):
                    pool.dma_start(O[name + "_p"][l, 0], tails[0:HALO, c0_:c1_]).then_inc(tails_out.sem, 16)
                    pool.dma_start(O[name + "_s"][l].rearrange("b j c -> (b j) c"), tails[HALO:, c0_:c1_]
                                   ).then_inc(tails_out.sem, 16)
                pool.wait_ge(rgo_ready.sem, rgo_ready.at(l, 1))
                idle["pool"].stand(pool)
                pool.dma_start(O["rglru_p"][l], rgo[0:1, :]).then_inc(rgo_out.sem, 16)
                pool.dma_start(O["rglru_s"][l], rgo[1:, :]).then_inc(rgo_out.sem, 16)
                pool.wait_ge(rgo_out.sem, rgo_out.at(l, 32))
                idle["pool"].stand(pool)

                def load_h0(b):
                    pool.dma_start(h0s[b % 3][:, :].rearrange("n (h v) -> n h v", v=SSD_HD),
                                   A["state_ssd"][l, b].rearrange("h n v -> n h v")).then_inc(h0_in[b % 3].sem, 16)

                for b in range(3):
                    load_h0(b)
                pool.wait_ge(S_ready.sem, S_ready.at(l, 4))
                idle["pool"].stand(pool)
                pool.dma_start(O["ssd_p"][l, 0].rearrange("h n v -> n h v"),
                               S[:].rearrange("n (h v) -> n h v", v=SSD_HD)).then_inc(S_out.sem, 16)
                for b in range(DEC_BATCH):
                    pool.wait_ge(h0_new.sem, h0_new.at(l, 2 * b + 2))
                    idle["pool"].stand(pool)
                    pool.dma_start(O["ssd_s"][l, b].rearrange("h n v -> n h v"),
                                   h0s[b % 3][:, :].rearrange("n (h v) -> n h v", v=SSD_HD)
                                   ).then_inc(h0_out[b % 3].sem, 16)
                    if b and b + 2 < DEC_BATCH:
                        c = b - 1
                        pool.wait_ge(h0_out[c % 3].sem, h0_out[c % 3].at(l, 16 * (c // 3 + 1)))
                        idle["pool"].stand(pool)
                        load_h0(c + 3)
                pool.wait_ge(ssd_done.sem, ssd_done.at(l, 1))
                idle["pool"].stand(pool)

                def load_r0(b):
                    pool.dma_start(r0s[:, b % 3, :].rearrange("n (h v) -> n h v", v=RET_HD),
                                   A["state_ret"][l, b].rearrange("h n v -> n h v")).then_inc(r0_in[b % 3].sem, 16)

                for b in range(3):
                    load_r0(b)
                pool.wait_ge(rope_ready.sem, rope_ready.at(l, NT))
                idle["pool"].stand(pool)
                pool.dma_start(bias[:], A["b_ada"][l].rearrange("(c n) -> c n", n=CH)).then_inc(bias_in.sem, 16)
                pool.wait_ge(R_ready.sem, R_ready.at(l, 2))
                idle["pool"].stand(pool)
                pool.dma_start(O["ret_p"][l, 0].rearrange("h n v -> n h v"),
                               R[:].rearrange("n (h v) -> n h v", v=RET_HD)).then_inc(R_out.sem, 16)
                for b in range(DEC_BATCH):
                    pool.wait_ge(r0_new.sem, r0_new.at(l, b + 1))
                    idle["pool"].stand(pool)
                    pool.dma_start(O["ret_s"][l, b].rearrange("h n v -> n h v"),
                                   r0s[:, b % 3, :].rearrange("n (h v) -> n h v", v=RET_HD)
                                   ).then_inc(r0_out[b % 3].sem, 16)
                    if b and b + 2 < DEC_BATCH:
                        c = b - 1
                        pool.wait_ge(r0_out[c % 3].sem, r0_out[c % 3].at(l, 16 * (c // 3 + 1)))
                        idle["pool"].stand(pool)
                        load_r0(c + 3)
                pool.wait_ge(tails_out.sem, tails_out.at(l, 64))
                idle["pool"].stand(pool)
                pool.wait_ge(S_out.sem, S_out.at(l, 16))
                idle["pool"].stand(pool)
                pool.wait_ge(R_out.sem, R_out.at(l, 16))
                idle["pool"].stand(pool)
                for b in range(3):
                    pool.wait_ge(h0_out[b].sem, h0_out[b].at(l, 16 * OF_BUF[b]))
                    idle["pool"].stand(pool)
                    pool.wait_ge(r0_out[b].sem, r0_out[b].at(l, 16 * OF_BUF[b]))
                    idle["pool"].stand(pool)
                pool.sem_inc(stores_out.sem, 1)
                pool.wait_ge(ret_done.sem, ret_done.at(l, 1))
                idle["pool"].stand(pool)
                pool.dma_start(lnp[:, 0, :], A["ln1_g"][l].unsqueeze(0).to_broadcast([P, D_MODEL])).then_inc(ln1_in.sem, 16)
                pool.dma_start(lnp[:, 1, :], A["ln1_b"][l].unsqueeze(0).to_broadcast([P, D_MODEL])).then_inc(ln1_in.sem, 16)
                pool.wait_ge(x1_done.sem, x1_done.at(l, 1))
                idle["pool"].stand(pool)
                pool.dma_start(lnp[:, 0, :], A["ln2_g"][l].unsqueeze(0).to_broadcast([P, D_MODEL])).then_inc(ln2_in.sem, 16)
                pool.dma_start(lnp[:, 1, :], A["ln2_b"][l].unsqueeze(0).to_broadcast([P, D_MODEL])).then_inc(ln2_in.sem, 16)

        @block.tensor
        def _(pe):
            mm, tr = nc.tensor.matmul, nc.tensor.transpose
            pe.wait_ge(con_in, 16 * 7)
            pe.wait_ge(c_silu, 1)
            for k in range(KT):
                last = tr(ps[:, 6, 9 * k:9 * k + 9], h_tm[0:9, 0, k * P:(k + 1) * P], C("ident", 9, 0, 9))
            last.then_inc(c_turned, 1)
            pe.wait_ge(c_ready, 1)
            before = pe.alloc_register("pairs_before")
            pe.reg_mov(before, 0)
            with pe.Fori(0, DEPTH) as l:
                pe.wait_ge(settled, l + 1)

                def stream(n):
                    pe.wait_ge(st_full[n % NS].sem, st_full[n % NS].at(l, 16 * (n // NS + 1)))
                    return ring[:, n % NS, :].rearrange("p (k n) -> p k n",
                                                        n=D_MODEL if STREAM[n][0] == "out" else CH)

                def ada(c, n):
                    w = stream(n)
                    pe.wait_ge(*emptied(l, ("ada", c)))
                    o = bank(("ada", c))
                    for r in range(2):
                        for g in range(4):
                            k = 4 * r + g
                            mm(o[32 * g:32 * g + 32, :], cT[:, k, :], w[:, k, :], start=(r == 0), stop=(r == 1 and g > 0),
                                      skip_group_check=True)
                    mm(o[0:32, :], C("ident", 12, c, 1).to_broadcast([12, 32]), bias[:], start=False, stop=True,
                       skip_group_check=True).then_inc(FL, 1)

                def spread(c):
                    pe.wait_ge(*takes(l, ("ada", c)))
                    idle["pe"].stand(pe)
                    pe.wait_ge(*emptied(l, ("mp", c)))
                    o = bank(("mp", c))
                    mm(o[:, :], C("fold", P, 0, 1).to_broadcast([P, P]), ada_at(c), start=True, stop=True).then_inc(FL, 1)
                    pe.wait_ge(*emptied(l, ("ms", c)))
                    o = bank(("ms", c))
                    mm(o[0:TS, :], C("gs"), ada_at(c), start=True, stop=True).then_inc(FL, 1)

                def free_slot(n):
                    pe.drain().then_inc(st_used[n % NS].sem, 1)

                def columns(j):
                    pe.wait_ge(*takes(l, ("ada", 2 * j + 1)))
                    idle["pe"].stand(pe)
                    pe.wait_ge(*emptied(l, ("mt", j)))
                    idle["pe"].stand(pe)
                    o = bank(("mt", j))
                    W_ = 1 + DEC_BATCH
                    for k in range(KT):
                        last = mm(o[:, k * W_:(k + 1) * W_], ada_at(2 * j + k // 4)[:, k % 4 * P:(k % 4 + 1) * P], C("fold", P, 0, W_),
                                  start=True, stop=True)
                    last.then_inc(FL, 1)

                def turn_x(q):
                    pe.wait_ge(*emptied(l, ("xt", q)))
                    o = bank(("xt", q))
                    for k in range(2):
                        for i in range(2):
                            last = tr(o[:, k * SEQ + i * P:k * SEQ + (i + 1) * P], x_tm[:, i, (2 * q + k) * P:(2 * q + k + 1) * P],
                                      C("ident"))
                    last.then_inc(FL, 1)

                pe.wait_ge(bias_in.sem, bias_in.at(l, 16))
                for c in range(4):
                    ada(c, c)
                    free_slot(c)
                pe.wait_ge(small_in.sem, small_in.at(l, 16 * 13))
                pe.wait_ge(*emptied(l, ("vec",)))
                o = bank(("vec",))
                tr(o[:, 0:V_N], vrow[:], C("ident", V_N, 0, V_N)).then_inc(FL, 1)
                pe.wait_ge(*emptied(l, ("halo",)))
                idle["pe"].stand(pe)
                o = bank(("halo",))
                n = DEC_BATCH * HALO
                for m in range(XT + RT):
                    last = tr(o[:, m * n:(m + 1) * n], hrow[:, m * P:(m + 1) * P], C("ident", n, 0, n))
                last.then_inc(FL, 1)
                columns(0)
                pe.wait_ge(begun, l + 1)
                turn_x(0)
                turn_x(1)
                columns(1)
                turn_x(2)
                turn_x(3)
                pe.wait_ge(*emptied(l, ("xts",)))
                idle["pe"].stand(pe)
                o = bank(("xts",))
                for k in range(KT):
                    last = tr(o[:, k * TS:(k + 1) * TS], x_tm[0:TS, 2, k * P:(k + 1) * P], C("ident", TS, 0, TS))
                last.then_inc(FL, 1)
                n = 4

                def turn_rows(src, key, i):
                    R_ = ROWS[i]
                    for a in range(2):
                        pe.wait_ge(*emptied(l, (key, i, a)))
                        if i == 2:
                            idle["pe"].stand(pe)
                        o = bank((key, i, a))
                        for k in range(4):
                            last = tr(o[:, k * R_:(k + 1) * R_], src[0:R_, i, (4 * a + k) * P:(4 * a + k + 1) * P],
                                      C("ident", R_, 0, R_))
                        last.then_inc(FL, 1)

                pe.wait_ge(*takes(l, ("xt", 3)))
                idle["pe"].stand(pe)
                pe.wait_ge(*takes(l, ("xts",)))
                idle["pe"].stand(pe)

                def features(w, m, key):
                    pe.wait_ge(*emptied(l, key))
                    o = bank(key)
                    for k in range(KT):
                        last = mm(o[:, 0:T], w[:, k, m * P:(m + 1) * P], hT[:, k, :], start=(k == 0), stop=(k == KT - 1))
                    last.then_inc(FL, 1)

                def quarters(o, y, w):
                    for r in range(2):
                        for g in range(4):
                            last = mm(o[32 * g:32 * g + 32, :], y(4 * r + g), w(4 * r + g), start=(r == 0), stop=(r == 1),
                                      skip_group_check=True)
                    return last

                def tokens(w, key, c, i):
                    if i == 2:
                        pe.wait_ge(*takes(l, (key, c, "s")))
                        idle["pe"].stand(pe)
                    pe.wait_ge(*emptied(l, (key, c, i)))
                    o = bank((key, c, i))
                    if i == "s":
                        last = quarters(o, lambda k: hT[:, k, SEQ:T], lambda k: w[:, k, :])
                    elif i == 2:
                        last = mm(o[0:TS, :], C("fold"), h_tm[:, 2, c % 2 * CH:(c % 2 + 1) * CH], start=True, stop=True)
                    else:
                        for k in range(KT):
                            last = mm(o[:, :], hT[:, k, T0[i]:T0[i] + P], w[:, k, :], start=(k == 0), stop=(k == KT - 1))
                    last.then_inc(FL, 1)

                for key in ("rgx", "rgg"):
                    w = stream(n)
                    for m in range(RT):
                        features(w, m, (key, m))
                    free_slot(n)
                    n += 1
                for m in range(XT + 1):
                    if m < XT:
                        if m % 4 == 0:
                            w = stream(n)
                        features(w, m % 4, ("fm", m))
                        if m % 4 == 3:
                            free_slot(n)
                            n += 1
                    if m >= 3:
                        u = m - 3
                        pe.wait_ge(cv_out.sem, cv_out.at(l, RT + u + 1))
                        pe.wait_ge(*emptied(l, ("xst", u)))
                        o = bank(("xst", u))
                        src = xsT[:, u % 4, :] if u < 8 else BCT[:, u - 8, :]
                        for i in range(NT):
                            last = tr(o[0:ROWS[i], i * P:(i + 1) * P], src[:, T0[i]:T0[i] + ROWS[i]], C("ident"))
                        last.then_inc(FL, 1)
                pe.wait_ge(cv_ready.sem, cv_ready.at(l, XT + RT))
                for q in range((XT + RT) // 4):
                    pe.wait_ge(*emptied(l, ("tail", q)))
                    o = bank(("tail", q))
                    for m in range(4):
                        last = tr(o[0:HALO * (1 + DEC_BATCH), m * P:(m + 1) * P], tailT[:, 4 * q + m, :], C("ident"))
                    last.then_inc(FL, 1)
                pe.wait_ge(*emptied(l, ("dt",)))
                o = bank(("dt",))
                for i in range(NT):
                    for k in range(KT):
                        last = mm(o[0:ROWS[i], i * SSD_HEADS:(i + 1) * SSD_HEADS], hT[:, k, T0[i]:T0[i] + ROWS[i]],
                                  wdt[:, k, :], start=(k == 0), stop=(k == KT - 1))
                last.then_inc(FL, 1)
                pe.wait_ge(late_in.sem, late_in.at(l, 16 * 3))
                idle["pe"].stand(pe)
                pe.wait_ge(*emptied(l, ("h0rg",)))
                idle["pe"].stand(pe)
                o = bank(("h0rg",))
                for m in range(RT):
                    last = tr(o[:, m * DEC_BATCH:(m + 1) * DEC_BATCH], grow[:, m * P:(m + 1) * P],
                              C("ident", DEC_BATCH, 0, DEC_BATCH))
                last.then_inc(FL, 1)

                pe.wait_ge(wab_in.sem, wab_in.at(l, 16 * 16))
                for key, w in (("rga", 0), ("rgi", 1)):
                    for m in range(RT):
                        pe.wait_ge(cv_out.sem, cv_out.at(l, m + 1))
                        pe.wait_ge(*emptied(l, (key, m)))
                        o = bank((key, m))
                        mm(o[:, 0:T], wab[:, w, m, :], xcT[:, m, :], start=True, stop=True).then_inc(FL, 1)
                w = stream(n)
                for j in PARTS:
                    tokens(w, "z", 0, j)
                free_slot(n)
                n += 1

                pe.wait_ge(loga_ready.sem, loga_ready.at(l, 1))
                pe.wait_ge(*emptied(l, ("cum",)))
                o = bank(("cum",))
                for i in range(NT):
                    R_ = ROWS[i]
                    for kind, name in enumerate(("tri", "ones") if i < 2 else ("tri_s", "blk_s")):
                        at = (kind * NT + i) * SSD_HEADS
                        mm(o[0:R_, at:at + SSD_HEADS], C(name, R_, 0, R_), dts[0:R_, 3, i, :], start=True, stop=True)
                at = 2 * NT * SSD_HEADS
                mm(o[:, at:at + DEC_BATCH * SSD_HEADS], C("ones", TS, 0, P), tmp[0:TS, 0:DEC_BATCH * SSD_HEADS],
                   start=True, stop=True).then_inc(FL, 1)
                w_z1 = stream(n)
                tokens(w_z1, "z", 1, "s")
                tokens(w_z1, "z", 1, 0)
                pe.wait_ge(rgl_ready.sem, rgl_ready.at(l, 1))
                pe.wait_ge(*emptied(l, ("rgo",)))
                o = bank(("rgo",))
                for m in range(RT):
                    last = tr(o[0:1 + DEC_BATCH, m * P:(m + 1) * P], rgl[:, m, :], C("ident"))
                last.then_inc(FL, 1)

                def ssd(i, n0):
                    R_, t0 = ROWS[i], T0[i]
                    tri = "tri" if i < 2 else "tri_s"
                    HQ = 4 if i < 2 else SSD_HEADS
                    pe.wait_ge(*emptied(l, ("cb", i)))
                    if i == 2:
                        idle["pe"].stand(pe)
                    o = bank(("cb", i))
                    for g in range(SSD_GROUPS):
                        last = mm(o[0:R_, g * R_:(g + 1) * R_], BCT[:, g, t0:t0 + R_], BCT[:, 2 + g, t0:t0 + R_],
                                  start=True, stop=True)
                    last.then_inc(FL, 1)
                    for q in range(SSD_HEADS // HQ):
                        pe.wait_ge(*emptied(l, ("dec", i, q)))
                        if i == 2:
                            idle["pe"].stand(pe)
                        o = bank(("dec", i, q))
                        for j in range(HQ):
                            h = q * HQ + j
                            last = mm(o[0:R_, j * R_:(j + 1) * R_], dts[0:R_, 3, i, h:h + 1].to_broadcast([R_, R_]),
                                      C(tri, R_, 0, R_), start=True, stop=True)
                        last.then_inc(FL, 1)
                    if i == 1:
                        pe.wait_ge(S_ready.sem, S_ready.at(l, 2))
                        for g in range(2):
                            pe.wait_ge(*emptied(l, ("yo", i, g)))
                            o = bank(("yo", i, g))
                            mm(o[:, :], BCT[:, 2 + g, t0:t0 + R_], S[:, g * 512:(g + 1) * 512], start=True, stop=True
                               ).then_inc(FL, 1)
                    if i == 2:
                        for c, j in FILLER[-1]:
                            tokens(stream(n0 + c - 2), "q", c, j)
                    pe.wait_ge(xw_ready.sem, xw_ready.at(l, i + 1))
                    if i < 2:
                        for g in range(2):
                            pe.wait_ge(*emptied(l, ("cs", i, g)))
                            o = bank(("cs", i, g))
                            mm(o[:, :], xs[:, i, D_SSD + g * P:D_SSD + (g + 1) * P], xw[:, g * 512:(g + 1) * 512],
                               start=True, stop=True).then_inc(FL, 1)
                    else:
                        pe.wait_ge(Cm_ready.sem, Cm_ready.at(l, 1))
                        for b in range(DEC_BATCH):
                            pe.wait_ge(h0_in[b % 3].sem, h0_in[b % 3].at(l, 16 * (b // 3 + 1)))
                            for g in range(2):
                                last = mm(ps[0:TS, 6 + g, :], CmB[:, g, b, :], h0s[b % 3][:, g * 512:(g + 1) * 512],
                                          start=(b == 0), stop=(b == DEC_BATCH - 1), skip_group_check=True)
                                if b == DEC_BATCH - 1:
                                    last.then_inc(hold_full.sem, 1)
                            pe.wait_ge(Bm_ready.sem, Bm_ready.at(l, b + 1))
                            for g in range(2):
                                pe.wait_ge(*emptied(l, ("st", b, g)))
                                o = bank(("st", b, g))
                                mm(o[:, :], BmB[:, b % 2, g * P:(g + 1) * P], xw[0:TS, g * 512:(g + 1) * 512],
                                   start=True, stop=True).then_inc(FL, 1)
                            for c, j in FILLER.get(b, ()):
                                tokens(stream(n0 + c - 2), "q", c, j)
                                if j == NT - 1:
                                    free_slot(n0 + c - 2)
                    if i == 0:
                        for j in (1, 2):
                            tokens(w_z1, "z", 1, j)
                        free_slot(n0)
                    pe.wait_ge(P_ready.sem, P_ready.at(l, (4, 8, 9)[i]))
                    for g in range(2):
                        pe.wait_ge(*emptied(l, ("yi", i, g)))
                        if i == 2:
                            idle["pe"].stand(pe)
                        o = bank(("yi", i, g))
                        for j in range(HG):
                            h = g * HG + j
                            p_ = (Pm[0:R_, h // 4, (h % 4) * P:(h % 4) * P + P] if i < 2
                                  else Pm[0:R_, 0, h * TS:(h + 1) * TS])
                            last = mm(o[0:R_, j * SSD_HD:(j + 1) * SSD_HD], p_, xdt[0:R_, h * SSD_HD:(h + 1) * SSD_HD],
                                      start=True, stop=True)
                        last.then_inc(FL, 1)

                ssd(0, n)
                n += 1
                for i in range(2):
                    if i:
                        ssd(i, n)
                    w = stream(n)
                    for j in PARTS:
                        tokens(w, "q", i, j)
                    free_slot(n)
                    n += 1
                ssd(2, n)
                n += 2
                n_out, n_ada = n, n + 2

                def mix_a(i, a):
                    w = [stream(n_out), stream(n_out + 1)]
                    if a == 0:
                        pe.wait_ge(*takes(l, ("yt", i, 1)))
                        idle["pe"].stand(pe)
                    pe.wait_ge(*emptied(l, ("mix_a", i, a)))
                    o = bank(("mix_a", i, a))
                    if i == 2:
                        last = quarters(o, lambda k: hT[:, k, SEQ:T], lambda k: w[k // 4][:, k % 4, a * 512:(a + 1) * 512])
                    else:
                        for k in range(KT):
                            last = mm(o[:, :], hT[:, k, T0[i]:T0[i] + P], w[k // 4][:, k % 4, a * 512:(a + 1) * 512],
                                      start=(k == 0), stop=(k == KT - 1))
                    last.then_inc(FL, 1)

                def ada_here(c):
                    ada(c, n_ada + c - 4)
                    free_slot(n_ada + c - 4)

                for i in range(2):
                    pe.wait_ge(y_ready.sem, y_ready.at(l, i + 1))
                    turn_rows(h_tm, "yt", i)
                for a in range(2):
                    mix_a(0, a)
                pe.wait_ge(y_ready.sem, y_ready.at(l, 3))
                turn_rows(h_tm, "yt", 2)
                mix_a(1, 0)
                for i in range(NT):
                    pe.wait_ge(rope_ready.sem, rope_ready.at(l, i + 1))
                    turn_rows(rq, "qk", i)

                def turn_ret(i):
                    R_ = ROWS[i]
                    pe.wait_ge(yr_ready.sem, yr_ready.at(l, i + 1))
                    pe.wait_ge(*emptied(l, ("yrt", i)))
                    if i == 2:
                        idle["pe"].stand(pe)
                    o = bank(("yrt", i))
                    for h in range(RET_HEADS):
                        last = tr(o[:, h * R_:(h + 1) * R_], Y2[0:R_, h * P:(h + 1) * P], C("ident", R_, 0, R_))
                    last.then_inc(FL, 1)

                def ret(i):
                    R_, t0 = ROWS[i], T0[i]
                    pe.wait_ge(*emptied(l, ("sc", i)))
                    if i == 2:
                        idle["pe"].stand(pe)
                    o = bank(("sc", i))
                    for h in range(RET_HEADS):
                        last = mm(o[0:R_, h * R_:(h + 1) * R_], qkT[:, RET_HEADS + h, t0:t0 + R_], qkT[:, h, t0:t0 + R_],
                                  start=True, stop=True)
                    last.then_inc(FL, 1)
                    if i:
                        turn_ret(i - 1)
                    if i == 0:
                        mix_a(1, 1)
                    if i == 1:
                        pe.wait_ge(R_ready.sem, R_ready.at(l, 1))
                        pe.wait_ge(*emptied(l, ("ro", i)))
                        o = bank(("ro", i))
                        for h in range(RET_HEADS):
                            last = mm(o[:, h * P:(h + 1) * P], qkT[:, h, t0:t0 + R_], R[:, h * P:(h + 1) * P],
                                      start=True, stop=True)
                        last.then_inc(FL, 1)
                    pe.wait_ge(vw_ready.sem, vw_ready.at(l, i + 1))
                    if i < 2:
                        pe.wait_ge(*emptied(l, ("rs", i)))
                        o = bank(("rs", i))
                        for h in range(RET_HEADS):
                            last = mm(o[:, h * P:(h + 1) * P], rq[:, i, D_RET + h * P:D_RET + (h + 1) * P],
                                      vw[:, h * P:(h + 1) * P], start=True, stop=True)
                        last.then_inc(FL, 1)
                    else:
                        pe.wait_ge(Qm_ready.sem, Qm_ready.at(l, 1))
                        for b in range(DEC_BATCH):
                            pe.wait_ge(r0_in[b % 3].sem, r0_in[b % 3].at(l, 16 * (b // 3 + 1)))
                            for h in range(RET_HEADS):
                                last = mm(ps[0:TS, 6, h * P:(h + 1) * P], QmB[:, h, b, :], r0s[:, b % 3, h * P:(h + 1) * P],
                                          start=(b == 0 and h == 0), stop=(b == DEC_BATCH - 1), skip_group_check=True)
                            if b == DEC_BATCH - 1:
                                last.then_inc(hold_full.sem, 1)
                            pe.wait_ge(Km_ready.sem, Km_ready.at(l, b + 1))
                            pe.wait_ge(*emptied(l, ("rt", b)))
                            o = bank(("rt", b))
                            for h in range(RET_HEADS):
                                last = mm(o[:, h * P:(h + 1) * P], Km[:, b % 2, h * P:(h + 1) * P],
                                          vw[0:TS, h * P:(h + 1) * P], start=True, stop=True)
                            last.then_inc(FL, 1)
                            if 1 <= b <= 6:
                                ada_here(5 + b)
                    if i == 0:
                        mix_a(2, 0)
                    pe.wait_ge(Pr_ready.sem, Pr_ready.at(l, i + 1))
                    pe.wait_ge(*emptied(l, ("ri", i)))
                    if i == 2:
                        idle["pe"].stand(pe)
                    o = bank(("ri", i))
                    for h in range(RET_HEADS):
                        last = mm(o[0:R_, h * P:(h + 1) * P], Pr[0:R_, h * R_:(h + 1) * R_],
                                  qkvg[0:R_, i, 2 * D_RET + h * P:2 * D_RET + (h + 1) * P], start=True, stop=True)
                    last.then_inc(FL, 1)
                    if i == 0:
                        mix_a(2, 1)
                        free_slot(n_out)
                        free_slot(n_out + 1)
                    if i == 1:
                        pe.wait_ge(bias_in.sem, bias_in.at(l, 32))
                        ada_here(4)
                        ada_here(5)

                pe.wait_ge(hold_free.sem, hold_free.at(l, 2))
                pe.wait_ge(*takes(l, ("qk", 2, 1)))
                idle["pe"].stand(pe)
                for i in range(NT):
                    ret(i)
                for c in (4, 5):
                    spread(c)

                pe.wait_ge(*takes(l, ("yrt", 1)))
                idle["pe"].stand(pe)
                n = n_ada + 8
                w = [stream(n), stream(n + 1)]
                y = lambda k, i: (yrg, yreT)[k // 4][:, k % 4, T0[i]:T0[i] + ROWS[i]]

                def mix(i, a):
                    if i == 2:
                        pe.wait_ge(*takes(l, ("mix_s", a)))
                        idle["pe"].stand(pe)
                    pe.wait_ge(*emptied(l, ("mix", i, a)))
                    o = bank(("mix", i, a))
                    if i == 2:
                        mm(o[0:TS, :], C("fold"), h_tm[:, 2, a * 512:(a + 1) * 512], start=True, stop=False)
                        last = mm(o[0:TS, :], C("fold"), spare[:, a, :], start=False, stop=True)
                    else:
                        for k in range(8):
                            last = mm(o[:, :], y(k, i), w[k // 4][:, k % 4, a * 512:(a + 1) * 512],
                                      start=(k == 0), stop=(k == 7))
                    last.then_inc(FL, 1)

                for i, a in MIX_ORDER[:2]:
                    mix(i, a)
                turn_ret(2)
                pe.wait_ge(*takes(l, ("yrt", 2)))
                idle["pe"].stand(pe)
                for a in range(2):
                    pe.wait_ge(*emptied(l, ("mix_s", a)))
                    quarters(bank(("mix_s", a)), lambda k: y(k, 2), lambda k: w[k // 4][:, k % 4, a * 512:(a + 1) * 512]
                             ).then_inc(FL, 1)
                for i, a in MIX_ORDER[2:5]:
                    mix(i, a)
                for c in range(6, 10):
                    spread(c)
                mix(*MIX_ORDER[5])
                free_slot(n)
                free_slot(n + 1)
                n += 2
                for c in (10, 11):
                    spread(c)
                pe.drain().then_inc(mix_over.sem, 1)
                assert n == len(STREAM)

                for n_, i in enumerate(NORM_ORDER):
                    pe.wait_ge(h2_ready.sem, h2_ready.at(l, n_ + 1))
                    turn_rows(h_tm, "h2t", i)
                    if n_ == 0:
                        continue
                    if n_ == 1:
                        pe.wait_ge(*emptied(l, ("logit",)))
                        idle["pe"].stand(pe)
                    pe.wait_ge(*takes(l, ("h2t", i, 1)))
                    idle["pe"].stand(pe)
                    o = bank(("logit",))
                    for j in (NORM_ORDER[:2], NORM_ORDER[2:])[n_ - 1]:
                        for k in range(KT):
                            last = mm(o[0:ROWS[j], j * N_EXPERTS:(j + 1) * N_EXPERTS], hT[:, k, T0[j]:T0[j] + ROWS[j]],
                                      rw[:, k, :], start=(k == 0), stop=(k == KT - 1))
                last.then_inc(FL, 1)
                pe.wait_ge(oh_ready.sem, oh_ready.at(l, 1))
                pe.wait_ge(*emptied(l, ("rank",)))
                o = bank(("rank",))
                for i in range(NT + 1):
                    R_ = ROWS[i] if i < NT else P
                    upto = list(range(min(i, NT - 1) + 1))
                    for j in upto:
                        K_ = ROWS[j]
                        st = C("strict" if j == i else "ones", K_, 0, R_)
                        last = mm(o[0:R_, i * N_EXPERTS:(i + 1) * N_EXPERTS], st, rt[0:K_, 7, j, :],
                                  start=(j == 0), stop=(j == upto[-1]))
                last.then_inc(FL, 1)

                def gather(q, count):
                    pe.wait_ge(sel_ready, count)
                    for k in range(KT):
                        for i in range(NT):
                            last = mm(ps[:, 6, k * 2 * BLK:(k + 1) * 2 * BLK], h_tm[0:ROWS[i], i, k * P:(k + 1) * P],
                                      sel[0:ROWS[i], 0, i, :], start=(i == 0), stop=(i == NT - 1))
                    last.then_inc(g_full, 1)

                pe.wait_ge(hold_free.sem, hold_free.at(l, 3))
                idle["pe"].stand(pe)
                done = pe.snap(before)
                gather(0, done + l + 1)
                pe.wait_ge(dtm_ready.sem, dtm_ready.at(l, 1))
                for v in range(4):
                    pe.wait_ge(*emptied(l, ("bc", v)))
                    o = bank(("bc", v))
                    for i in range(NT):
                        R_ = ROWS[i]
                        last = mm(o[:, T0[i]:T0[i] + R_], dtm[0:R_, v // 2, i, v % 2:v % 2 + 1].to_broadcast([R_, P]),
                                  C("ident", R_, 0, R_), start=True, stop=True)
                    last.then_inc(FL, 1)

                pe.wait_ge(*takes(l, ("bc", 3)))
                idle["pe"].stand(pe)
                pairs = pe.value_load(npi[0:1, 0:1], min_val=2, max_val=NBMAX // 2)

                with pe.Fori(0, pairs) as q:
                    d = pe.snap(done + q)
                    pe.wait_ge(g_taken, d + l + 2)
                    for b in range(2):
                        w = (ring, ring1)[b]
                        pe.wait_ge(gu_full[b], 32 * d + 32)
                        pe.wait_ge(hb_ready, 2 * d + 1)
                        for k in range(KT):
                            for j in range(4):
                                last = mm(ps[32 * j:32 * j + 32, b, 0:2 * P], xTb[:, k, b * BLK:(b + 1) * BLK],
                                          w[:, 0:2, k * D_EXPERT + j * P:k * D_EXPERT + (j + 1) * P],
                                          start=(k == 0), stop=(k == KT - 1), skip_group_check=True)
                        last.then_inc(u_full, 1)
                        pe.drain().then_inc(gu_used[b], 1)

                    def turn(b):
                        pe.wait_ge(hb_ready, 2 * d + 2 + b)
                        pe.wait_ge(ht_ready, 2 * d + 1 + b)
                        tr(ps[:, 7, b * P:(b + 1) * P], hb[:, b, :], C("ident")).then_inc(t_full, 1)

                    turn(0)
                    gather(q + 1, d + l + 2)
                    turn(1)
                    for b in range(2):
                        w = (ring, ring1)[b]
                        pe.wait_ge(dn_full[b], 16 * d + 16)
                        pe.wait_ge(ht_ready, 2 * d + 2 + b)
                        for a in range(2):
                            pe.wait_ge((ysa, ysd)[a], 2 * d + 1 + b)
                            for j in range(4):
                                last = mm(ps[32 * j:32 * j + 32, 2 + a, :], hTb[:, b, j * BLK:(j + 1) * BLK],
                                          w[:, 2, j * D_MODEL + a * 512:j * D_MODEL + (a + 1) * 512],
                                          start=True, stop=True)
                            last.then_inc(d_full, 1)
                        pe.drain().then_inc(dn_used[b], 1)
                    pe.wait_ge(selw_ready, d + 1)
                    pe.wait_ge(ysa, 2 * d + 3)
                    pe.wait_ge(ysd, 2 * d + 3)
                    for j in range(5):
                        pe.wait_ge(acc_taken, 5 * d + 1 + (0, 0, 1, 2, 3)[j])
                        o = ps[:, 4 + j % 2, :]
                        if j < 4:
                            i, a = divmod(j, 2)
                            for b in range(2):
                                last = mm(o[:, :], selw[:, b, T0[i]:T0[i] + P], ys[:, b, a * 512:(a + 1) * 512],
                                          start=(b == 0), stop=(b == 1))
                        else:
                            for b in range(2):
                                for c in range(4):
                                    last = mm(o[32 * c:32 * c + 32, 0:256], selw[:, b, T0[2]:T], ys[:, b, c * 256:(c + 1) * 256],
                                              start=(b == 0), stop=(b == 1), skip_group_check=True)
                        last.then_inc(s_full, 1)
                pe.reg_add(before, before, pairs)

        @block.scalar
        def _(act):
            f = nc.scalar.activation
            cp = lambda o_, i_: f(o_, i_, ACT.Copy)
            act.wait_ge(con_in, 16 * 7)
            f(h_tm[0:9, 0, :], h_tm[0:9, 0, :], ACT.Silu).then_inc(c_silu, 1)
            for s_ in (g_taken, ht_ready, ysa):
                act.sem_inc(s_, 1)
            before = act.alloc_register("pairs_before")
            act.reg_mov(before, 0)
            with act.Fori(0, DEPTH) as l:
                def take_rows(dst, key, i):
                    R_ = ROWS[i]
                    for a in range(2):
                        act.wait_ge(filled.sem, fills(l, (key, i, a)))
                        o = bank((key, i, a))
                        cp(dst[:, 4 * a:4 * a + 4, T0[i]:T0[i] + R_],
                           o[:, 0:4 * R_].rearrange("p (k t) -> p k t", k=4)).then_inc(TA, 1)

                def take_ada(chunks):
                    for c in chunks:
                        act.wait_ge(filled.sem, fills(l, ("ada", c)))
                        o = bank(("ada", c))
                        cp(ada_at(c), o[:, :]).then_inc(TA, 1)

                take_ada(range(4))
                act.wait_ge(modT_ready.sem, modT_ready.at(l, 1))
                for q in range(4):
                    act.wait_ge(filled.sem, fills(l, ("xt", q)))
                    o = bank(("xt", q))
                    for k in range(2):
                        last = f(hT[:, 2 * q + k, 0:SEQ], o[:, k * SEQ:(k + 1) * SEQ], ACT.Identity,
                                 scale=modT[:, 1, 2 * q + k, 0:1], bias=modT[:, 0, 2 * q + k, 0:1])
                    last.then_inc(TA, 1)

                act.wait_ge(lam_abs.sem, lam_abs.at(l, 1))
                f(cl[:, 2, :], cl[:, 1, :], ACT.Exp, scale=-1.0)
                act.drain()
                f(cl[:, 2, :], cl[:, 2, :], ACT.Ln, bias=1.0).then_inc(lam_ln.sem, 1)

                def take_raw(u, key):
                    act.wait_ge(filled.sem, fills(l, key))
                    o = bank(key)
                    if u >= 4:
                        act.wait_ge(cv_ready.sem, cv_ready.at(l, u - 3))
                    cp(raw[:, u % 4, HALO:SS], o[:, 0:SEQ])
                    cp(raw[:, u % 4, SS:].rearrange("p (b j) -> p b j", b=DEC_BATCH)[:, :, HALO:],
                       o[:, SEQ:T].rearrange("p (b j) -> p b j", b=DEC_BATCH)).then_inc(TA, 1)

                def conv_out(u):
                    act.wait_ge(cv_ready.sem, cv_ready.at(l, u + 1))
                    fn = ACT.Copy if u < RT else ACT.Silu
                    m = u - RT
                    dst = xcT[:, u, :] if u < RT else xsT[:, m % 4, :] if m < 8 else BCT[:, m - 8, :]
                    src = cv[:, u % 2, :]
                    f(dst[:, 0:SEQ], src[:, 0:SEQ], fn)
                    f(dst[:, SEQ:T].rearrange("p (b j) -> p b j", b=DEC_BATCH)[:, 0:DEC_BATCH - 1, :],
                      src[:, SS:SS + 7 * (DEC_BATCH - 1)].rearrange("p (b j) -> p b j", j=7)[:, :, 0:DEC_SEQ], fn)
                    f(dst[:, T - DEC_SEQ:T], src[:, CVW - DEC_SEQ:CVW], fn).then_inc(cv_out.sem, 1)

                for m in range(RT):
                    take_raw(m, ("rgx", m))
                for m in range(RT):
                    act.wait_ge(filled.sem, fills(l, ("rgg", m)))
                    o = bank(("rgg", m))
                    f(yrg[:, m, :], o[:, 0:T], ACT.Gelu_apprx_tanh).then_inc(TA, 1)
                for u in range(RT):
                    conv_out(u)
                for m in range(XT + 1):
                    if m < XT:
                        take_raw(RT + m, ("fm", m))
                    if m >= 2:
                        conv_out(RT + m - 2)
                    if m >= 3:
                        u = m - 3
                        act.wait_ge(filled.sem, fills(l, ("xst", u)))
                        o = bank(("xst", u))
                        cp(xs[:, 0:2, u * P:(u + 1) * P],
                           o[:, 0:2 * P].rearrange("p (i n) -> p i n", i=2))
                        cp(xs[0:TS, 2, u * P:(u + 1) * P], o[0:TS, 2 * P:3 * P]).then_inc(TA, 1)
                conv_out(RT + XT - 1)
                for q in range((XT + RT) // 4):
                    act.wait_ge(filled.sem, fills(l, ("tail", q)))
                    o = bank(("tail", q))
                    cp(tails[:, q * 512:(q + 1) * 512], o[0:HALO * (1 + DEC_BATCH), :]) .then_inc(TA, 1)

                def take_partial(key, c):
                    act.wait_ge(filled.sem, fills(l, (key, c, "s")))
                    o = bank((key, c, "s"))
                    cp(h_tm[:, 2, c % 2 * CH:(c % 2 + 1) * CH], o[:, :]).then_inc(TA, 1)

                def take_z(c, i):
                    act.wait_ge(filled.sem, fills(l, ("z", c, i)))
                    o = bank(("z", c, i))
                    f(zb[0:ROWS[i], i, c * CH:(c + 1) * CH], o[0:ROWS[i], :], ACT.Silu).then_inc(TA, 1)

                act.wait_ge(dt_abs.sem, dt_abs.at(l, 1))
                f(dts[:, 2, :, :], dts[:, 2, :, :], ACT.Exp, scale=-1.0)
                f(bc16[:, 1, :], bc16[:, 1, :], ACT.Exp)
                act.drain()
                f(dts[:, 2, :, :], dts[:, 2, :, :], ACT.Ln, bias=1.0).then_inc(dt_ln.sem, 1)

                for key, dst, row in (("rga", rgr, V_BA), ("rgi", rgi, V_BX)):
                    for m in range(RT):
                        act.wait_ge(filled.sem, fills(l, (key, m)))
                        o = bank((key, m))
                        f(dst[:, m, :], o[:, 0:T], ACT.Sigmoid, bias=vecT[:, row + m:row + m + 1]).then_inc(TA, 1)
                act.drain()
                act.wait_ge(lam_c.sem, lam_c.at(l, 1))
                for m in range(RT):
                    f(rgt[:, m, :], rgr[:, m, :], ACT.Tanh, scale=cl[:, 1, m:m + 1])
                act.drain()
                for m in range(RT):
                    last = f(rgr[:, m, :], rgr[:, m, :], ACT.Exp, scale=cl[:, 0, m:m + 1])
                last.then_inc(rg_gates.sem, 1)
                act.wait_ge(rg_sq.sem, rg_sq.at(l, 1))
                f(rgt[:, :, :], rgt[:, :, :], ACT.Sqrt).then_inc(rg_root.sem, 1)
                take_partial("z", 0)
                for i in range(NT):
                    take_z(0, i)

                act.wait_ge(cum_ready.sem, cum_ready.at(l, 1))
                f(ex[:, 2, :, :], ex[:, 2, :, :], ACT.Exp)
                f(ex[:, 0:2, :, :], cum[:, :, :, :], ACT.Exp)
                f(tbh[:], tbh[:], ACT.Exp).then_inc(cum_exp.sem, 1)
                take_partial("z", 1)
                take_z(1, 0)

                def rstd(k, R_, lo, n_):
                    act.wait_ge(var_ready.sem, var_ready.at(l, k))
                    v = stat[0:R_, lo:lo + n_]
                    f(v, v, ACT.Ln, bias=C("eps", R_))
                    act.drain()
                    f(v, v, ACT.Exp, scale=-0.5).then_inc(rstd_ready.sem, 1)

                for i in range(NT):
                    for q in range(4 if i < 2 else 1):
                        n_ = (0, 4, 8)[i] + q
                        act.wait_ge(arg_ready.sem, arg_ready.at(l, n_ + 1))
                        b_ = AXb[0:ROWS[i], n_ % 2, :]
                        f(b_, b_, ACT.Exp).then_inc(exp_ready.sem, 1)
                    if i == 0:
                        take_z(1, 1)
                        take_z(1, 2)
                    if i < 2:
                        rstd(i + 1, ROWS[i], 0, 2)
                    if i == 0:
                        act.wait_ge(rg_done.sem, rg_done.at(l, 1))
                    for c in (i,) if i < 2 else (2, 3):
                        take_partial("q", c)
                        for j in range(NT):
                            act.wait_ge(filled.sem, fills(l, ("q", c, j)))
                            o = bank(("q", c, j))
                            f(qkvg[0:ROWS[j], j, c * CH:(c + 1) * CH], o[0:ROWS[j], :],
                              ACT.Copy if c < 3 else ACT.Silu).then_inc(TA, 1)

                def take_mix_a(i, a):
                    act.wait_ge(filled.sem, fills(l, ("mix_a", i, a)))
                    o = bank(("mix_a", i, a))
                    cp(h_tm[:, i, a * 512:(a + 1) * 512], o[:, :]).then_inc(TA, 1)

                take_rows(hT, "yt", 0)
                take_rows(hT, "yt", 1)
                rstd(3, TS, 0, 2)
                take_mix_a(0, 0)
                take_mix_a(0, 1)
                take_rows(hT, "yt", 2)
                take_mix_a(1, 0)
                for i in range(NT):
                    take_rows(qkT, "qk", i)

                def take_ret(i):
                    act.wait_ge(filled.sem, fills(l, ("yrt", i)))
                    o = bank(("yrt", i))
                    R_ = ROWS[i]
                    cp(yreT[:, :, T0[i]:T0[i] + R_], o[:, 0:4 * R_].rearrange("p (k t) -> p k t", k=4)).then_inc(TA, 1)

                for i in range(NT):
                    if i == 0:
                        take_mix_a(1, 1)
                        take_mix_a(2, 0)
                    if i:
                        take_ret(i - 1)
                    if i == 2:
                        take_ada(range(6, 12))
                    rstd(NT + i + 1, ROWS[i], 0, RET_HEADS)
                    if i == 0:
                        take_mix_a(2, 1)
                    if i == 1:
                        take_ada((4, 5))
                take_ret(2)
                for a in range(2):
                    act.wait_ge(filled.sem, fills(l, ("mix_s", a)))
                    o = bank(("mix_s", a))
                    cp(spare[:, a, :], o[:, :]).then_inc(TA, 1)
                rstd(2 * NT + 1, P, 0, 1)
                act.wait_ge(stores_out.sem, stores_out.at(l, 1))
                for c in range(6, 12):
                    if c == 8:
                        rstd(2 * NT + 2, TS, 2, 1)
                    if c == 10:
                        act.wait_ge(gate_used.sem, gate_used.at(l, 1))
                    dst, sl = (sh2, sc2, gate)[c // 2 - 3], slice(c % 2 * CH, (c % 2 + 1) * CH)
                    for w_, (name, R_) in enumerate((("mp", P), ("ms", TS))):
                        act.wait_ge(filled.sem, fills(l, (name, c)))
                        o = bank((name, c))
                        f(dst[0:R_, w_, sl], o[0:R_, :], ACT.Identity, bias=0.0 if c < 8 else 1.0).then_inc(TA, 1)
                rstd(3 * NT, P, 1, 1)
                for i in NORM_ORDER:
                    take_rows(hT, "h2t", i)
                act.wait_ge(score_fill.sem, score_fill.at(l, 1))
                act.wait_ge(filled.sem, fills(l, ("logit",)))
                o = bank(("logit",))
                f(rt[:, 0, 0:2, :], o[:, 0:2 * N_EXPERTS].rearrange("p (i e) -> p i e", i=2), ACT.Sigmoid)
                f(rt[0:TS, 0, 2, :], o[0:TS, 2 * N_EXPERTS:3 * N_EXPERTS], ACT.Sigmoid).then_inc(TA, 1)

                def take_gather(count):
                    act.wait_ge(g_full, count)
                    cp(xTb[:], ps[:, 6, :].rearrange("p (k t) -> p k t", k=KT)).then_inc(g_taken, 1)

                done = act.snap(before)
                take_gather(done + l + 1)
                act.wait_ge(plan_ready.sem, plan_ready.at(l, 1))
                idle["act"].stand(act)
                pairs = act.value_load(npi[0:1, 0:1], min_val=2, max_val=NBMAX // 2)

                with act.Fori(0, pairs) as q:
                    d = act.snap(done + q)
                    for b in range(2):
                        act.wait_ge(u_full, 2 * d + 1 + b)
                        f(sg[:, b, :], ps[:, b, 0:P], ACT.Silu).then_inc(sg_ready, 1)

                    def take_turned(b):
                        act.wait_ge(t_full, 2 * d + 1 + b)
                        cp(hTb[:, b, :], ps[:, 7, b * P:(b + 1) * P]).then_inc(ht_ready, 1)

                    take_turned(0)
                    take_gather(d + l + 2)
                    take_turned(1)
                    for b in range(2):
                        act.wait_ge(d_full, 4 * d + 1 + 2 * b)
                        cp(ys[:, b, 0:512], ps[:, 2, :]).then_inc(ysa, 1)
                act.reg_add(before, before, pairs)
                rstd(3 * NT + 1, P, 0, NT)

        @block.vector
        def _(dve):
            V = nc.vector
            tt, ts, stt, cpy = V.tensor_tensor, V.tensor_scalar, V.scalar_tensor_tensor, V.tensor_copy
            D = dve.drain
            V.memset(cT[:], 0.0)
            V.memset(dts[:], 0.0)
            V.memset(cum[:], 0.0)
            V.memset(stat[:], 1.0)
            for s_ in (small_room, hb_ready, ysd, acc_taken):
                dve.sem_inc(s_, 1)
            D()
            dve.wait_ge(c_turned, 1)
            cpy(cT[:, :, 0:9], ps[:, 6, 0:72].rearrange("p (k c) -> p k c", k=KT)).then_inc(c_ready, 1)
            dve.drain().then_inc(begun, 1)
            dve.sem_inc(settled, 1)
            before = dve.alloc_register("pairs_before")
            dve.reg_mov(before, 0)

            def over(ap, n_, axis=2):
                sh = list(ap.shape)
                sh.insert(axis, n_)
                return ap.unsqueeze(axis).to_broadcast(sh)

            with dve.Fori(0, DEPTH) as l:
                dve.wait_ge(filled.sem, fills(l, ("vec",)))
                o = bank(("vec",))
                cpy(vecT[:], o[:, 0:V_N]).then_inc(TD, 1)
                dve.wait_ge(filled.sem, fills(l, ("halo",)))
                o = bank(("halo",))
                cpy(halo[:].rearrange("p m n -> p (m n)"), o[:, 0:(XT + RT) * DEC_BATCH * HALO]).then_inc(TD, 1)
                V.memset(raw[:, :, 0:HALO], 0.0)
                D()
                lam = vecT[:, V_LAM:V_N]
                ts(cl[:, 1, :], lam, -1.0, None, ALU.mult)
                D()
                tt(cl[:, 1, :], cl[:, 1, :], lam, ALU.max)
                ts(cl[:, 0, :], lam, -1.0, 0.0, ALU.mult, ALU.max)
                D().then_inc(lam_abs.sem, 1)

                def mods(chunks):
                    for c in chunks:
                        j, a = divmod(c, 2)
                        dst = gate
                        one = 1.0
                        sl = slice(a * CH, (a + 1) * CH)
                        dve.wait_ge(filled.sem, fills(l, ("mp", c)))
                        o = bank(("mp", c))
                        ts(dst[:, 0, sl], o[:, :], one, None, ALU.add).then_inc(TD, 1)
                        dve.wait_ge(filled.sem, fills(l, ("ms", c)))
                        o = bank(("ms", c))
                        ts(dst[0:TS, 1, sl], o[0:TS, :], one, None, ALU.add).then_inc(TD, 1)

                for j in range(2):
                    dve.wait_ge(filled.sem, fills(l, ("mt", j)))
                    o = bank(("mt", j))
                    ts(modT[:, j].rearrange("p k c -> p (k c)"), o[:, 0:KT * (1 + DEC_BATCH)], float(j), None, ALU.add
                       ).then_inc(TD, 1)
                D().then_inc(modT_ready.sem, 1)
                dve.wait_ge(filled.sem, fills(l, ("xts",)))
                o = bank(("xts",))
                h4s = hT[:, :, SEQ:T].rearrange("p k (b j) -> p k b j", b=DEC_BATCH)
                tt(h4s, o[:, 0:KT * TS].rearrange("p (k b j) -> p k b j", k=KT, b=DEC_BATCH),
                   over(modT[:, 1, :, 1:], DEC_SEQ, 3), ALU.mult)
                D()
                tt(h4s, h4s, over(modT[:, 0, :, 1:], DEC_SEQ, 3), ALU.add).then_inc(TD, 1)
                dve.wait_ge(lam_ln.sem, lam_ln.at(l, 1))
                tt(cl[:, 3, :], cl[:, 0, :], cl[:, 2, :], ALU.add)
                D()
                ts(cl[:, 0, :], cl[:, 3, :], -RG_C, None, ALU.mult)
                ts(cl[:, 1, :], cl[:, 3, :], RG_C, None, ALU.mult)
                D().then_inc(lam_c.sem, 1)

                for u in range(RT + XT):
                    key = ("rgx", u) if u < RT else ("fm", u - RT)
                    m = u if u < RT else u - RT
                    mt = XT + u if u < RT else m
                    w0, nm, b0 = (V_RW, RT, V_RB) if u < RT else (V_XW, XT, V_XB)
                    tap = lambda j: vecT[:, w0 + j * nm + m:w0 + j * nm + m + 1]
                    r_, c_ = raw[:, u % 4, :], cv[:, u % 2, :]
                    seqs = r_[:, SS:].rearrange("p (b j) -> p b j", b=DEC_BATCH)
                    if u >= 4:
                        dve.wait_ge(cv_ready.sem, cv_ready.at(l, u - 3))
                    cpy(seqs[:, :, 0:HALO], halo[:, mt, :].rearrange("p (b j) -> p b j", b=DEC_BATCH))
                    D()
                    dve.wait_ge(*takes(l, key))
                    cpy(tailT[:, mt, 0:HALO], r_[:, SS - HALO:SS])
                    cpy(tailT[:, mt, HALO:].rearrange("p (b j) -> p b j", b=DEC_BATCH), seqs[:, :, DEC_SEQ:])
                    if u >= 2:
                        dve.wait_ge(cv_out.sem, cv_out.at(l, u - 1))
                    ts(c_, r_[:, 0:CVW], tap(0), vecT[:, b0 + m:b0 + m + 1], ALU.mult, ALU.add)
                    for j in range(1, CONV_WIDTH):
                        D()
                        stt(c_, r_[:, j:j + CVW], tap(j), c_, ALU.mult, ALU.add)
                    dve.drain().then_inc(cv_ready.sem, 1)

                dve.wait_ge(filled.sem, fills(l, ("dt",)))
                o = bank(("dt",))
                tt(dts[:, 0, 0:2, :], o[:, 0:32].rearrange("p (i h) -> p i h", i=2), over(bc16[:, 0, :], 2, 1), ALU.add)
                tt(dts[0:TS, 0, 2, :], o[0:TS, 32:48], bc16[0:TS, 0, :], ALU.add).then_inc(TD, 1)
                dve.wait_ge(filled.sem, fills(l, ("h0rg",)))
                o = bank(("h0rg",))
                cpy(h0rg[:].rearrange("p m n -> p (m n)"), o[:, 0:RT * DEC_BATCH]).then_inc(TD, 1)
                D()
                ts(dts[:, 1], dts[:, 0], -1.0, None, ALU.mult)
                D()
                tt(dts[:, 2], dts[:, 0], dts[:, 1], ALU.max)
                D().then_inc(dt_abs.sem, 1)
                dve.wait_ge(dt_ln.sem, dt_ln.at(l, 1))
                stt(dts[:, 1], dts[:, 0], 0.0, dts[:, 2], ALU.max, ALU.add)
                D()
                stt(dts[:, 3], dts[:, 1], -1.0, over(bc16[:, 1, :], NT, 1), ALU.mult, ALU.mult)
                D()
                tt(tmp[0:TS, 0:P].rearrange("p (b h) -> p b h", b=DEC_BATCH), over(dts[0:TS, 3, 2, :], DEC_BATCH, 1),
                   over(C("own", TS), SSD_HEADS), ALU.mult)
                D().then_inc(loga_ready.sem, 1)

                dve.wait_ge(rg_gates.sem, rg_gates.at(l, 1))
                tt(rgi[:], rgi[:], xcT[:], ALU.mult)
                D()
                tt(xcT[:], rgr[:], rgr[:], ALU.mult)
                D()
                stt(rgt[:], xcT[:], 1.0, rgt[:], ALU.add, ALU.mult)
                D().then_inc(rg_sq.sem, 1)
                dve.wait_ge(rg_root.sem, rg_root.at(l, 1))
                tt(rgi[:], rgi[:], rgt[:], ALU.mult)
                first = slice(SEQ, T, DEC_SEQ)
                tt(h0rg[:], h0rg[:], rgr[:, :, first], ALU.mult)
                D()
                tt(rgi[:, :, first], rgi[:, :, first], h0rg[:], ALU.add)
                V.memset(rgr[:, :, first], 0.0)
                D()
                for m in range(RT):
                    V.tensor_tensor_scan(xcT[:, m, :], rgr[:, m, :], rgi[:, m, :], 0.0, ALU.mult, ALU.add)
                D()
                cpy(rgl[:, :, 0:1], xcT[:, :, SEQ - 1:SEQ])
                cpy(rgl[:, :, 1:], xcT[:, :, SEQ + DEC_SEQ - 1:T:DEC_SEQ])
                D().then_inc(rgl_ready.sem, 1)
                tt(yrg[:], yrg[:], xcT[:], ALU.mult).then_inc(rg_done.sem, 1)

                dve.wait_ge(filled.sem, fills(l, ("cum",)))
                o = bank(("cum",))
                n_ = NT * SSD_HEADS
                v = o[:, 0:2 * n_].rearrange("p (k i h) -> p k i h", k=2, i=NT)
                cpy(cum[:, :, 0:2, :], v[:, :, 0:2, :])
                cpy(cum[0:TS, :, 2, :], v[0:TS, :, 2, :])
                cpy(tbh[:].rearrange("p b h -> p (b h)"), o[:, 2 * n_:2 * n_ + P]).then_inc(TD, 1)
                D()
                tt(ex[:, 2], cum[:, 1], cum[:, 0], ALU.subtract)
                D().then_inc(cum_ready.sem, 1)
                dve.wait_ge(filled.sem, fills(l, ("rgo",)))
                o = bank(("rgo",))
                dve.wait_ge(wab_in.sem, wab_in.at(l, 256))
                cpy(rgo[:], o[0:1 + DEC_BATCH, :]).then_inc(TD, 1)
                D().then_inc(rgo_ready.sem, 1)
                dve.wait_ge(cum_exp.sem, cum_exp.at(l, 1))
                dve.wait_ge(tails_out.sem, tails_out.at(l, 64))

                hv = lambda ap: ap.rearrange("p (h v) -> p h v", v=SSD_HD)

                def rstd(k, i=None):
                    D().then_inc(var_ready.sem, 1)
                    dve.wait_ge(rstd_ready.sem, rstd_ready.at(l, k))

                for i in range(NT):
                    R_ = ROWS[i]
                    HQ = 4 if i < 2 else SSD_HEADS
                    mask = C("tri" if i < 2 else "tri_s", R_, 0, R_)
                    tt(hv(xdt[0:R_, :]), hv(xs[0:R_, i, 0:D_SSD]), over(dts[0:R_, 1, i, :], SSD_HD), ALU.mult)
                    D()
                    tt(hv(xw[0:R_, :]), hv(xdt[0:R_, :]), over(ex[0:R_, 2, i, :], SSD_HD), ALU.mult)
                    D().then_inc(xw_ready.sem, 1)
                    dve.wait_ge(filled.sem, fills(l, ("cb", i)))
                    o = bank(("cb", i))
                    sm = Sm[0:R_, 0:2 * R_].rearrange("p (g t) -> p g t", g=2)
                    tt(sm, o[0:R_, 0:2 * R_].rearrange("p (g t) -> p g t", g=2), over(mask, 2, 1), ALU.mult).then_inc(TD, 1)
                    nq = SSD_HEADS // HQ
                    base_ = (0, 4, 8)[i]

                    def arg(q):
                        dve.wait_ge(filled.sem, fills(l, ("dec", i, q)))
                        o = bank(("dec", i, q))
                        for j in range(HQ):
                            h = q * HQ + j
                            last = ts(AXb[0:R_, (base_ + q) % 2, j * R_:(j + 1) * R_], o[0:R_, j * R_:(j + 1) * R_],
                                      cum[0:R_, 0, i, h:h + 1], 0.0, ALU.subtract, ALU.min)
                        last.then_inc(TD, 1)
                        dve.drain().then_inc(arg_ready.sem, 1)

                    def scores(q):
                        dve.wait_ge(exp_ready.sem, exp_ready.at(l, base_ + q + 1))
                        a_ = AXb[0:R_, (base_ + q) % 2, :]
                        if i < 2:
                            tt(Pm[:, q, :].rearrange("p (j t) -> p j t", j=4), a_.rearrange("p (j t) -> p j t", j=4),
                               over(sm[:, q // 2, :], 4, 1), ALU.mult)
                        else:
                            for g in range(2):
                                tt(Pm[0:R_, 0, g * 256:(g + 1) * 256].rearrange("p (j t) -> p j t", j=HG),
                                   a_[:, g * 256:(g + 1) * 256].rearrange("p (j t) -> p j t", j=HG),
                                   over(sm[:, g, :], HG, 1), ALU.mult)
                        D().then_inc(P_ready.sem, 1)

                    for q in range(nq):
                        arg(q)
                        if q:
                            scores(q - 1)
                    scores(nq - 1)
                    ea = lambda g: over(ex[0:R_, 0, i, g * HG:(g + 1) * HG], SSD_HD)
                    Y = lambda g: h_tm[0:R_, i, g * 512:(g + 1) * 512]
                    if i == 1:
                        for g in range(2):
                            dve.wait_ge(filled.sem, fills(l, ("yo", i, g)))
                            o = bank(("yo", i, g))
                            tt(hv(Y(g)), hv(o[:, :]), ea(g), ALU.mult).then_inc(TD, 1)
                    if i < 2:
                        for g in range(2):
                            dve.wait_ge(filled.sem, fills(l, ("cs", i, g)))
                            o = bank(("cs", i, g))
                            sg_ = S[:, g * 512:(g + 1) * 512]
                            if i == 0:
                                cpy(sg_, o[:, :]).then_inc(TD, 1)
                            else:
                                tt(hv(sg_), hv(sg_), over(ex[:, 1, i, g * HG:(g + 1) * HG], SSD_HD), ALU.mult)
                                D()
                                tt(sg_, sg_, o[:, :], ALU.add).then_inc(TD, 1)
                            dve.drain().then_inc(S_ready.sem, 1)
                    else:
                        dve.wait_ge(S_out.sem, S_out.at(l, 16))
                        for g in range(2):
                            tt(CmB[:, g], over(BCT[:, 2 + g, SEQ:T], DEC_BATCH, 1),
                               C("bmask").rearrange("p (b t) -> p b t", b=DEC_BATCH), ALU.mult)
                        D().then_inc(Cm_ready.sem, 1)
                        for b in range(DEC_BATCH):
                            ts(BmB[:, b % 2, :], xs[0:TS, 2, D_SSD:], C("own", TS, b, 1), None, ALU.mult)
                            D().then_inc(Bm_ready.sem, 1)
                            dve.wait_ge(h0_in[b % 3].sem, h0_in[b % 3].at(l, 16 * (b // 3 + 1)))
                            for g in range(2):
                                dve.wait_ge(filled.sem, fills(l, ("st", b, g)))
                                o = bank(("st", b, g))
                                sg_ = h0s[b % 3][:, g * 512:(g + 1) * 512]
                                tt(hv(sg_), hv(sg_), over(tbh[:, b, g * HG:(g + 1) * HG], SSD_HD), ALU.mult)
                                D()
                                tt(sg_, sg_, o[:, :], ALU.add).then_inc(TD, 1)
                                dve.drain().then_inc(h0_new.sem, 1)
                        for g in range(2):
                            dve.wait_ge(hold_full.sem, hold_full.at(l, g + 1))
                            tt(hv(Y(g)), hv(ps[0:TS, 6 + g, :]), ea(g), ALU.mult).then_inc(hold_free.sem, 1)
                    D()
                    for g in range(2):
                        dve.wait_ge(filled.sem, fills(l, ("yi", i, g)))
                        o = bank(("yi", i, g))
                        if i == 0:
                            cpy(Y(g), o[0:R_, :]).then_inc(TD, 1)
                        else:
                            tt(Y(g), Y(g), o[0:R_, :], ALU.add).then_inc(TD, 1)
                    tt(hv(xdt[0:R_, :]), hv(xs[0:R_, i, 0:D_SSD]), over(bc16[0:R_, 2, :], SSD_HD), ALU.mult)
                    D()
                    y_ = h_tm[0:R_, i, :]
                    tt(y_, y_, xdt[0:R_, :], ALU.add)
                    D()
                    dve.wait_ge(*takes(l, ("z", 1, i)))
                    tt(y_, y_, zb[0:R_, i, :], ALU.mult)
                    D()
                    for g in range(2):
                        V.bn_stats(stat[0:R_, 8 + 6 * g:14 + 6 * g], Y(g))
                    D()
                    for g in range(2):
                        V.bn_aggr(stat[0:R_, 32 + 2 * g:34 + 2 * g], stat[0:R_, 8 + 6 * g:14 + 6 * g])
                    D()
                    mv = stat[0:R_, 32:36].rearrange("p (g k) -> p g k", k=2)
                    tt(stat[0:R_, 0:2], mv[:, :, 0], mv[:, :, 0], ALU.mult)
                    D()
                    tt(stat[0:R_, 0:2], stat[0:R_, 0:2], mv[:, :, 1], ALU.add)
                    rstd(i + 1)
                    for g in range(2):
                        stt(Y(g), Y(g), stat[0:R_, g:g + 1], lnp[0:R_, 0, g * 512:(g + 1) * 512], ALU.mult, ALU.mult)
                    D().then_inc(y_ready.sem, 1)
                D().then_inc(ssd_done.sem, 1)

                for b in range(3):
                    dve.wait_ge(h0_out[b].sem, h0_out[b].at(l, 16 * OF_BUF[b]))
                hh = lambda ap: ap.rearrange("p (h c v) -> p h c v", c=2, v=RET_HD // 2)
                for i in range(NT):
                    R_ = ROWS[i]
                    for j in range(2):
                        dve.wait_ge(*takes(l, ("q", j, i)))
                    src, dst = hh(qkvg[0:R_, i, 0:2 * D_RET]), hh(rq[0:R_, i, :])
                    t1 = tmp[0:R_, 0:512].rearrange("p (h v) -> p h v", v=64)
                    t2 = tmp[0:R_, 512:1024].rearrange("p (h v) -> p h v", v=64)
                    cs_ = over(C("cos", R_, 64 * i, 64), 8, 1)
                    sn_ = over(C("sin", R_, 64 * i, 64), 8, 1)
                    tt(dst[:, :, 0, :], src[:, :, 0, :], cs_, ALU.mult)
                    tt(t1, src[:, :, 1, :], sn_, ALU.mult)
                    tt(dst[:, :, 1, :], src[:, :, 1, :], cs_, ALU.mult)
                    tt(t2, src[:, :, 0, :], sn_, ALU.mult)
                    D()
                    tt(dst[:, :, 0, :], dst[:, :, 0, :], t1, ALU.subtract)
                    tt(dst[:, :, 1, :], dst[:, :, 1, :], t2, ALU.add)
                    D().then_inc(rope_ready.sem, 1)
                h4 = lambda ap: ap.rearrange("p (h v) -> p h v", h=RET_HEADS)
                dve.wait_ge(*takes(l, ("q", 3, NT - 1)))
                for i in range(NT):
                    R_ = ROWS[i]
                    sfx = "_s" if i == 2 else ""
                    tt(h4(vw[0:R_, :]), h4(qkvg[0:R_, i, 2 * D_RET:3 * D_RET]), over(C("kdec" + sfx, R_), P), ALU.mult)
                    D().then_inc(vw_ready.sem, 1)
                    if i == 2:
                        dve.wait_ge(*takes(l, ("qk", 2, 0)))
                        for h in range(RET_HEADS):
                            tt(QmB[:, h], over(qkT[:, h, SEQ:T], DEC_BATCH, 1),
                               C("bmask").rearrange("p (b t) -> p b t", b=DEC_BATCH), ALU.mult)
                        D().then_inc(Qm_ready.sem, 1)
                    dve.wait_ge(filled.sem, fills(l, ("sc", i)))
                    o = bank(("sc", i))
                    tt(Pr[0:R_, 0:4 * R_], o[0:R_, 0:4 * R_], C("dr" + sfx, R_), ALU.mult).then_inc(TD, 1)
                    D().then_inc(Pr_ready.sem, 1)
                    if i:
                        dve.wait_ge(filled.sem, filled.at(l, PLACE["yrt", i - 1] + 1))
                    if i == 1:
                        dve.wait_ge(filled.sem, fills(l, ("ro", i)))
                        o = bank(("ro", i))
                        tt(h4(Y2[:]), h4(o[:, :]), over(C("qdec"), P), ALU.mult).then_inc(TD, 1)
                    if i < 2:
                        dve.wait_ge(filled.sem, fills(l, ("rs", i)))
                        o = bank(("rs", i))
                        if i == 0:
                            cpy(R[:], o[:, :]).then_inc(TD, 1)
                        else:
                            tt(h4(R[:]), h4(R[:]), over(C("gam"), P), ALU.mult)
                            D()
                            tt(R[:], R[:], o[:, :], ALU.add).then_inc(TD, 1)
                        dve.drain().then_inc(R_ready.sem, 1)
                    else:
                        for b in range(DEC_BATCH):
                            ts(Km[:, b % 2, :], rq[0:TS, 2, D_RET:], C("own", TS, b, 1), None, ALU.mult)
                            D().then_inc(Km_ready.sem, 1)
                            dve.wait_ge(r0_in[b % 3].sem, r0_in[b % 3].at(l, 16 * (b // 3 + 1)))
                            dve.wait_ge(filled.sem, fills(l, ("rt", b)))
                            o = bank(("rt", b))
                            r_ = r0s[:, b % 3, :]
                            tt(h4(r_), h4(r_), over(C("gam_s"), P), ALU.mult)
                            D()
                            tt(r_, r_, o[:, :], ALU.add).then_inc(TD, 1)
                            dve.drain().then_inc(r0_new.sem, 1)
                        dve.wait_ge(hold_full.sem, hold_full.at(l, 3))
                        tt(h4(Y2[0:TS, :]), h4(ps[0:TS, 6, :]), over(C("qdec_s", TS), P), ALU.mult).then_inc(hold_free.sem, 1)
                    D()
                    y_ = Y2[0:R_, :]
                    dve.wait_ge(filled.sem, fills(l, ("ri", i)))
                    o = bank(("ri", i))
                    if i == 0:
                        cpy(y_, o[0:R_, :]).then_inc(TD, 1)
                    else:
                        tt(y_, y_, o[0:R_, :], ALU.add).then_inc(TD, 1)
                    D()
                    for h in range(RET_HEADS):
                        V.bn_stats(stat[0:R_, 8 + 6 * h:14 + 6 * h], y_[:, h * P:(h + 1) * P])
                    D()
                    for h in range(RET_HEADS):
                        V.bn_aggr(stat[0:R_, 32 + 2 * h:34 + 2 * h], stat[0:R_, 8 + 6 * h:14 + 6 * h])
                    D()
                    mv = stat[0:R_, 32:40].rearrange("p (g k) -> p g k", k=2)
                    cpy(stat[0:R_, 0:RET_HEADS], mv[:, :, 1])
                    rstd(NT + i + 1)
                    for h in range(RET_HEADS):
                        ts(y_[:, h * P:(h + 1) * P], y_[:, h * P:(h + 1) * P], stat[0:R_, 32 + 2 * h:33 + 2 * h],
                           stat[0:R_, h:h + 1], ALU.subtract, ALU.mult)
                    D()
                    tt(y_, y_, lnp[0:R_, 1, 0:D_RET], ALU.mult)
                    D()
                    tt(y_, y_, qkvg[0:R_, i, 3 * D_RET:], ALU.mult)
                    D().then_inc(yr_ready.sem, 1)
                D().then_inc(ret_done.sem, 1)

                def norm(tiles, k, gain_in):
                    for i in tiles:
                        for a in range(2):
                            V.bn_stats(stat[0:ROWS[i], 8 + 12 * i + 6 * a:14 + 12 * i + 6 * a],
                                       x_tm[0:ROWS[i], i, a * 512:(a + 1) * 512])
                    D()
                    for i in tiles:
                        V.bn_aggr(stat[0:ROWS[i], 48 + 2 * i:50 + 2 * i], stat[0:ROWS[i], 8 + 12 * i:20 + 12 * i])
                    D()
                    for i in tiles:
                        cpy(stat[0:ROWS[i], i:i + 1], stat[0:ROWS[i], 49 + 2 * i:50 + 2 * i])
                    rstd(k)
                    for i in tiles:
                        x_ = x_tm[0:ROWS[i], i, :]
                        ts(x_, x_, stat[0:ROWS[i], 48 + 2 * i:49 + 2 * i], stat[0:ROWS[i], i:i + 1],
                           ALU.subtract, ALU.mult)
                    D()
                    if 0 in tiles:
                        dve.wait_ge(gain_in.sem, gain_in.at(l, 32))
                    for n_ in range(2):
                        for i in tiles:
                            x_ = x_tm[0:ROWS[i], i, :]
                            tt(x_, x_, lnp[0:ROWS[i], n_, :], (ALU.mult, ALU.add)[n_])
                        D()

                mods(range(4, 6))

                def modulate(i):
                    R_, w_ = ROWS[i], int(i == 2)
                    tt(h_tm[0:R_, i, :], x_tm[0:R_, i, :], sc2[0:R_, w_, :], ALU.mult)
                    D()
                    tt(h_tm[0:R_, i, :], h_tm[0:R_, i, :], sh2[0:R_, w_, :], ALU.add).then_inc(h2_ready.sem, 1)

                for i, a in MIX_ORDER:
                    R_, w_ = ROWS[i], int(i == 2)
                    sl = slice(a * 512, (a + 1) * 512)
                    dve.wait_ge(filled.sem, fills(l, ("mix", i, a)))
                    o = bank(("mix", i, a))
                    if i == 2:
                        tt(h_tm[0:R_, i, sl], o[0:R_, :], gate[0:R_, w_, sl], ALU.mult).then_inc(TD, 1)
                    else:
                        tt(h_tm[0:R_, i, sl], o[0:R_, :], h_tm[0:R_, i, sl], ALU.add).then_inc(TD, 1)
                        D()
                        tt(h_tm[0:R_, i, sl], h_tm[0:R_, i, sl], gate[0:R_, w_, sl], ALU.mult)
                    if a == 1:
                        D()
                        stt(x_tm[0:R_, i, :], x_tm[0:R_, i, :], ALPHA, h_tm[0:R_, i, :], ALU.mult, ALU.add)
                        D()
                        if i == 1:
                            dve.sem_inc(gate_used.sem, 1)
                        norm((i,), 2 * NT + 1 + NORM_ORDER.index(i), ln1_in)
                        if i == 2:
                            dve.wait_ge(*takes(l, ("ms", 9)))
                            modulate(0)
                            modulate(2)
                D().then_inc(x1_done.sem, 1)
                modulate(1)
                D()

                V.memset(rt[:, 0], 0.5)
                V.memset(dtm[:], 0.0)
                D().then_inc(score_fill.sem, 1)
                dve.wait_ge(*takes(l, ("logit",)))
                dve.sem_inc(small_room, 1)
                G3 = NT * N_GROUPS
                g8 = lambda k_: rt[:, k_].rearrange("p i (g e) -> p (i g) e", e=EPG)
                pref = over(C("pref"), NT, 1)
                small_ = lambda k_: rt[:, 12].rearrange("p i e -> p (i e)")[:, k_ * G3:(k_ + 1) * G3]

                def top(v, oh, s_, m_, pf):
                    V.tensor_reduce(m_, v, AX_X, ALU.max)
                    D()
                    tt(oh, v, over(m_, v.shape[2]), ALU.is_equal)
                    D()
                    tt(oh, oh, pf, ALU.mult)
                    D()
                    V.tensor_reduce(s_, oh, AX_X, ALU.max)
                    D()
                    tt(oh, oh, over(s_, v.shape[2]), ALU.is_equal)
                    D()

                tt(rt[:, 1], rt[:, 0], over(rbias[:], NT, 1), ALU.add)
                tt(rt[:, 8], pref, pref, ALU.max)
                D()
                top(g8(1), g8(5), small_(0), small_(1), g8(8))
                stt(rt[:, 6], rt[:, 5], -1e30, rt[:, 1], ALU.mult, ALU.add)
                D()
                V.tensor_reduce(small_(2), g8(6), AX_X, ALU.max)
                D()
                tt(small_(1), small_(1), small_(2), ALU.add)
                D()
                g4 = lambda k_: small_(k_).rearrange("p (i g) -> p i g", g=N_GROUPS)
                n1, n2 = stat[:, 0:NT], stat[:, 4:4 + NT]
                top(g4(1), g4(2), n1, n2, over(C("pref", P, 0, N_GROUPS), NT, 1))
                ts(small_(3), small_(2), 1e30, -1e30, ALU.mult, ALU.add)
                tt(g8(2), g8(1), over(small_(2), EPG), ALU.mult)
                D()
                tt(g8(2), g8(2), over(small_(3), EPG), ALU.add)
                D()
                top(rt[:, 2], rt[:, 3], n1, n2, pref)
                stt(rt[:, 2], rt[:, 3], -1e30, rt[:, 2], ALU.mult, ALU.add)
                D()
                top(rt[:, 2], rt[:, 4], n1, n2, pref)
                for k in range(2):
                    tt(rt[:, 5 + k], rt[:, 3 + k], rt[:, 0], ALU.mult)
                D()
                for k in range(2):
                    V.tensor_reduce(dtm[:, 1, :, k], rt[:, 5 + k], AX_X, ALU.add)
                D()
                tt(n1, dtm[:, 1, :, 0], dtm[:, 1, :, 1], ALU.add)
                D()
                V.reciprocal(n2, n1)
                D()
                tt(dtm[:, 1], dtm[:, 1], over(n2, 2), ALU.mult)
                for k in range(2):
                    tt(rt[:, 3 + k], rt[:, 3 + k], over(C("valid"), N_EXPERTS), ALU.mult)
                D()
                tt(rt[:, 7], rt[:, 3], rt[:, 4], ALU.add)
                D().then_inc(oh_ready.sem, 1)
                dve.wait_ge(filled.sem, fills(l, ("rank",)))
                o = bank(("rank",))
                cpy(rt[:, 9, 0:2, :], o[:, 0:64].rearrange("p (i e) -> p i e", i=2))
                cpy(rt[0:TS, 9, 2, :], o[0:TS, 64:96])
                cpy(nblk[:, 0, :], o[:, 96:128]).then_inc(TD, 1)
                V.memset(nblk[:, 4, :], 1.0)
                D()
                ts(npi[:], nblk[:, 0, :], float(BLK - 1), None, ALU.add)
                D()
                ts(npi[:], npi[:], BLK.bit_length() - 1, None, ALU.arith_shift_right)
                D()
                cpy(nblk[:, 1, :], npi[:])
                D()
                tt(nblk[:, 1, :], nblk[:, 1, :], C("atleast"), ALU.max)
                D()
                V.tensor_tensor_scan(nblk[:, 2, :], nblk[:, 4, :], nblk[:, 1, :], 0.0, ALU.mult, ALU.add)
                D()
                tt(nblk[:, 3, :], nblk[:, 2, :], nblk[:, 1, :], ALU.subtract)
                D()
                ts(nblk[:, 3, :], nblk[:, 3, :], float(BLK), None, ALU.mult)
                D()
                tt(bew[:], over(C("iota", 1, 0, NBMAX), N_EXPERTS), over(nblk[0:1, 2, :], NBMAX, 1), ALU.is_ge)
                for i in range(NT):
                    R_ = ROWS[i]
                    tt(rt[0:R_, 10, i, :], rt[0:R_, 9, i, :], nblk[0:R_, 3, :], ALU.add)
                    D()
                    for k in range(2):
                        tt(rt[0:R_, 5 + k, i, :], rt[0:R_, 3 + k, i, :], rt[0:R_, 10, i, :], ALU.mult)
                    D()
                    for k in range(2):
                        V.tensor_reduce(dtm[0:R_, 0, i, k:k + 1], rt[0:R_, 5 + k, i, :], AX_X, ALU.add)
                D().then_inc(dtm_ready.sem, 1)

                def select(move):
                    dv = dtm[:, 0].rearrange("p i k -> p (i k)")
                    st_ = selt[:].rearrange("p i k s -> p (i k) s")
                    if move:
                        ts(dv, dv, float(-2 * BLK), None, ALU.add)
                        D()
                    tt(st_, over(C("iota"), 2 * NT, 1), over(dv, 2 * BLK), ALU.is_equal)
                    D()
                    tt(sel[:, 0], selt[:, :, 0, :], selt[:, :, 1, :], ALU.add)
                    D().then_inc(sel_ready, 1)

                select(False)
                V.tensor_reduce(rt[0:1, 11, :, :].rearrange("p i e -> p (i e)")[:, 0:NBMAX], bew[:], AX_X, ALU.add)
                ts(npi[0:1, 0:1], nblk[0:1, 2, N_EXPERTS - 1:N_EXPERTS], 1.0, None, ALU.add)
                D()
                ts(bei[:, 0:NBMAX], rt[0:1, 11, :, :].rearrange("p i e -> p (i e)")[:, 0:NBMAX], float(N_EXPERTS - 1), None, ALU.min)
                ts(npi[0:1, 0:1], npi[0:1, 0:1], 1, None, ALU.arith_shift_right)
                D().then_inc(plan_ready.sem, 1)
                for v in range(4):
                    dve.wait_ge(filled.sem, fills(l, ("bc", v)))
                    o = bank(("bc", v))
                    cpy(dbc[:, v, :], o[:, 0:T]).then_inc(TD, 1)
                V.memset(acc[:], 0.0)
                V.memset(accs[:], 0.0)
                cpy(scol[:], C("slot"))
                D()

                done = dve.snap(before)
                pairs = dve.value_load(npi[0:1, 0:1], min_val=2, max_val=NBMAX // 2)

                with dve.Fori(0, pairs) as q:
                    d = dve.snap(done + q)
                    dve.wait_ge(g_full, d + l + 1)
                    select(True)
                    for b in range(2):
                        stt(selw[:, b, :], dbc[:, 0, :], scol[:, b:b + 1], dbc[:, 2, :], ALU.is_equal, ALU.mult)
                        stt(selt2[:, b, :], dbc[:, 1, :], scol[:, b:b + 1], dbc[:, 3, :], ALU.is_equal, ALU.mult)
                    D()
                    tt(selw[:], selw[:], selt2[:], ALU.add)
                    ts(scol[:], scol[:], float(2 * BLK), None, ALU.add)
                    D().then_inc(selw_ready, 1)
                    for b in range(2):
                        dve.wait_ge(sg_ready, 2 * d + 1 + b)
                        tt(hb[:, b, :], sg[:, b, :], ps[:, b, P:2 * P], ALU.mult)
                        D().then_inc(hb_ready, 1)
                    for b in range(2):
                        dve.wait_ge(d_full, 4 * d + 2 + 2 * b)
                        cpy(ys[:, b, 512:1024], ps[:, 3, :])
                        D().then_inc(ysd, 1)
                    for j in range(5):
                        dve.wait_ge(s_full, 5 * d + 1 + j)
                        if j < 4:
                            i, a = divmod(j, 2)
                            v = acc[:, i, a * 512:(a + 1) * 512]
                            tt(v, v, ps[:, 4 + j % 2, :], ALU.add)
                        else:
                            tt(accs[:], accs[:], ps[:, 4, 0:256], ALU.add)
                        D().then_inc(acc_taken, 1)
                dve.reg_add(before, before, pairs)
                after = dve.snap(before)
                dve.wait_ge(g_taken, after + l + 2)
                dve.sem_inc(settled, 1)

                for c in range(4):
                    cpy(h_tm[0:TS, 2, c * 256:(c + 1) * 256], accs[32 * c:32 * c + TS, :])
                for i in range(2):
                    tt(acc[:, i, :], acc[:, i, :], gate[:, 0, :], ALU.mult)
                D()
                tt(h_tm[0:TS, 2, :], h_tm[0:TS, 2, :], gate[0:TS, 1, :], ALU.mult)
                D()
                for i in range(NT):
                    R_ = ROWS[i]
                    m_ = acc[:, i, :] if i < 2 else h_tm[0:TS, 2, :]
                    stt(x_tm[0:R_, i, :], x_tm[0:R_, i, :], ALPHA, m_, ALU.mult, ALU.add)
                D()
                norm(range(NT), 3 * NT + 1, ln2_in)
                D().then_inc(begun, 1)


_IN = ["x_prompt", "x_sample", "c_prompt", "c_sample", "state_ssd", "state_ssd_conv", "state_rglru",
       "state_rglru_conv", "state_ret", "w_ada", "b_ada", "w_in", "ssd_conv_w", "ssd_conv_b", "ssd_dt_bias",
       "ssd_a_log", "ssd_d", "ssd_norm_w", "rg_conv_w", "rg_conv_b", "rg_wa", "rg_ba", "rg_wx", "rg_bx",
       "rg_lambda", "ret_gn_w", "w_out", "ln1_g", "ln1_b", "router_w", "router_bias", "exp_w_gate", "exp_w_up",
       "exp_w_down", "ln2_g", "ln2_b"]
_OUT = [("y_prompt", (1, SEQ, D_MODEL)), ("y_sample", (DEC_BATCH, DEC_SEQ, D_MODEL))]
for _s, _b in (("p", 1), ("s", DEC_BATCH)):
    _OUT += [(f"ssd_{_s}", (DEPTH, _b, SSD_HEADS, SSD_STATE, SSD_HD)),
             (f"ssd_conv_{_s}", (DEPTH, _b, HALO, SSD_CONV_DIM)),
             (f"rglru_{_s}", (DEPTH, _b, D_RG)),
             (f"rglru_conv_{_s}", (DEPTH, _b, HALO, D_RG)),
             (f"ret_{_s}", (DEPTH, _b, RET_HEADS, RET_HD, RET_HD))]


def kernel(**inputs):
    import numpy as np
    import concourse.bacc as bacc
    from concourse.bass_utils import run_bass_kernel_spmd

    nc = bacc.Bacc("TRN2", target_bir_lowering=False, num_devices=1)
    arrays, A, O = {}, {}, {}
    given = [(name, np.ascontiguousarray(inputs[name])) for name in _IN]
    given.append(("con", const_table()[1]))
    for name, a in given:
        arrays[f"in_{name}"] = a
        A[name] = nc.dram_tensor(f"in_{name}", a.shape, mybir.dt.from_np(a.dtype), kind="ExternalInput").ap()
    for name, shape in _OUT:
        O[name] = nc.dram_tensor(f"out_{name}", shape, F32, kind="ExternalOutput").ap()
    trunk(nc, A, O)
    r = run_bass_kernel_spmd(nc, [arrays], core_ids=[0])
    return tuple(r.results[0][f"out_{name}"] for name, _ in _OUT)
```
